# Optimizing a Trainium2 kernel written in Bass

```python
import math
import jax, jax.numpy as jnp
from jax import lax
import numpy as np

D_MODEL = 1024
BATCH = 1
SEQ = 512
DEPTH = 1

DA_HEADS = 8
DA_HEAD_DIM = 64
DA_V_DIM = 2 * DA_HEAD_DIM
DA_QK = DA_HEADS * 2 * DA_HEAD_DIM
DA_WIDTH = DA_HEADS * DA_V_DIM
DN_HEADS = 8
DN_KEY_DIM = 128
DN_VAL_DIM = 128
DN_QK = DN_HEADS * DN_KEY_DIM
DN_WIDTH = DN_HEADS * DN_VAL_DIM
DN_CONV = 4
DN_CHUNK = 64
MEM_LEN = 256
CA_HEADS = 4
CA_HEAD_DIM = 256
CA_WIDTH = CA_HEADS * CA_HEAD_DIM
N_BRANCH = 3
BRANCH_WIDTH = 1024
D_FF = 4 * D_MODEL
REL_BUCKETS = 32
REL_MAX_EXACT = 16
REL_MAX_DIST = 128
Q_BLOCK = 128
EPS = 1e-6

IN_SPLITS = (DA_QK, DA_QK, DA_WIDTH,
             DN_QK, DN_QK, DN_WIDTH, DN_WIDTH,
             DN_HEADS, DN_HEADS,
             CA_WIDTH,
             N_BRANCH * D_MODEL)
IN_WIDTH = sum(IN_SPLITS)
SPLIT_IDX = tuple(int(i) for i in np.cumsum(IN_SPLITS)[:-1])

kernel_name = "hybrid_diffattn_gdn_memxattn_gated_merge"

def rms_norm(x, g):
    xf = x.astype(jnp.float32)
    y = xf * lax.rsqrt(jnp.mean(xf * xf, axis=-1, keepdims=True) + EPS)
    return (y * g.astype(jnp.float32)).astype(x.dtype)

def l2norm(x):
    return x * lax.rsqrt(jnp.sum(x * x, axis=-1, keepdims=True) + EPS)

def lambda_init(layer):
    return 0.8 - 0.6 * math.exp(-0.3 * layer)

def t5_causal_bucket(dist):
    nf = jnp.maximum(dist, 1).astype(jnp.float32)
    large = REL_MAX_EXACT + (jnp.log(nf / REL_MAX_EXACT) / math.log(REL_MAX_DIST / REL_MAX_EXACT)
                             * (REL_BUCKETS - REL_MAX_EXACT)).astype(jnp.int32)
    large = jnp.minimum(large, REL_BUCKETS - 1)
    return jnp.where(dist < REL_MAX_EXACT, dist, large)

def diff_attention(q, k, v, rel_bias, lam_vecs, subln_g, lam_init):
    B, S = q.shape[0], q.shape[1]
    nb = S // Q_BLOCK
    scale = DA_HEAD_DIM ** -0.5
    lv = lam_vecs.astype(jnp.float32)
    lam = jnp.exp(jnp.sum(lv[0] * lv[1])) - jnp.exp(jnp.sum(lv[2] * lv[3])) + lam_init
    kpos = jnp.arange(S, dtype=jnp.int32)
    qb = q.reshape(B, nb, Q_BLOCK, DA_HEADS, 2, DA_HEAD_DIM).transpose(1, 0, 2, 3, 4, 5)
    starts = jnp.arange(nb, dtype=jnp.int32) * Q_BLOCK

    def block(args):
        qi, start = args
        s = jnp.einsum('bqhmd,bkhmd->bhmqk', qi, k,
                       preferred_element_type=jnp.float32) * scale
        dist = (start + jnp.arange(Q_BLOCK, dtype=jnp.int32))[:, None] - kpos[None, :]
        bias = rel_bias.astype(jnp.float32)[t5_causal_bucket(jnp.maximum(dist, 0))]
        s = s + bias.transpose(2, 0, 1)[None, :, None]
        s = jnp.where(dist >= 0, s, -jnp.inf)
        p = jax.nn.softmax(s, axis=-1)
        w = p[:, :, 0] - lam * p[:, :, 1]
        return jnp.einsum('bhqk,bkhe->bqhe', w.astype(v.dtype), v)

    o = lax.map(block, (qb, starts))
    o = o.transpose(1, 0, 2, 3, 4).reshape(B, S, DA_HEADS, DA_V_DIM)
    o = rms_norm(o, subln_g) * (1.0 - lam_init)
    return o.reshape(B, S, DA_WIDTH)

def short_conv(x, w):
    C = x.shape[-1]
    y = lax.conv_general_dilated(x, w[:, None, :].astype(x.dtype), window_strides=(1,),
                                 padding=[(DN_CONV - 1, 0)],
                                 dimension_numbers=('NWC', 'WIO', 'NWC'),
                                 feature_group_count=C)
    return jax.nn.silu(y)

def gated_delta_rule(q, k, v, g, beta):
    B, S, H, dk = q.shape
    dv = v.shape[-1]
    C = DN_CHUNK
    N = S // C
    f32 = jnp.float32
    out_dtype = v.dtype

    def chunk(t):
        return jnp.moveaxis(t.reshape((B, N, C, H) + t.shape[3:]), 3, 1)

    q = chunk(l2norm(q.astype(f32)) * dk ** -0.5)
    k = chunk(l2norm(k.astype(f32)))
    v = chunk(v.astype(f32))
    g = chunk(g.astype(f32))
    beta = chunk(beta.astype(f32))
    G = jnp.cumsum(g, axis=-1)
    idx = jnp.arange(C)
    causal = idx[:, None] >= idx[None, :]
    strict = idx[:, None] > idx[None, :]
    decay = jnp.exp(jnp.where(causal, G[..., :, None] - G[..., None, :], -jnp.inf))
    k_beta = k * beta[..., None]
    v_beta = v * beta[..., None]
    lower = jnp.where(strict, jnp.einsum('bhnid,bhnjd->bhnij', k_beta, k) * decay, 0.0)
    rhs = jnp.concatenate([v_beta, k_beta * jnp.exp(G)[..., None]], axis=-1)
    sol = lax.linalg.triangular_solve(lower + jnp.eye(C, dtype=f32), rhs, left_side=True,
                                      lower=True, unit_diagonal=True)
    u, w = sol[..., :dv], sol[..., dv:]
    intra = jnp.where(causal, jnp.einsum('bhnid,bhnjd->bhnij', q, k) * decay, 0.0)
    q_dec = q * jnp.exp(G)[..., None]
    k_tail = k * jnp.exp(G[..., -1:] - G)[..., None]
    decay_last = jnp.exp(G[..., -1])

    def step(state, xs):
        qd, kt, u_c, w_c, a_c, dl = xs
        v_new = u_c - jnp.einsum('bhcd,bhde->bhce', w_c, state)
        o = jnp.einsum('bhcd,bhde->bhce', qd, state) + jnp.einsum('bhij,bhje->bhie', a_c, v_new)
        state = state * dl[..., None, None] + jnp.einsum('bhcd,bhce->bhde', kt, v_new)
        return state, o

    xs = tuple(jnp.moveaxis(a, 2, 0) for a in (q_dec, k_tail, u, w, intra, decay_last))
    _, o = lax.scan(step, jnp.zeros((B, H, dk, dv), f32), xs)
    return o.transpose(1, 0, 3, 2, 4).reshape(B, S, H, dv).astype(out_dtype)

def memory_attention(q, mk, mv):
    s = jnp.einsum('bshd,bmhd->bhsm', q, mk, preferred_element_type=jnp.float32) * CA_HEAD_DIM ** -0.5
    p = jax.nn.softmax(s, axis=-1)
    o = jnp.einsum('bhsm,bmhd->bshd', p.astype(mv.dtype), mv)
    return o.reshape(q.shape[0], q.shape[1], CA_WIDTH)

def setup_inputs(seed: int = 0) -> dict:
    key = jax.random.key(seed)
    ks = jax.random.split(key, 24)
    nrm = jax.random.normal
    f32 = jnp.float32
    return {
        "x": nrm(ks[0], (BATCH, SEQ, D_MODEL), f32),
        "mem": nrm(ks[1], (BATCH, MEM_LEN, D_MODEL), f32),
        "rel_bias": 0.5 * nrm(ks[2], (REL_BUCKETS, DA_HEADS), f32),
        "w_in": nrm(ks[3], (DEPTH, D_MODEL, IN_WIDTH), f32) * D_MODEL ** -0.5,
        "conv_w": nrm(ks[4], (DEPTH, DN_CONV, 2 * DN_QK + DN_WIDTH), f32) * DN_CONV ** -0.5,
        "dn_a_log": jnp.log(jax.random.uniform(ks[5], (DEPTH, DN_HEADS), f32, 1.0, 16.0)),
        "dn_dt_bias": 0.1 * nrm(ks[6], (DEPTH, DN_HEADS), f32),
        "dn_norm_g": 1.0 + 0.1 * nrm(ks[7], (DEPTH, DN_VAL_DIM), f32),
        "da_lambda": 0.1 * nrm(ks[8], (DEPTH, 4, DA_HEAD_DIM), f32),
        "da_subln_g": 1.0 + 0.1 * nrm(ks[9], (DEPTH, DA_V_DIM), f32),
        "mem_norm_g": 1.0 + 0.1 * nrm(ks[10], (DEPTH, D_MODEL), f32),
        "w_mem_kv": nrm(ks[11], (DEPTH, D_MODEL, 2 * CA_WIDTH), f32) * D_MODEL ** -0.5,
        "w_branch": nrm(ks[12], (DEPTH, N_BRANCH, BRANCH_WIDTH, D_MODEL), f32) * BRANCH_WIDTH ** -0.5,
        "w_out": nrm(ks[13], (DEPTH, D_MODEL, D_MODEL), f32) * D_MODEL ** -0.5,
        "ln_mix_pre": 1.0 + 0.1 * nrm(ks[14], (DEPTH, D_MODEL), f32),
        "ln_mix_post": 1.0 + 0.1 * nrm(ks[15], (DEPTH, D_MODEL), f32),
        "ln_ff_pre": 1.0 + 0.1 * nrm(ks[16], (DEPTH, D_MODEL), f32),
        "ln_ff_post": 1.0 + 0.1 * nrm(ks[17], (DEPTH, D_MODEL), f32),
        "w_ff1": nrm(ks[18], (DEPTH, D_MODEL, D_FF), f32) * D_MODEL ** -0.5,
        "w_ff2": nrm(ks[19], (DEPTH, D_FF, D_MODEL), f32) * D_FF ** -0.5,
    }

def reference(x, mem, rel_bias, w_in, conv_w, dn_a_log, dn_dt_bias, dn_norm_g, da_lambda,
              da_subln_g, mem_norm_g, w_mem_kv, w_branch, w_out, ln_mix_pre, ln_mix_post,
              ln_ff_pre, ln_ff_post, w_ff1, w_ff2):
    B, S = x.shape[0], x.shape[1]
    h = x
    for l in range(DEPTH):
        n = rms_norm(h, ln_mix_pre[l])
        (da_q, da_k, da_v, dn_q, dn_k, dn_v, dn_z, dn_b, dn_a, ca_q, gate_logits) = [
            n @ wp for wp in jnp.split(w_in[l], SPLIT_IDX, axis=-1)]

        y_a = diff_attention(da_q.reshape(B, S, DA_HEADS, 2, DA_HEAD_DIM),
                             da_k.reshape(B, S, DA_HEADS, 2, DA_HEAD_DIM),
                             da_v.reshape(B, S, DA_HEADS, DA_V_DIM),
                             rel_bias, da_lambda[l], da_subln_g[l], lambda_init(l))

        qkv = short_conv(jnp.concatenate([dn_q, dn_k, dn_v], axis=-1), conv_w[l])
        cq, ck, cv = jnp.split(qkv, (DN_QK, 2 * DN_QK), axis=-1)
        beta = jax.nn.sigmoid(dn_b.astype(jnp.float32))
        g = -jnp.exp(dn_a_log[l].astype(jnp.float32)) * jax.nn.softplus(
            dn_a.astype(jnp.float32) + dn_dt_bias[l].astype(jnp.float32))
        o_dn = gated_delta_rule(cq.reshape(B, S, DN_HEADS, DN_KEY_DIM),
                                ck.reshape(B, S, DN_HEADS, DN_KEY_DIM),
                                cv.reshape(B, S, DN_HEADS, DN_VAL_DIM), g, beta)
        y_b = (rms_norm(o_dn, dn_norm_g[l])
               * jax.nn.silu(dn_z.reshape(B, S, DN_HEADS, DN_VAL_DIM))).reshape(B, S, DN_WIDTH)

        mkv = rms_norm(mem, mem_norm_g[l]) @ w_mem_kv[l]
        mk, mv = jnp.split(mkv, 2, axis=-1)
        Mn = mem.shape[1]
        y_c = memory_attention(ca_q.reshape(B, S, CA_HEADS, CA_HEAD_DIM),
                               mk.reshape(B, Mn, CA_HEADS, CA_HEAD_DIM),
                               mv.reshape(B, Mn, CA_HEADS, CA_HEAD_DIM))

        ys = jnp.stack([y_a, y_b, y_c], axis=2)
        proj = jnp.einsum('bsiw,iwd->bsid', ys, w_branch[l])
        gates = jax.nn.sigmoid(gate_logits.reshape(B, S, N_BRANCH, D_MODEL))
        mixed = jnp.sum(gates * proj, axis=2)
        h = h + rms_norm(mixed @ w_out[l], ln_mix_post[l])

        n = rms_norm(h, ln_ff_pre[l])
        f = jnp.square(jax.nn.relu(n @ w_ff1[l])) @ w_ff2[l]
        h = h + rms_norm(f, ln_ff_post[l])
    return h


_drawn_inputs = setup_inputs


def setup_inputs(seed=0):
    import zlib

    import numpy as np

    out = dict(_drawn_inputs(seed))
    spreads = {}
    factors = {'dn_dt_bias': 36.675,
     'mem_norm_g': 4.746,
     'dn_a_log': 3.177,
     'dn_norm_g': 4.55,
     'da_subln_g': 2.768}
    for name, (base, spread) in spreads.items():
        noise = np.random.default_rng([zlib.crc32(name.encode()), seed]).standard_normal(out[name].shape)
        drawn = base * np.exp(spread * noise) if base else spread * noise
        out[name] = __import__('jax').numpy.asarray(drawn.astype(out[name].dtype))
    for name, factor in factors.items():
        out[name] = (out[name] * factor).astype(out[name].dtype)
    return out
```

```python
import math
from contextlib import ExitStack

import numpy as np

import concourse.bass as bass
from concourse import mybir

F32 = mybir.dt.float32
F32R = mybir.dt.float32r
I32 = mybir.dt.int32
ALU = mybir.AluOpType
ACT = mybir.ActivationFunctionType
AX_X = mybir.AxisListType.X

P = 128
D = 1024
S = 512
KT = D // P
ST = S // P
MEM = 256
MT = MEM // P
DFF = 4 * D
HA, DA = 8, 64
HB = 8
HC = 4
EPS = 1e-6
LAM_INIT = 0.8 - 0.6 * math.exp(-0.3 * 0)
BUCKETS, MAX_EXACT, MAX_DIST = 32, 16, 128
SPAN = 3 * P
NEG = -1e30
NM = 7

COL = {"aq": 0, "ak": D, "av": 2 * D, "dq": 3 * D, "dk": 4 * D, "dv": 5 * D, "dz": 6 * D,
       "ba": 7 * D, "cq": 7 * D + 2 * HB, "gate": 8 * D + 2 * HB}

RAW, SPL = 3, 3

C_ID, C_UPTO, C_AFTER, C_MASK0, C_CAUS = 0, 1, 2, 3, 3 + NM
NCONST = 4 + NM
PC_PRE, PC_MEM, PC_FF = 0, 8, 16
PC_SUB, PC_DNG = 24, 25
PC_CONV = 26
PC_ALOG = PC_CONV + 96
PC_DTB = PC_ALOG + HB
PC_LAM = PC_DTB + HB
NPAR = PC_LAM + 4 * DA

PARTS = {"mv": "A", "cs": "AD", "ct": "A", "cv": "A", "av": "A", "as0": "A", "as1": "AD", "at": "A",
         "ap": "AD", "ay": "A",
         "dq": "AD", "dk": "AD", "dv": "DP", "dE": "A", "dqT": "AD", "dqd": "A", "dkT": "AP",
         "dkb": "AP", "dL": "D", "dA": "DP", "T1": "A", "Za": "A", "Wb": "DP", "Wl": "D", "Tc": "A",
         "dU": "A", "dW": "A", "sa": "D", "sb": "AD", "dO": "D"}
COVER = {"cs": 3, "cv": 2, "as0": 3, "as1": 4, "at": 2, "ap": 2, "dq": 2, "dk": 2}


def attn_steps():
    out = [("mv", 0), ("mv", 1)]
    for h in range(HC):
        out += [("cs", h), ("ct", h), ("cv", h)]
    for h in range(HA):
        out += [("av", h), ("as0", h), ("as1", h), ("at", h), ("ap", h), ("ay", h)]
    return out


def delta_steps():
    out = []
    for p in range(HB // 2):
        out += [(k, p, 0) for k in ("dq", "dk", "dv", "dE", "dqT", "dqd", "dkT", "dkb", "dL", "dA", "T1")]
        for lv in range(1, NM):
            out += [("Za", p, lv), ("Wb" if lv < NM - 1 else "Wl", p, lv)]
            if lv < NM - 1:
                out.append(("Tc", p, lv))
        out += [("dU", p, 0), ("dW", p, 0)]
        for c in range(ST):
            if c:
                out.append(("sa", p, c))
            out.append(("sb", p, c))
        out.append(("dO", p, 0))
    return out


def plan_mixing():
    attn, delta = attn_steps(), delta_steps()
    groups = [[("mk", j) for j in range(KT)] + [("mv", j) for j in range(KT)]]

    def pair(p):
        return [(k, 2 * p + i) for k in ("dq", "dk", "dv") for i in range(2)]

    def z(p):
        return [("dz", 2 * p + i) for i in range(2)]

    def a(h):
        return [("aq", h), ("ak", h), ("av", h)]

    groups += [pair(0), z(0), [("cq", 0), ("cq", 1)], [("cq", 2), ("cq", 3)],
               [("cq", 4), ("cq", 5)], [("cq", 6), ("cq", 7)], a(0), a(1), pair(1), z(1), a(2), a(3),
               a(4), pair(2), z(2), a(5), a(6), pair(3), a(7), z(3)]
    gates = [("gate", i * KT + m) for i in (2, 0, 1) for m in range(KT)]
    tiles, slots = [], []
    done = {}
    evac = {}
    need_free = {}
    for p in range(1, HB // 2):
        for k in ("dq", "dk", "dv"):
            for i in range(2):
                need_free[(k, 2 * p + i)] = ("dv", p - 1, 0)
        for i in range(2):
            need_free[("dz", 2 * p + i)] = ("dO", p - 1, 0)
    for j in range(2 * HC):
        need_free[("cq", j)] = ("mv", 1) if j < 4 else ("cs", j // 2 - 2)
    for h in range(HA):
        for k in ("aq", "ak", "av"):
            need_free[(k, h)] = ("cv", HC - 1) if h < 2 else ("as1", h - 2)
    need_tile = {}
    need_tile[("mv", 0)] = need_tile[("mv", 1)] = ("mv", KT - 1)
    for h in range(HC):
        need_tile[("cs", h)] = ("cq", 2 * h + 1)
    for h in range(HA):
        need_tile[("av", h)] = ("av", h)
    for p in range(HB // 2):
        need_tile[("dq", p, 0)] = ("dv", 2 * p + 1)
        need_tile[("dO", p, 0)] = ("dz", 2 * p + 1)
    ai = di = 0
    a_next = d_next = 0
    finish = {}
    todo = [g for g in groups]
    now = []
    half = 0
    slot = 0
    while todo or gates or now or ai < len(attn) or di < len(delta) or finish.get(slot):
        if not now:
            if todo and all(need_free.get(t) is None or need_free[t] in done for t in todo[0][:1]):
                now = list(todo.pop(0))
            elif gates:
                now = [gates.pop(0)]
        main = ev = None
        if now:
            main = (len(tiles), half)
            if half == 1:
                t = now.pop(0)
                tiles.append(t)
                ev = len(tiles) - 1
                evac[t] = slot
                if t[0] in ("dq", "dk", "dv", "dz"):
                    finish[slot + 1] = ev
                    evac[t] = slot + 1
            half ^= 1
        sa = sd = None
        if ai < len(attn) and slot >= a_next:
            t = need_tile.get(attn[ai])
            if t is None or evac.get(t, slot + 9) < slot:
                sa = ai
                done[attn[ai]] = slot
                a_next = slot + COVER.get(attn[ai][0], 1)
                ai += 1
        if di < len(delta) and slot >= d_next:
            t = need_tile.get(delta[di])
            if t is None or evac.get(t, slot + 9) < slot:
                sd = di
                done[delta[di]] = slot
                d_next = slot + COVER.get(delta[di][0], 1)
                di += 1
        slots.append((main, ev, finish.get(slot), sa, sd))
        slot += 1
    return tiles, slots, need_free


def plan_tiles():
    tiles, slots, need_free = plan_mixing()
    n_mix = len(tiles)
    tiles = list(tiles)
    for i in (2, 0, 1):
        tiles += [("br", i * KT + m) for m in range(KT)]
    tiles += [("out", m) for m in range(KT)]
    for half in range(2):
        tiles += [("f1", half * 16 + f) for f in range(16)]
        tiles += [("f2", (2 * half + g) * KT + m) for m in range(KT) for g in range(2)]
    return tiles, n_mix, slots, need_free


def counts(steps, part):
    out = [0]
    for s in steps:
        out.append(out[-1] + (part in PARTS[s[0]]))
    return out


def kinds_before(steps, names):
    out = [0]
    for s in steps:
        out.append(out[-1] + (s[0] in names))
    return out


def view(ap, dims, offset=0):
    return bass.AP(tensor=ap.tensor, offset=ap.offset + offset, ap=[list(ap.ap[0])] + [list(d) for d in dims])


def along(ap, n):
    return view(ap, [list(ap.ap[1]), [0, n]])


def over(ap, m):
    return view(ap, [[0, m], list(ap.ap[1])])


def flat(ap3):
    return ap3.rearrange("p a b -> p (a b)")


def build(nc, weights, x, mem, w_ba, params, consts, onehot, relb, post_g, y_dram, gate_dram, f_dram, frep_dram, out):
    TILES, N_MIX, SLOTS, NEED_FREE = plan_tiles()
    NT = len(TILES)
    ATTN, DELTA = attn_steps(), delta_steps()
    a_idx = {s: i for i, s in enumerate(ATTN)}
    d_idx = {s: i for i, s in enumerate(DELTA)}
    aA, aD = counts(ATTN, "A"), counts(ATTN, "D")
    dA, dD, dP = counts(DELTA, "A"), counts(DELTA, "D"), counts(DELTA, "P")
    n_max = kinds_before(ATTN, ("cs", "as0", "as1"))
    n_spill = kinds_before(ATTN, ("cv", "ay"))
    conv_tiles = [t for t in range(N_MIX) if TILES[t][0] in ("dq", "dk", "dv")]
    z_tiles = [t for t in range(N_MIX) if TILES[t][0] == "dz"]
    gate_tiles = [t for t in range(N_MIX) if TILES[t][0] == "gate"]
    n_conv = {t: i for i, t in enumerate(conv_tiles)}
    n_z = {t: i for i, t in enumerate(z_tiles)}
    n_gate = {t: i for i, t in enumerate(gate_tiles)}
    SC_A = DA ** -0.5
    SC_C = (D // HC) ** -0.5

    with ExitStack() as ctx:
        def sem(name):
            return ctx.enter_context(nc.semaphore(name))

        def sb_in(c):
            return lambda name, shape, dt=F32: c.enter_context(nc.sbuf_tensor(name, shape, dt))

        sb = sb_in(ctx)
        acc = ctx.enter_context(nc.psum_tensor("acc", [P, 2, 512], F32))
        ps_a = ctx.enter_context(nc.psum_tensor("ps_a", [P, 3, 512], F32))
        ps_d = ctx.enter_context(nc.psum_tensor("ps_d", [P, 3, 512], F32))
        side = [ps_a, ps_d]

        w_raw = sb("w_raw", [P, RAW, KT, P])
        w_hi = sb("w_hi", [P, SPL, KT, P], F32R)
        w_lo = sb("w_lo", [P, SPL, KT, P], F32R)
        cst = sb("cst", [P, NCONST, P])
        par = sb("par", [P, NPAR])
        ones = sb("ones", [P, P])
        sml = sb("sml", [P, 160])
        smd = sb("smd", [P, 96])
        ident = cst[:, C_ID, :]

        mix = ExitStack()
        sm = sb_in(mix)
        n_hi = sm("n_hi", [P, KT, S], F32R)
        n_lo = sm("n_lo", [P, KT, S], F32R)
        strip = sm("strip", [P, HA, 2 * P])
        beta = sm("beta", [P, HB, ST])
        hbeta = sm("hbeta", [P, HB, ST])
        gdec = sm("gdec", [P, HB, ST])
        e_in = sm("e_in", [P, HB, ST])
        e_tail = sm("e_tail", [P, HB, ST])
        e_all = sm("e_all", [P, HB, ST])
        conv_x = sm("conv_x", [P, 2, S + 4])
        conv_y = sm("conv_y", [P, 2, S])
        conv_o = sm("conv_o", [P, 3, 2, S])
        zs = sm("zs", [P, 2, S])
        z_t = sm("z_t", [P, S])
        y_st = sm("y_st", [P, 2, S])
        gate_st = sm("gate_st", [P, S])
        state = sm("state", [P, 2, P])
        vnew = sm("vnew", [P, 2, P])

        first = ExitStack()
        sf = sb_in(first)
        x_tok = sf("x_tok", [P, ST, D])
        m_tok = sf("m_tok", [P, MT, D])
        m_hi = sf("m_hi", [P, KT, MEM], F32R)
        m_lo = sf("m_lo", [P, KT, MEM], F32R)
        full = sf("full", [P, 2, S])
        ba = sf("ba", [P, 6, HB, ST])
        first.close()
        dl = ExitStack()
        sd_ = sb_in(dl)
        names = ["Q", "SCR", "K", "KB", "V", "QT", "QDT", "KTT", "KBT", "ET", "LT", "AT", "TT"]
        B = {n: sd_("d_" + n, [P, 8, P]) for n in names}
        Q, SCR, K, KB, V, QT, QDT, KTT, KBT, ET, LT, AT, TT = (B[n] for n in names)
        XT, TN, Z, U, WT, O = KBT, QT, KTT, Q, SCR, LT

        c1 = ExitStack()
        sc_ = sb_in(c1)
        mk_T = sc_("mk_T", [P, KT, MEM])
        mv_tok = sc_("mv_tok", [P, MT, D])
        p_c = sc_("p_c", [P, ST, MEM])
        pT_c = sc_("pT_c", [P, MT, S])
        c1.close()
        c2 = ExitStack()
        sa_ = sb_in(c2)
        p_a = sa_("p_a", [P, 2, 10 * P])
        wT = sa_("wT", [P, 10 * P])
        v_tok = sa_("v_tok", [P, S])
        o_a = sa_("o_a", [P, ST, P])
        hold = sa_("hold", [P, 1280])
        c3 = ExitStack()
        s3 = sb_in(c3)
        mv_T = s3("mv_T", [P, KT, MEM])
        w_ba_sb = s3("w_ba_sb", [P, KT, 2 * HB])
        wb_hi = s3("wb_hi", [P, KT, 2 * HB], F32R)
        wb_lo = s3("wb_lo", [P, KT, 2 * HB], F32R)
        c3.close()
        c3 = ExitStack()
        s3 = sb_in(c3)
        cq_T = s3("cq_T", [P, 2, 2, S])
        c3.close()
        c3 = ExitStack()
        s3 = sb_in(c3)
        qkv_T = s3("qkv_T", [P, 2, 3, S])
        onehot_sb = strip[0:BUCKETS, 0:2, :].rearrange("p a b -> p (a b)")[:, 0:SPAN]
        c3.close()
        c2.close()
        dl.close()
        mix.close()

        late = ExitStack()
        sl = sb_in(late)
        mx_hi = sl("mx_hi", [P, KT, S], F32R)
        mx_lo = sl("mx_lo", [P, KT, S], F32R)
        y_raw = sl("y_raw", [P, KT, S])
        mix_acc = sl("mix_acc", [P, KT, S])
        y_hi = sl("y_hi", [P, 2, KT, S], F32R)
        y_lo = sl("y_lo", [P, 2, KT, S], F32R)
        g_in = sl("g_in", [P, 3, S])
        g_tmp = sl("g_tmp", [P, S])
        late.close()
        late = ExitStack()
        sl = sb_in(late)
        h_lo = sl("h_lo", [P, 2 * KT, S], F32R)
        h1 = sl("h1", [P, ST, D])
        post = sl("post", [P, 2, D])
        f_T = sl("f_T", [P, KT, S])
        tok = sl("tok", [P, D])
        rows = sl("rows", [P, D])
        junk = sl("junk", [P, D])
        n2_hi = sl("n2_hi", [P, KT, S], F32R)
        n2_lo = sl("n2_lo", [P, KT, S], F32R)
        h_hi = sl("h_hi", [P, 2 * KT, S], F32R)
        relu = sl("relu", [P, 2, S])
        sq = sl("sq", [P, 2, S])
        late.close()

        ld = [sem(f"ld{i}") for i in range(RAW)]
        hi_ready = sem("hi_ready")
        lo_ready = sem("lo_ready")
        tile_used = sem("tile_used")
        acc_free = sem("acc_free")
        in_par, in_x, in_mem, in_oh, in_ba, in_relb, in_cst = (
            sem(n) for n in ("in_par", "in_x", "in_mem", "in_oh", "in_ba", "in_relb", "in_cst"))
        ones_set = sem("ones_set")
        pad_set = sem("pad_set")
        vch = sem("vch")
        ach = sem("ach")
        pch = sem("pch")
        su_sq = sem("su_sq")
        su_norm = sem("su_norm")
        su_tr = sem("su_tr")
        su_full = sem("su_full")
        su_hi = sem("su_hi")
        su_lo = sem("su_lo")
        ba_split = sem("ba_split")
        ba_mm = sem("ba_mm")
        ba_act = sem("ba_act")
        ba_dve = sem("ba_dve")
        g_ready = sem("g_ready")
        g_mm = sem("g_mm")
        g_exp = sem("g_exp")
        f_mm = sem("f_mm")
        f_sb = sem("f_sb")
        f_out = sem("f_out")
        f_rep = sem("f_rep")
        strip_in = sem("strip_in")
        strip_ok = sem("strip_ok")
        lam_sum = sem("lam_sum")
        lam_exp = sem("lam_exp")
        a_mm = sem("a_mm")
        a_act = sem("a_act")
        a_dve = sem("a_dve")
        a_max = sem("a_max")
        d_mm = sem("d_mm")
        d_act = sem("d_act")
        d_dve = sem("d_dve")
        d_pool = sem("d_pool")
        cx_ready = sem("cx_ready")
        cy_ready = sem("cy_ready")
        ct_ready = sem("ct_ready")
        co_ready = sem("co_ready")
        zt_ready = sem("zt_ready")
        z_ready = sem("z_ready")
        y_out = sem("y_out")
        yb_out = sem("yb_out")
        gs_ready = sem("gs_ready")
        g_out = sem("g_out")
        y_in = [sem(f"y_in{i}") for i in range(3)]
        yh_ready = sem("yh_ready")
        yl_ready = sem("yl_ready")
        gin = [sem(f"gin{i}") for i in range(3)]
        gated = sem("gated")
        merged = sem("merged")
        mxh_ready = sem("mxh_ready")
        mxl_ready = sem("mxl_ready")
        o_ev = sem("o_ev")
        tr1 = sem("tr1")
        ss1 = sem("ss1")
        t1d = sem("t1d")
        ss2 = sem("ss2")
        n2n = sem("n2n")
        tr2 = sem("tr2")
        n2f = sem("n2f")
        n2h = sem("n2h")
        n2l = sem("n2l")
        in_x2, in_post = sem("in_x2"), sem("in_post")
        relu_ok = sem("relu_ok")
        sq_ok = sem("sq_ok")
        hh_ok = sem("hh_ok")
        hl_ok = sem("hl_ok")
        f_ev = sem("f_ev")
        tr3 = sem("tr3")
        ss3 = sem("ss3")
        fin = sem("fin")
        o_done = sem("o_done")

        block = ctx.enter_context(nc.Block())

        LAMS, LAME, NLAM = smd[:, 2:4], smd[:, 4:6], smd[:, 6:7]
        relb_sb = sml[0:BUCKETS, 32:32 + HA]
        ealog = sml[:, 64:64 + HB]
        f_row = qkv_T[0:HA, 1, 2, 0:SPAN]
        p_a_scr = flat(conv_o[:, 0])
        lam_prod = z_t[:, 0:2 * DA].rearrange("p (a d) -> p a d", a=2)
        BR = (2, 0, 1)
        N_BR = 3 * KT
        Y_AT = {0: 0, 2: 1, KT: 2}
        G_SLOT = 8
        BIAS_SLOTS = [10, 16, 26]
        GSUB, GDN = smd[:, 7:8], smd[:, 8:9]
        mxa, nba = smd[:, 16:20], smd[:, 20:24]
        sma, rca = smd[:, 24:32], smd[:, 32:40]
        ssa, rsa, tma = smd[:, 40:44], smd[:, 44:48], smd[:, 48:52]
        ssd, rsd, tmd = smd[:, 56:64], smd[:, 64:72], smd[:, 72:80]

        N_SU = MT * 2 + KT
        bank_of = {3: 0, 2: 512 + 128, 1: 1024 + 256, 0: 512}
        pack_of = {0: 0, 1: P, 2: 3 * P, 3: 6 * P}

        def t_bank(kt, q):
            return {0: q * P, 1: 512 + q * P, 2: 1024 + q * P, 3: 512}[kt]

        def t_pack(kt, q):
            return t_bank(kt, q) if kt != 2 else 1024 + (q - 2) * P

        LATE = []
        t = N_MIX
        while t < NT:
            k = 2 if TILES[t][0] == "f2" else 1
            LATE.append((TILES[t], t, k))
            t += k
        L_F1 = [32, 56]
        L_F2 = [48, 72]

        def tiles_of(n):
            return LATE[n][1] if n < len(LATE) else NT

        def two(ps):
            return flat(ps[:])[:, 0:1024]

        def blocks(ap):
            return ap.rearrange("p (a b) -> p a b", b=P)

        @block.sync
        def _(sp):
            sp.dma_start(m_tok[:], mem.rearrange("(t p) d -> p t d", p=P)).then_inc(in_mem, 16)
            sp.dma_start(cst[:], consts).then_inc(in_cst, 16)
            sp.dma_start(par[:], params).then_inc(in_par, 16)
            sp.dma_start(x_tok[:], x.rearrange("(t p) d -> p t d", p=P)).then_inc(in_x, 16)
            sp.dma_start(w_ba_sb[:], w_ba).then_inc(in_ba, 16)
            sp.dma_start(onehot_sb, onehot).then_inc(in_oh, 16)
            sp.dma_start(relb_sb, relb).then_inc(in_relb, 16)

            def load(t):
                if t < NT:
                    if t >= RAW:
                        sp.wait_ge(lo_ready, t - RAW + 1)
                    sp.dma_start(w_raw[:, t % RAW], weights[t]).then_inc(ld[t % RAW], 16)

            for t in range(RAW):
                load(t)
            def bias(step):
                if step == 0:
                    sp.wait_ge(f_sb, 1)
                    sp.dma_start(f_dram, f_row).then_inc(f_out, 16)
                elif step == 1:
                    sp.wait_ge(f_out, 16)
                    sp.dma_start(frep_dram, bass.AP(tensor=f_dram.tensor, offset=f_dram.offset,
                                                    ap=[[SPAN, HA], [0, P], [1, SPAN]])).then_inc(f_rep, 16)
                elif step == 2:
                    sp.wait_ge(f_rep, 16)
                    sp.dma_start(strip[:], bass.AP(tensor=frep_dram.tensor, offset=frep_dram.offset + P - 1,
                                                   ap=[[SPAN - 1, P], [P * SPAN, HA], [1, 2 * P]])).then_inc(strip_in, 16)

            for n, (main, ev, fi, sa, sd) in enumerate(SLOTS):
                if n in BIAS_SLOTS:
                    bias(BIAS_SLOTS.index(n))
                if ev is not None:
                    load(ev + RAW)
                    if TILES[ev][0] == "gate":
                        n = n_gate[ev]
                        sp.wait_ge(gs_ready, n + 1)
                        sp.dma_start(gate_dram[TILES[ev][1]], gate_st[:]).then_inc(g_out, 16)
                if sa is not None and ATTN[sa][0] in ("cv", "ay"):
                    kind, h = ATTN[sa]
                    sp.wait_ge(a_act, aA[sa + 1])
                    if kind == "cv":
                        sp.dma_start(y_dram[2, :, 2 * h:2 * h + 2], y_st[:]).then_inc(y_out, 16)
                    else:
                        sp.dma_start(y_dram[0, :, h], y_st[:, 0]).then_inc(y_out, 16)
                if sd is not None and DELTA[sd][0] == "dO":
                    p = DELTA[sd][1]
                    sp.wait_ge(d_dve, dD[sd + 1])
                    sp.dma_start(y_dram[1, :, 2 * p:2 * p + 2],
                                 flat(ET[:]).rearrange("p (a b) -> p a b", a=2)).then_inc(yb_out, 16)
            sp.wait_ge(y_out, 16 * n_spill[-1])
            sp.wait_ge(yb_out, 16 * (HB // 2))
            sp.wait_ge(g_out, 16 * len(gate_tiles))
            sp.wait_ge(tile_used, N_MIX)
            sp.wait_ge(acc_free, N_MIX)
            for r, (tile, t0, k) in enumerate(LATE):
                if r < N_BR:
                    b, m = r // KT, r % KT
                    if r in Y_AT:
                        n = Y_AT[r]
                        if n:
                            sp.wait_ge(yl_ready, KT * n)
                        sp.dma_start(y_raw[:], y_dram[BR[n]]).then_inc(y_in[n], 16)
                    if r >= 3:
                        sp.wait_ge(gated, r - 2)
                    sp.dma_start(g_in[:, r % 3], gate_dram[tile[1]]).then_inc(gin[r % 3], 16)
                if r == N_BR + 2:
                    sp.wait_ge(tile_used, tiles_of(N_BR))
                    sp.wait_ge(mxl_ready, KT)
                    sp.dma_start(post[:], post_g).then_inc(in_post, 16)
                    sp.dma_start(h1[:], x.rearrange("(t p) d -> p t d", p=P)).then_inc(in_x2, 16)
                for j in range(k):
                    load(t0 + j + RAW)
            for i in range(ST):
                sp.wait_ge(fin, i + 1)
                sp.dma_start(out[i * P:(i + 1) * P, :], h1[:, i]).then_inc(o_done, 16)
            sp.wait_ge(o_done, 16 * ST)

        @block.gpsimd
        def _(pool):
            def split_lo(t):
                if t < NT:
                    pool.wait_ge(hi_ready, t + 1)
                    if t >= SPL:
                        pool.wait_ge(tile_used, t - SPL + 1)
                    nc.gpsimd.tensor_tensor(w_lo[:, t % SPL], w_raw[:, t % RAW],
                                            w_hi[:, t % SPL].bitcast(F32), ALU.subtract).then_inc(lo_ready, 1)

            nc.gpsimd.memset(ones[:], 1.0).then_inc(ones_set, 1)
            nc.gpsimd.memset(conv_x[:, :, 0:3], 0.0).then_inc(pad_set, 1)
            for j in range(N_SU):
                pool.wait_ge(su_full, j + 1)
                pool.wait_ge(su_hi, j + 1)
                if j < 4:
                    dst, hi = m_lo[:, 2 * j:2 * j + 2], m_hi[:, 2 * j:2 * j + 2]
                    src = full[:, j % 2].rearrange("p (a b) -> p a b", a=2)
                else:
                    dst, hi, src = n_lo[:, j - 4], n_hi[:, j - 4], full[:, j % 2]
                nc.gpsimd.tensor_tensor(dst, src, hi.bitcast(F32), ALU.subtract).then_inc(su_lo, 1)
                if j == 3:
                    for t in range(SPL):
                        split_lo(t)

            def delta(i):
                kind, p, lv = DELTA[i]
                if "P" not in PARTS[kind]:
                    return
                pool.wait_ge(d_mm, i + 1)
                heads = slice(2 * p, 2 * p + 2)
                if kind == "dv":
                    pool.wait_ge(g_exp, 1)
                    last = nc.gpsimd.tensor_tensor(SCR[:], over(cst[:, C_AFTER, :], 8),
                                                   along(flat(gdec[:, heads]), P), ALU.mult)
                elif kind == "dkT":
                    last = nc.gpsimd.tensor_tensor(K[:], K[:], along(flat(e_tail[:, heads]), P), ALU.mult)
                elif kind == "dkb":
                    last = nc.gpsimd.tensor_tensor(KB[:], KB[:], along(flat(e_in[:, heads]), P), ALU.mult)
                elif kind == "dA":
                    pool.wait_ge(d_dve, dD[i + 1])
                    nc.gpsimd.tensor_tensor(AT[:], AT[:], over(cst[:, C_UPTO, :], 8), ALU.mult)
                    last = nc.gpsimd.tensor_tensor(XT[:], LT[:], over(cst[:, C_MASK0 + 1, :], 8), ALU.mult)
                elif kind == "Wb":
                    last = nc.gpsimd.tensor_tensor(XT[:], LT[:], over(cst[:, C_MASK0 + lv + 1, :], 8), ALU.mult)
                last.then_inc(d_pool, 1)

            for main, ev, fi, sa, sd in SLOTS:
                if ev is not None:
                    split_lo(ev + SPL)
                    if TILES[ev][0] == "gate":
                        n = n_gate[ev]
                        pool.wait_ge(acc_free, ev + 1)
                        nc.gpsimd.tensor_scalar(gate_st[:], gate_st[:], 0.5, 0.5, ALU.mult,
                                                ALU.add).then_inc(gs_ready, 1)
                if sd is not None:
                    delta(sd)

            def y_lo_tile(b, kk):
                pool.wait_ge(yh_ready, b * KT + kk + 1)
                if b == 2 and kk == 0:
                    pool.wait_ge(tile_used, tiles_of(KT))
                nc.gpsimd.tensor_tensor(y_lo[:, b % 2, kk], y_raw[:, kk], y_hi[:, b % 2, kk].bitcast(F32),
                                        ALU.subtract).then_inc(yl_ready, 1)

            for r, (tile, t0, k) in enumerate(LATE):
                if r in Y_AT:
                    for kk in range(KT):
                        y_lo_tile(Y_AT[r], kk)
                for j in range(k):
                    split_lo(t0 + j + SPL)
                if r < N_BR and r // KT == 2:
                    m = r % KT
                    pool.wait_ge(mxh_ready, m + 1)
                    nc.gpsimd.tensor_tensor(mx_lo[:, m], mix_acc[:, m], mx_hi[:, m].bitcast(F32),
                                            ALU.subtract).then_inc(mxl_ready, 1)
                if r == N_BR + KT - 1:
                    for i in range(ST):
                        pool.wait_ge(n2h, i + 1)
                        nc.gpsimd.tensor_tensor(n2_lo[:, :, i * P:(i + 1) * P], blocks(tok[:]),
                                                n2_hi[:, :, i * P:(i + 1) * P].bitcast(F32),
                                                ALU.subtract).then_inc(n2l, 1)
                if tile[0] == "f1":
                    f = tile[1]
                    pool.wait_ge(hh_ok, f + 1)
                    nc.gpsimd.tensor_tensor(h_lo[:, f % 16], sq[:, f % 2], h_hi[:, f % 16].bitcast(F32),
                                            ALU.subtract).then_inc(hl_ok, 1)

        @block.scalar
        def _(act):
            act.wait_ge(in_mem, 16)
            for i in range(MT + ST):
                if i == MT:
                    act.wait_ge(in_x, 16)
                src = m_tok[:, i] if i < MT else x_tok[:, i - MT]
                if i:
                    act.wait_ge(su_sq, i)
                nc.scalar.activation(p_a_scr, src, ACT.Square, accum_out=sml[:, i:i + 1]).then_inc(su_sq, 1)
            for j in range(N_SU):
                act.wait_ge(su_full, j + 1)
                if j < 4:
                    ins = nc.scalar.copy(m_hi[:, 2 * j:2 * j + 2], full[:, j % 2].rearrange("p (a b) -> p a b", a=2))
                else:
                    ins = nc.scalar.copy(n_hi[:, j - 4], full[:, j % 2])
                ins.then_inc(su_hi, 1)
            act.wait_ge(f_mm, 1)
            nc.scalar.mul(f_row, ps_a[0:HA, 0, 0:SPAN], 1.0 / SC_A).then_inc(f_sb, 1)
            act.wait_ge(lam_sum, 1)
            nc.scalar.activation(LAME, LAMS, ACT.Exp).then_inc(lam_exp, 1)
            act.wait_ge(ba_dve, 1)
            nc.scalar.activation(ba[:, 0], ba[:, 0], ACT.Tanh, scale=0.5)
            nc.scalar.activation(ba[:, 2], ba[:, 2], ACT.Exp)
            nc.scalar.activation(ealog, par[:, PC_ALOG:PC_ALOG + HB], ACT.Exp).then_inc(ba_act, 1)

            def evacuate(t):
                kind, j = TILES[t]
                bank = acc[:, t % 2]
                act.wait_ge(tile_used, t + 1)
                free = NEED_FREE.get(TILES[t])
                if free in a_idx:
                    act.wait_ge(a_mm, a_idx[free] + 1)
                elif kind == "dz" and free is not None:
                    act.wait_ge(d_dve, dD[d_idx[free] + 1])
                if kind == "mk":
                    last = nc.scalar.copy(mk_T[:, j], bank[:, 0:MEM])
                elif kind == "mv":
                    if j == 0:
                        act.wait_ge(ba_split, 1)
                    last = nc.scalar.copy(mv_T[:, j], bank[:, 0:MEM])
                elif kind == "cq":
                    last = nc.scalar.copy(cq_T[:, (j // 2) % 2, j % 2], bank)
                elif kind in ("aq", "ak", "av"):
                    if (kind, j) == ("av", 1):
                        act.wait_ge(f_out, 16)
                    last = nc.scalar.copy(qkv_T[:, j % 2, ("aq", "ak", "av").index(kind)], bank)
                elif kind in ("dq", "dk", "dv"):
                    n = n_conv[t]
                    if n == 0:
                        act.wait_ge(pad_set, 1)
                    if n >= 2:
                        act.wait_ge(co_ready, n - 1)
                    last = nc.scalar.copy(conv_x[:, n % 2, 3:3 + S], bank)
                elif kind == "dz":
                    last = nc.scalar.copy(zs[:, j % 2], bank)
                elif kind == "gate":
                    n = n_gate[t]
                    if n:
                        act.wait_ge(g_out, 16 * n)
                    last = nc.scalar.activation(gate_st[:], bank, ACT.Tanh, scale=0.5)
                last.then_inc(acc_free, 1)

            def finish(t):
                if t in n_conv:
                    n = n_conv[t]
                    act.wait_ge(cy_ready, n + 1)
                    nc.scalar.activation(conv_x[:, n % 2, 3:3 + S], conv_y[:, n % 2], ACT.Tanh,
                                         scale=0.5).then_inc(ct_ready, 1)
                else:
                    n = n_z[t]
                    if n:
                        act.wait_ge(z_ready, n)
                    act.wait_ge(acc_free, t + 1)
                    nc.scalar.activation(z_t[:], zs[:, n % 2], ACT.Tanh, scale=0.5).then_inc(zt_ready, 1)

            def attn(i):
                kind, h = ATTN[i]
                act.wait_ge(a_mm, i + 1)
                if kind == "mv":
                    last = nc.scalar.copy(mv_tok[:, :, h * 512:(h + 1) * 512], ps_a[:, 0:2])
                elif kind == "cs":
                    act.wait_ge(a_max, n_max[i + 1])
                    for s in range(ST):
                        last = nc.scalar.activation(p_c[:, s], ps_a[:, s // 2, (s % 2) * MEM:(s % 2 + 1) * MEM],
                                                    ACT.Exp, bias=nba[:, s:s + 1], scale=SC_C,
                                                    accum_out=sma[:, s:s + 1])
                elif kind == "ct":
                    last = nc.scalar.copy(pT_c[:], ps_a[:, 0:2])
                elif kind in ("cv", "ay"):
                    if n_spill[i]:
                        act.wait_ge(y_out, 16 * n_spill[i])
                    if kind == "cv":
                        last = nc.scalar.copy(y_st[:], ps_a[:, 0:2])
                    else:
                        last = nc.scalar.activation(y_st[:, 0], ps_a[:, 0], ACT.Copy, scale=GSUB)
                elif kind == "av":
                    last = nc.scalar.copy(v_tok[:], ps_a[:, 0])
                elif kind in ("as0", "as1"):
                    m = int(kind[2])
                    act.wait_ge(a_max, n_max[i + 1])
                    for q in range(ST):
                        w = (q + 1) * P
                        src = flat(ps_a[:])[:, bank_of[q]:bank_of[q] + w]
                        last = nc.scalar.activation(p_a[:, m, pack_of[q]:pack_of[q] + w], src, ACT.Exp,
                                                    bias=nba[:, q:q + 1], scale=SC_A,
                                                    accum_out=sma[:, 4 * m + q:4 * m + q + 1])
                elif kind == "at":
                    nc.scalar.copy(wT[:, 0:1024], two(ps_a))
                    last = nc.scalar.copy(wT[:, 1024:1280], ps_a[:, 2, 256:512])
                elif kind == "ap":
                    last = nc.scalar.copy(flat(o_a[:]), ps_a[:, 0])
                last.then_inc(a_act, 1)

            def delta(i):
                kind, p, c = DELTA[i]
                if "A" not in PARTS[kind]:
                    return
                act.wait_ge(d_mm, i + 1)
                if kind == "dE":
                    if p:
                        act.wait_ge(yb_out, 16 * p)
                    last = nc.scalar.activation(flat(ET[:]), two(ps_d), ACT.Exp)
                elif kind == "sb":
                    o_v = O[:].rearrange("p (h c) d -> p h c d", h=2)[:, :, c]
                    last = nc.scalar.copy(o_v, ps_d[:, 0, 0:256].rearrange("p (h d) -> p h d", h=2))
                else:
                    dst = {"dq": Q, "dk": K, "dqT": QT, "dqd": QDT, "dkT": KTT, "dkb": KBT, "T1": TN, "Tc": TN,
                           "Za": Z, "dU": U, "dW": WT}[kind]
                    last = nc.scalar.copy(flat(dst[:]), two(ps_d))
                last.then_inc(d_act, 1)

            for n, (main, ev, fi, sa, sd) in enumerate(SLOTS):
                if n == G_SLOT:
                    act.wait_ge(g_mm, 1)
                    for m, dst in enumerate((e_in, e_tail, e_all)):
                        last = nc.scalar.activation(flat(dst[:]), ps_d[:, 0, m * 32:(m + 1) * 32], ACT.Exp)
                    last.then_inc(g_exp, 1)
                if ev is not None:
                    evacuate(ev)
                if fi is not None:
                    finish(fi)
                if sa is not None:
                    attn(sa)
                if sd is not None:
                    delta(sd)

            for r in range(N_BR, N_BR + KT):
                m = r - N_BR
                act.wait_ge(tile_used, tiles_of(r + 1))
                if m == 0:
                    act.wait_ge(mxl_ready, KT)
                nc.scalar.copy(f_T[:, m], acc[:, r % 2]).then_inc(o_ev, 1)
            for i in range(ST):
                act.wait_ge(tr1, i + 1)
                nc.scalar.activation(junk[:], two(side[i % 2]), ACT.Square,
                                     accum_out=sml[:, 96 + i:97 + i]).then_inc(ss1, 1)
                act.wait_ge(t1d, i + 1)
                act.wait_ge(ss1, i + 1)
                nc.scalar.activation(junk[:], h1[:, i], ACT.Square,
                                     accum_out=sml[:, 100 + i:101 + i]).then_inc(ss2, 1)
                act.wait_ge(ss2, i + 1)
            for f in range(DFF // P):
                act.wait_ge(relu_ok, f + 1)
                if f >= 2:
                    act.wait_ge(hl_ok, f - 1)
                nc.scalar.activation(sq[:, f % 2], relu[:, f % 2], ACT.Square).then_inc(sq_ok, 1)
            for i in range(ST):
                act.wait_ge(tr3, i + 1)
                if i:
                    act.wait_ge(ss3, i)
                nc.scalar.activation(junk[:], two(side[i % 2]), ACT.Square,
                                     accum_out=sml[:, 104 + i:105 + i]).then_inc(ss3, 1)

        @block.vector
        def _(dve):
            n_own = [0]

            def link(ins):
                n_own[0] += 1
                ins.then_inc(vch, 1)
                dve.wait_ge(vch, n_own[0])

            V_ = nc.vector

            def rsqrt(dst, src, tmp):
                link(V_.tensor_scalar(tmp.bitcast(I32), src.bitcast(I32), 1, None, ALU.logical_shift_right))
                link(V_.tensor_scalar(dst.bitcast(I32), tmp.bitcast(I32), -1.0, float(0x5f3759df), ALU.mult, ALU.add))
                for _ in range(3):
                    link(V_.tensor_tensor(tmp, dst, dst, ALU.mult))
                    link(V_.scalar_tensor_tensor(out=tmp, in0=tmp, scalar=-0.5, in1=src, op0=ALU.mult, op1=ALU.mult))
                    link(V_.scalar_tensor_tensor(out=dst, in0=tmp, scalar=1.5, in1=dst, op0=ALU.add, op1=ALU.mult))

            def split_hi(t):
                if t < NT:
                    dve.wait_ge(ld[t % RAW], 16 * (t // RAW + 1))
                    if t >= SPL:
                        dve.wait_ge(tile_used, t - SPL + 1)
                        dve.wait_ge(lo_ready, t - SPL + 1)
                    V_.tensor_copy(w_hi[:, t % SPL], w_raw[:, t % RAW]).then_inc(hi_ready, 1)

            for i0, n, rows_t in ((0, MT, m_tok), (MT, ST, x_tok)):
                dve.wait_ge(su_sq, i0 + n)
                v, r, tm = sml[:, i0:i0 + n], sml[:, 8 + i0:8 + i0 + n], sml[:, 16 + i0:16 + i0 + n]
                link(V_.tensor_scalar(v, v, 1.0 / D, EPS, ALU.mult, ALU.add))
                rsqrt(r, v, tm)
                for i in range(n):
                    V_.tensor_scalar(rows_t[:, i], rows_t[:, i], r[:, i:i + 1], None, ALU.mult).then_inc(su_norm, 1)
                if i0 == 0:
                    dve.wait_ge(in_par, 16)
                for j in range(4) if i0 == 0 else range(4, N_SU):
                    dve.wait_ge(su_tr, j + 1)
                    if j >= 2:
                        dve.wait_ge(su_lo, j - 1)
                    bank = side[(j // 3) % 2][:, j % 3]
                    if j < 4:
                        V_.tensor_scalar(full[:, j % 2, 0:MEM], bank[:, 0:MEM],
                                         par[:, PC_MEM + 2 * j:PC_MEM + 2 * j + 1], None, ALU.mult)
                        last = V_.tensor_scalar(full[:, j % 2, MEM:S], bank[:, MEM:S],
                                                par[:, PC_MEM + 2 * j + 1:PC_MEM + 2 * j + 2], None, ALU.mult)
                    else:
                        last = V_.tensor_scalar(full[:, j % 2], bank, par[:, PC_PRE + j - 4:PC_PRE + j - 3], None, ALU.mult)
                    last.then_inc(su_full, 1)
                if i0 == 0:
                    for t in range(SPL):
                        split_hi(t)
                    dve.wait_ge(in_ba, 16)
                    link(V_.tensor_copy(wb_hi[:], w_ba_sb[:]))
                    V_.tensor_tensor(wb_lo[:], w_ba_sb[:], wb_hi[:].bitcast(F32), ALU.subtract).then_inc(ba_split, 1)
                    lamv = par[:, PC_LAM:PC_LAM + 4 * DA].rearrange("p (a b d) -> p a b d", a=2, b=2)
                    link(V_.tensor_tensor(lam_prod, lamv[:, :, 0], lamv[:, :, 1], ALU.mult))
                    V_.reduce_sum(LAMS, lam_prod, AX_X).then_inc(lam_sum, 1)
                    V_.tensor_scalar(GSUB, par[:, PC_SUB:PC_SUB + 1], 1.0 - LAM_INIT, None, ALU.mult)
                    V_.tensor_scalar(GDN, par[:, PC_DNG:PC_DNG + 1], 0.5, None, ALU.mult)
            dve.wait_ge(ba_mm, 1)
            bav = ps_d[:, 0, 0:ST * 2 * HB].rearrange("p (c h) -> p h c", c=ST)
            V_.tensor_copy(ba[:, 0], bav[:, 0:HB])
            link(V_.tensor_tensor(ba[:, 1], bav[:, HB:2 * HB], along(par[:, PC_DTB:PC_DTB + HB], ST), ALU.add))
            link(V_.tensor_scalar(ba[:, 2], ba[:, 1], -1.0, None, ALU.mult))
            V_.tensor_tensor(ba[:, 2], ba[:, 2], ba[:, 1], ALU.min).then_inc(ba_dve, 1)
            dve.wait_ge(lam_exp, 1)
            link(V_.tensor_tensor(NLAM, LAME[:, 1:2], LAME[:, 0:1], ALU.subtract))
            link(V_.tensor_scalar(NLAM, NLAM, LAM_INIT, None, ALU.subtract))
            dve.wait_ge(ba_act, 1)
            V_.tensor_scalar(beta[:], ba[:, 0], 0.5, 0.5, ALU.mult, ALU.add)
            V_.tensor_scalar(hbeta[:], ba[:, 0], 0.25, 0.25, ALU.mult, ALU.add)
            link(V_.tensor_scalar(ba[:, 3], ba[:, 2], 2.0, None, ALU.add))
            link(V_.reciprocal(ba[:, 4], ba[:, 3]))
            link(V_.tensor_tensor(ba[:, 4], ba[:, 4], ba[:, 2], ALU.mult))
            link(V_.tensor_tensor(ba[:, 5], ba[:, 4], ba[:, 4], ALU.mult))
            link(V_.tensor_scalar(ba[:, 3], ba[:, 5], 1.0 / 17, None, ALU.mult))
            for n in range(15, 1, -2):
                link(V_.scalar_tensor_tensor(out=ba[:, 3], in0=ba[:, 3], scalar=1.0 / n, in1=ba[:, 5],
                                             op0=ALU.add, op1=ALU.mult))
            link(V_.scalar_tensor_tensor(out=ba[:, 3], in0=ba[:, 3], scalar=1.0, in1=ba[:, 4], op0=ALU.add, op1=ALU.mult))
            link(V_.tensor_scalar(ba[:, 1], ba[:, 1], 0.0, None, ALU.max))
            link(V_.scalar_tensor_tensor(out=ba[:, 1], in0=ba[:, 3], scalar=2.0, in1=ba[:, 1], op0=ALU.mult, op1=ALU.add))
            V_.scalar_tensor_tensor(out=gdec[:], in0=ba[:, 1], scalar=-1.0, in1=along(ealog, ST),
                                    op0=ALU.mult, op1=ALU.mult).then_inc(g_ready, 1)

            def conv(t):
                kind, h = TILES[t]
                n = n_conv[t]
                col = PC_CONV + 4 * ({"dq": 0, "dk": 8, "dv": 16}[kind] + h)
                dve.wait_ge(acc_free, t + 1)
                y = conv_y[:, n % 2]
                link(V_.tensor_scalar(y, conv_x[:, n % 2, 0:S], par[:, col:col + 1], None, ALU.mult))
                for j in (1, 2, 3):
                    ins = V_.scalar_tensor_tensor(out=y, in0=conv_x[:, n % 2, j:j + S], scalar=par[:, col + j:col + j + 1],
                                                  in1=y, op0=ALU.mult, op1=ALU.add)
                    if j < 3:
                        link(ins)
                ins.then_inc(cy_ready, 1)

            def finish(t):
                kind, h = TILES[t]
                if t in n_conv:
                    n = n_conv[t]
                    dve.wait_ge(ct_ready, n + 1)
                    if h >= 2:
                        dve.wait_ge(d_mm, d_idx[("dv", h // 2 - 1, 0)] + 1)
                    V_.scalar_tensor_tensor(out=conv_o[:, ("dq", "dk", "dv").index(kind), h % 2],
                                            in0=conv_x[:, n % 2, 3:3 + S], scalar=1.0, in1=conv_y[:, n % 2],
                                            op0=ALU.add, op1=ALU.mult).then_inc(co_ready, 1)
                else:
                    n = n_z[t]
                    dve.wait_ge(zt_ready, n + 1)
                    V_.scalar_tensor_tensor(out=zs[:, n % 2], in0=z_t[:], scalar=1.0, in1=zs[:, n % 2],
                                            op0=ALU.add, op1=ALU.mult).then_inc(z_ready, 1)

            def attn(i):
                kind, h = ATTN[i]
                if kind not in ("cs", "as0", "as1", "ap"):
                    return
                dve.wait_ge(a_mm, i + 1)
                if kind == "cs":
                    link(V_.reduce_max(mxa, two(ps_a).rearrange("p (a b) -> p a b", a=ST), AX_X))
                    V_.tensor_scalar(nba, mxa, -SC_C, None, ALU.mult).then_inc(a_max, 1)
                    dve.wait_ge(a_act, aA[i + 1])
                    link(V_.reciprocal(rca[:, 0:4], sma[:, 0:4]))
                    last = V_.tensor_tensor(p_c[:], p_c[:], along(rca[:, 0:4], MEM), ALU.mult)
                    last.then_inc(a_dve, 1)
                elif kind in ("as0", "as1"):
                    if (kind, h) == ("as0", 0):
                        dve.wait_ge(strip_in, 16)
                        link(V_.tensor_tensor(strip[:, :, P:2 * P], strip[:, :, P:2 * P],
                                              over(cst[:, C_CAUS, :], HA), ALU.add))
                    ps = flat(ps_a[:])
                    near = view(ps, [[512, 3], [1, 2 * P]], 256)
                    V_.tensor_tensor(near, near, over(strip[:, h], 3), ALU.add)
                    link(V_.tensor_tensor(ps[:, 512:512 + P], ps[:, 512:512 + P], strip[:, h, P:2 * P], ALU.add))
                    for q in range(ST):
                        ins = V_.reduce_max(mxa[:, q:q + 1], ps[:, bank_of[q]:bank_of[q] + (q + 1) * P], AX_X)
                    link(ins)
                    V_.tensor_scalar(nba, mxa, -SC_A, None, ALU.mult).then_inc(a_max, 1)
                    if kind == "as1":
                        dve.wait_ge(a_act, aA[i + 1])
                        link(V_.reciprocal(rca, sma))
                        link(V_.tensor_scalar(rca[:, 4:8], rca[:, 4:8], NLAM, None, ALU.mult))
                        for q in range(ST):
                            c = slice(pack_of[q], pack_of[q] + (q + 1) * P)
                            ins = V_.tensor_scalar(p_a[:, 1, c], p_a[:, 1, c], rca[:, 4 + q:5 + q], None, ALU.mult)
                        link(ins)
                        for q in range(ST):
                            c = slice(pack_of[q], pack_of[q] + (q + 1) * P)
                            ins = V_.scalar_tensor_tensor(out=p_a[:, 0, c], in0=p_a[:, 0, c], scalar=rca[:, q:q + 1],
                                                          in1=p_a[:, 1, c], op0=ALU.mult, op1=ALU.add)
                        ins.then_inc(a_dve, 1)
                else:
                    dve.wait_ge(a_act, aA[i + 1])
                    link(V_.tensor_tensor(p_a[:, 1, 0:S], flat(o_a[:]), flat(o_a[:]), ALU.mult))
                    link(V_.reduce_sum(ssa, p_a[:, 1, 0:S].rearrange("p (a b) -> p a b", a=ST), AX_X))
                    link(V_.tensor_scalar(ssa, ssa, 1.0 / P, EPS, ALU.mult, ALU.add))
                    rsqrt(rsa, ssa, tma)
                    V_.tensor_tensor(o_a[:], o_a[:], along(rsa, P), ALU.mult).then_inc(a_dve, 1)

            def scale_by_norm(buf, mul, add, factor):
                link(V_.tensor_tensor(SCR[:], buf[:], buf[:], ALU.mult))
                link(V_.reduce_sum(ssd, SCR[:], AX_X))
                link(V_.tensor_scalar(ssd, ssd, mul, add, ALU.mult, ALU.add))
                rsqrt(rsd, ssd, tmd)
                if factor != 1.0:
                    link(V_.tensor_scalar(rsd, rsd, factor, None, ALU.mult))
                return V_.tensor_tensor(buf[:], buf[:], along(rsd, P), ALU.mult)

            def delta(i):
                kind, p, c = DELTA[i]
                if "D" not in PARTS[kind]:
                    return
                dve.wait_ge(d_mm, i + 1)
                heads = slice(2 * p, 2 * p + 2)
                ps = blocks(two(ps_d))
                if kind == "dq":
                    dve.wait_ge(d_act, dA[i + 1])
                    last = scale_by_norm(Q, 1.0, 4 * EPS, P ** -0.5)
                elif kind == "dk":
                    dve.wait_ge(d_act, dA[i + 1])
                    link(scale_by_norm(K, 1.0, 4 * EPS, 1.0))
                    last = V_.tensor_tensor(KB[:], K[:], along(flat(beta[:, heads]), P), ALU.mult)
                elif kind == "dv":
                    last = V_.tensor_tensor(V[:], ps, along(flat(hbeta[:, heads]), P), ALU.mult)
                elif kind == "dqT":
                    last = V_.tensor_tensor(Q[:], Q[:], along(flat(e_in[:, heads]), P), ALU.mult)
                elif kind == "dL":
                    link(V_.tensor_tensor(LT[:], ps, ET[:], ALU.mult))
                    link(V_.tensor_tensor(SCR[:], LT[:], over(cst[:, C_MASK0, :], 8), ALU.mult))
                    last = V_.tensor_tensor(TT[:], over(ident, 8), SCR[:], ALU.subtract)
                elif kind == "dA":
                    last = V_.tensor_tensor(AT[:], ps, ET[:], ALU.mult)
                elif kind in ("Wb", "Wl"):
                    last = V_.tensor_tensor(TT[:], TT[:], ps, ALU.subtract)
                elif kind == "sa":
                    u_v = U[:].rearrange("p (h c) d -> p h c d", h=2)[:, :, c]
                    last = V_.tensor_tensor(vnew[:], u_v, ps_d[:, 0, 0:256].rearrange("p (h d) -> p h d", h=2),
                                            ALU.subtract)
                elif kind == "sb":
                    for hh in range(2):
                        kv = ps_d[:, 1, hh * P:(hh + 1) * P]
                        if c == 0:
                            last = V_.tensor_copy(state[:, hh], kv)
                        else:
                            last = V_.scalar_tensor_tensor(out=state[:, hh], in0=state[:, hh],
                                                           scalar=e_all[:, 2 * p + hh, c:c + 1], in1=kv,
                                                           op0=ALU.mult, op1=ALU.add)
                    if c == ST - 1:
                        link(last)
                        dve.wait_ge(d_act, dA[i + 1])
                        last = scale_by_norm(O, 1.0 / P, EPS, 1.0)
                elif kind == "dO":
                    dve.wait_ge(z_ready, 2 * (p + 1))
                    last = V_.scalar_tensor_tensor(out=flat(ET[:]), in0=two(ps_d), scalar=GDN, in1=flat(zs[:]),
                                                   op0=ALU.mult, op1=ALU.mult)
                last.then_inc(d_dve, 1)

            for main, ev, fi, sa, sd in SLOTS:
                if ev is not None:
                    split_hi(ev + SPL)
                    if ev in n_conv:
                        conv(ev)
                if fi is not None:
                    finish(fi)
                if sa is not None:
                    attn(sa)
                if sd is not None:
                    delta(sd)

            def y_hi_tiles(b):
                dve.wait_ge(y_in[b], 16)
                if b == 2:
                    dve.wait_ge(tile_used, tiles_of(KT))
                for kk in range(KT):
                    V_.tensor_copy(y_hi[:, b % 2, kk], y_raw[:, kk]).then_inc(yh_ready, 1)

            def rms_rows(i, col, g_row):
                v, r, tm = sml[:, col + i:col + i + 1], sml[:, 112:113], sml[:, 113:114]
                link(V_.tensor_scalar(v, v, 1.0 / D, EPS, ALU.mult, ALU.add))
                rsqrt(r, v, tm)
                link(V_.scalar_tensor_tensor(out=tok[:], in0=two(side[i % 2]), scalar=r, in1=g_row,
                                             op0=ALU.mult, op1=ALU.mult))

            for r, (tile, t0, k) in enumerate(LATE):
                if r in Y_AT:
                    y_hi_tiles(Y_AT[r])
                for j in range(k):
                    split_hi(t0 + j + SPL)
                bank = acc[:, r % 2]
                if r < N_BR:
                    b, m = r // KT, r % KT
                    dve.wait_ge(tile_used, tiles_of(r + 1))
                    dve.wait_ge(gin[r % 3], 16 * (r // 3 + 1))
                    if b == 0:
                        V_.tensor_tensor(mix_acc[:, m], bank, g_in[:, r % 3], ALU.mult).then_inc(gated, 1)
                    else:
                        V_.tensor_tensor(g_tmp[:], bank, g_in[:, r % 3], ALU.mult).then_inc(gated, 1)
                        dve.wait_ge(gated, r + 1)
                        ins = V_.tensor_tensor(mix_acc[:, m], mix_acc[:, m], g_tmp[:], ALU.add)
                        link(ins)
                        if b == 2:
                            V_.tensor_copy(mx_hi[:, m], mix_acc[:, m]).then_inc(mxh_ready, 1)
                elif r == N_BR + KT - 1:
                    dve.wait_ge(in_post, 16)
                    dve.wait_ge(in_x2, 16)
                    for i in range(ST):
                        dve.wait_ge(ss1, i + 1)
                        if i:
                            dve.wait_ge(n2l, i)
                        rms_rows(i, 96, post[:, 0])
                        V_.tensor_tensor(h1[:, i], h1[:, i], tok[:], ALU.add).then_inc(t1d, 1)
                        dve.wait_ge(ss2, i + 1)
                        v, rr, tm = sml[:, 100 + i:101 + i], sml[:, 112:113], sml[:, 113:114]
                        link(V_.tensor_scalar(v, v, 1.0 / D, EPS, ALU.mult, ALU.add))
                        rsqrt(rr, v, tm)
                        V_.tensor_scalar(rows[:], h1[:, i], rr, None, ALU.mult).then_inc(n2n, 1)
                        dve.wait_ge(tr2, i + 1)
                        link(V_.tensor_tensor(blocks(tok[:]), blocks(two(side[i % 2])),
                                              along(par[:, PC_FF:PC_FF + KT], P), ALU.mult))
                        V_.tensor_copy(n2_hi[:, :, i * P:(i + 1) * P], blocks(tok[:])).then_inc(n2h, 1)
                elif tile[0] == "f1":
                    f = tile[1]
                    dve.wait_ge(tile_used, tiles_of(r + 1))
                    if f >= 2:
                        dve.wait_ge(sq_ok, f - 1)
                    V_.tensor_scalar(relu[:, f % 2], bank, 0.0, None, ALU.max).then_inc(relu_ok, 1)
                    dve.wait_ge(sq_ok, f + 1)
                    V_.tensor_copy(h_hi[:, f % 16], sq[:, f % 2]).then_inc(hh_ok, 1)
                elif tile[0] == "f2":
                    dve.wait_ge(tile_used, tiles_of(r + 1))
                    m = tile[1] % KT
                    if r < L_F2[0] + KT:
                        V_.tensor_copy(f_T[:, m], bank).then_inc(f_ev, 1)
                    else:
                        V_.tensor_tensor(f_T[:, m], f_T[:, m], bank, ALU.add).then_inc(f_ev, 1)
            for i in range(ST):
                dve.wait_ge(ss3, i + 1)
                rms_rows(i, 104, post[:, 1])
                V_.tensor_tensor(h1[:, i], h1[:, i], tok[:], ALU.add).then_inc(fin, 1)
                dve.wait_ge(fin, i + 1)

        @block.tensor
        def _(pe):
            mm = nc.tensor.matmul

            pe.wait_ge(in_cst, 16)
            for j in range(N_SU):
                bank = side[(j // 3) % 2][:, j % 3]
                if j >= 6:
                    pe.wait_ge(su_full, j - 5)
                if j < 4:
                    pe.wait_ge(su_norm, MT)
                    for u in range(2):
                        for i in range(MT):
                            last = nc.tensor.transpose(bank[:, u * MEM + i * P:u * MEM + (i + 1) * P],
                                                       m_tok[:, i, (2 * j + u) * P:(2 * j + u + 1) * P], ident)
                else:
                    pe.wait_ge(su_norm, MT + ST)
                    for i in range(ST):
                        last = nc.tensor.transpose(bank[:, i * P:(i + 1) * P],
                                                   x_tok[:, i, (j - 4) * P:(j - 3) * P], ident)
                last.then_inc(su_tr, 1)
            pe.wait_ge(in_oh, 16)
            pe.wait_ge(in_relb, 16)
            pe.wait_ge(su_full, N_SU)
            pe.wait_ge(su_hi, N_SU)
            mm(ps_a[0:HA, 0, 0:SPAN], relb_sb, onehot_sb, start=True, stop=True).then_inc(f_mm, 1)
            pe.wait_ge(ba_split, 1)
            pe.wait_ge(su_lo, N_SU)
            for c in range(ST):
                dst = ps_d[:, 0, c * 2 * HB:(c + 1) * 2 * HB]
                for k in range(KT):
                    hi, lo = n_hi[:, k, c * P:(c + 1) * P], n_lo[:, k, c * P:(c + 1) * P]
                    mm(dst, hi, wb_hi[:, k], start=k == 0, stop=False)
                    mm(dst, hi, wb_lo[:, k], start=False, stop=False)
                    last = mm(dst, lo, wb_hi[:, k], start=False, stop=k == KT - 1)
            last.then_inc(ba_mm, 1)

            def weight_tile(bank, t, ks, hi_of, lo_of, start, stop, k_wait=None):
                for k in ks:
                    if k_wait is not None:
                        k_wait(k)
                    wh, wl = w_hi[:, t % SPL, k], w_lo[:, t % SPL, k]
                    mm(bank, wh, hi_of(k), start=start and k == 0, stop=False)
                    mm(bank, wh, lo_of(k), start=False, stop=False)
                    last = mm(bank, wl, hi_of(k), start=False, stop=stop and k == KT - 1)
                return last

            def main_half(t, half):
                kind = TILES[t][0]
                if half == 0:
                    pe.wait_ge(lo_ready, t + 1)
                    if t >= 2:
                        pe.wait_ge(acc_free, t - 1)
                ks = range(half * KT // 2, (half + 1) * KT // 2)
                if kind in ("mk", "mv"):
                    last = weight_tile(acc[:, t % 2, 0:MEM], t, ks, lambda k: m_hi[:, k], lambda k: m_lo[:, k], True, True)
                else:
                    last = weight_tile(acc[:, t % 2], t, ks, lambda k: n_hi[:, k], lambda k: n_lo[:, k], True, True)
                if half == 1:
                    last.then_inc(tile_used, 1)

            def attn(i):
                kind, h = ATTN[i]
                if i:
                    pe.wait_ge(a_act, aA[i])
                    if aD[i]:
                        pe.wait_ge(a_dve, aD[i])
                if kind == "mv":
                    if h == 0:
                        pe.wait_ge(acc_free, TILES.index(("mv", KT - 1)) + 1)
                    for j in range(4):
                        for mt in range(MT):
                            last = nc.tensor.transpose(ps_a[:, mt, j * P:(j + 1) * P],
                                                       mv_T[:, 4 * h + j, mt * P:(mt + 1) * P], ident)
                elif kind == "cs":
                    pe.wait_ge(acc_free, TILES.index(("cq", 2 * h + 1)) + 1)
                    for s in range(ST):
                        for dt in range(2):
                            last = mm(ps_a[:, s // 2, (s % 2) * MEM:(s % 2 + 1) * MEM],
                                      cq_T[:, h % 2, dt, s * P:(s + 1) * P], mk_T[:, 2 * h + dt],
                                      start=dt == 0, stop=dt == 1)
                elif kind == "ct":
                    for mt in range(MT):
                        for s in range(ST):
                            last = nc.tensor.transpose(ps_a[:, mt, s * P:(s + 1) * P],
                                                       p_c[:, s, mt * P:(mt + 1) * P], ident)
                elif kind == "cv":
                    for dt in range(2):
                        for mt in range(MT):
                            last = mm(ps_a[:, dt], mv_tok[:, mt, (2 * h + dt) * P:(2 * h + dt + 1) * P], pT_c[:, mt],
                                      start=mt == 0, stop=mt == MT - 1)
                elif kind == "av":
                    pe.wait_ge(acc_free, TILES.index(("av", h)) + 1)
                    for s in range(ST):
                        last = nc.tensor.transpose(ps_a[:, 0, s * P:(s + 1) * P], qkv_T[:, h % 2, 2, s * P:(s + 1) * P], ident)
                elif kind in ("as0", "as1"):
                    rows_m = slice(DA * int(kind[2]), DA * int(kind[2]) + DA)
                    ps = flat(ps_a[:])
                    for q in range(ST - 1, -1, -1):
                        last = mm(ps[:, bank_of[q]:bank_of[q] + (q + 1) * P], qkv_T[rows_m, h % 2, 0, q * P:(q + 1) * P],
                                  qkv_T[rows_m, h % 2, 1, 0:(q + 1) * P], start=True, stop=True)
                elif kind == "at":
                    ps = flat(ps_a[:])
                    for kt in range(ST):
                        for q in range(kt, ST):
                            last = nc.tensor.transpose(ps[:, t_bank(kt, q):t_bank(kt, q) + P],
                                                       p_a[:, 0, pack_of[q] + kt * P:pack_of[q] + (kt + 1) * P], ident)
                elif kind == "ap":
                    for q in range(ST):
                        for kt in range(q + 1):
                            last = mm(ps_a[:, 0, q * P:(q + 1) * P], wT[:, t_pack(kt, q):t_pack(kt, q) + P],
                                      v_tok[:, kt * P:(kt + 1) * P], start=kt == 0, stop=kt == q)
                elif kind == "ay":
                    for q in range(ST):
                        last = nc.tensor.transpose(ps_a[:, 0, q * P:(q + 1) * P], o_a[:, q], ident)
                last.then_inc(a_mm, 1)

            def delta(i):
                kind, p, c = DELTA[i]
                if i:
                    pe.wait_ge(d_act, dA[i])
                    pe.wait_ge(d_dve, dD[i])
                    if dP[i]:
                        pe.wait_ge(d_pool, dP[i])
                dst = [ps_d[:, m // 4, (m % 4) * P:(m % 4 + 1) * P] for m in range(8)]
                if kind in ("dq", "dk", "dv"):
                    pe.wait_ge(co_ready, 6 * (p + 1))
                    if i == 0:
                        pe.wait_ge(g_exp, 1)
                    for m in range(8):
                        last = nc.tensor.transpose(dst[m], conv_o[:, ("dq", "dk", "dv").index(kind), m // 4,
                                                                  (m % 4) * P:(m % 4 + 1) * P], ident)
                elif kind in ("dqT", "dqd", "dkT", "dkb", "T1", "Tc", "dO"):
                    src = {"dqT": Q, "dqd": Q, "dkT": K, "dkb": KB, "T1": TT, "Tc": TT, "dO": O}[kind]
                    for m in range(8):
                        last = nc.tensor.transpose(dst[m], src[:, m], ident)
                elif kind == "dE":
                    for m in range(8):
                        last = mm(dst[m], SCR[:, m], cst[:, C_UPTO, :], start=True, stop=True)
                elif kind in ("dL", "dA", "Za", "Wb", "Wl", "dU", "dW"):
                    a, b = {"dL": (KTT, KBT), "dA": (KTT, QT), "Za": (XT, TN), "Wb": (Z, TT), "Wl": (Z, TT),
                            "dU": (TT, V), "dW": (KB, TT)}[kind]
                    for m in range(8):
                        last = mm(dst[m], a[:, m], b[:, m], start=True, stop=True)
                elif kind == "sa":
                    for hh in range(2):
                        last = mm(ps_d[:, 0, hh * P:(hh + 1) * P], WT[:, 4 * hh + c], state[:, hh], start=True, stop=True)
                elif kind == "sb":
                    for hh in range(2):
                        vn = vnew[:, hh] if c else U[:, 4 * hh]
                        o_ps = ps_d[:, 0, hh * P:(hh + 1) * P]
                        if c:
                            mm(o_ps, QDT[:, 4 * hh + c], state[:, hh], start=True, stop=False)
                        mm(o_ps, AT[:, 4 * hh + c], vn, start=c == 0, stop=True)
                    for hh in range(2):
                        vn = vnew[:, hh] if c else U[:, 4 * hh]
                        last = mm(ps_d[:, 1, hh * P:(hh + 1) * P], K[:, 4 * hh + c], vn, start=True, stop=True)
                last.then_inc(d_mm, 1)

            for n, (main, ev, fi, sa, sd) in enumerate(SLOTS):
                if n == G_SLOT:
                    pe.wait_ge(g_ready, 1)
                    pe.wait_ge(ones_set, 1)
                    for m, w in enumerate((cst[:, C_UPTO, :], cst[:, C_AFTER, :], ones[:])):
                        last = mm(ps_d[:, 0, m * 32:(m + 1) * 32], w, flat(gdec[:]), start=True, stop=True)
                    last.then_inc(g_mm, 1)
                if main is not None:
                    main_half(*main)
                if sa is not None:
                    attn(sa)
                if sd is not None:
                    delta(sd)

            for r, (tile, t0, k) in enumerate(LATE):
                bank = acc[:, r % 2]
                k_wait = None
                if r < 2:
                    pe.wait_ge(acc_free, N_MIX - 1 + r)
                elif r - 2 < N_BR:
                    pe.wait_ge(gated, r - 1)
                elif r - 2 < N_BR + KT:
                    pe.wait_ge(o_ev, r - 1 - N_BR)
                elif LATE[r - 2][0][0] == "f1":
                    pe.wait_ge(relu_ok, LATE[r - 2][0][1] + 1)
                else:
                    pe.wait_ge(f_ev, r - 1 - L_F2[0] if r - 2 < L_F1[1] else r - 1 - L_F2[1] + KT)
                if tile[0] == "br":
                    b = r // KT
                    hi_of, lo_of = (lambda k, b=b: y_hi[:, b % 2, k]), (lambda k, b=b: y_lo[:, b % 2, k])
                    if r % KT == 0:
                        k_wait = lambda k, b=b: pe.wait_ge(yl_ready, KT * b + k + 1)
                elif tile[0] == "out":
                    hi_of, lo_of = (lambda k: mx_hi[:, k]), (lambda k: mx_lo[:, k])
                    if r == N_BR:
                        k_wait = lambda k: pe.wait_ge(mxl_ready, k + 1)
                elif tile[0] == "f1":
                    hi_of, lo_of = (lambda k: n2_hi[:, k]), (lambda k: n2_lo[:, k])
                    if tile[1] == 0:
                        pe.wait_ge(n2l, ST)
                for j in range(k):
                    t = t0 + j
                    pe.wait_ge(lo_ready, t + 1)
                    if tile[0] == "f2":
                        g = TILES[t][1] // KT
                        o = (g % 2) * KT
                        hi_of, lo_of = (lambda k, o=o: h_hi[:, o + k]), (lambda k, o=o: h_lo[:, o + k])
                        if r in L_F2:
                            k_wait = lambda k, g=g: pe.wait_ge(hl_ok, g * KT + k + 1)
                    last = weight_tile(bank, t, range(KT), hi_of, lo_of, j == 0, j == k - 1, k_wait)
                    if j < k - 1:
                        last.then_inc(tile_used, 1)
                last.then_inc(tile_used, 1)
                if r == N_BR + KT - 1:
                    pe.wait_ge(o_ev, KT)
                    for i in range(ST):
                        if i >= 2:
                            pe.wait_ge(n2h, i - 1)
                        for m in range(KT):
                            last = nc.tensor.transpose(side[i % 2][:, m // 4, (m % 4) * P:(m % 4 + 1) * P],
                                                       f_T[:, m, i * P:(i + 1) * P], ident)
                        last.then_inc(tr1, 1)
                        pe.wait_ge(n2n, i + 1)
                        for m in range(KT):
                            last = nc.tensor.transpose(side[i % 2][:, m // 4, (m % 4) * P:(m % 4 + 1) * P],
                                                       rows[:, m * P:(m + 1) * P], ident)
                        last.then_inc(tr2, 1)
            pe.wait_ge(f_ev, 2 * KT)
            for i in range(ST):
                if i >= 2:
                    pe.wait_ge(fin, i - 1)
                for m in range(KT):
                    last = nc.tensor.transpose(side[i % 2][:, m // 4, (m % 4) * P:(m % 4 + 1) * P],
                                               f_T[:, m, i * P:(i + 1) * P], ident)
                last.then_inc(tr3, 1)


def _consts():
    i = np.arange(P)
    c = np.zeros((P, NCONST, P), np.float32)
    c[:, C_ID] = np.eye(P)
    c[:, C_UPTO] = i[:, None] <= i[None, :]
    c[:, C_AFTER] = i[:, None] > i[None, :]
    for n in range(NM):
        b = 2 ** n
        c[:, C_MASK0 + n] = ((i[None, :] // (2 * b) == i[:, None] // (2 * b)) & (i[None, :] // b % 2 == 1)
                             & (i[:, None] // b % 2 == 0))
    c[:, C_CAUS] = np.where(i[None, :] > i[:, None], NEG, 0.0)
    return c


def _onehot():
    dist = np.maximum(2 * P - 1 - np.arange(SPAN), 0)
    nf = np.maximum(dist, 1).astype(np.float32)
    large = MAX_EXACT + (np.log(nf / np.float32(MAX_EXACT)) / np.float32(math.log(MAX_DIST / MAX_EXACT))
                         * np.float32(BUCKETS - MAX_EXACT)).astype(np.int32)
    bucket = np.where(dist < MAX_EXACT, dist, np.minimum(large, BUCKETS - 1))
    o = np.zeros((BUCKETS, SPAN), np.float32)
    o[bucket, np.arange(SPAN)] = 1.0
    o[BUCKETS - 1] -= 1.0
    return o


def kernel(**inputs):
    import concourse.bacc as bacc
    from concourse.bass_utils import run_bass_kernel_spmd

    a = {k: np.asarray(v) for k, v in inputs.items()}
    w_in, w_kv, w_br = a["w_in"][0], a["w_mem_kv"][0], a["w_branch"][0]
    w_out, w1, w2 = a["w_out"][0], a["w_ff1"][0], a["w_ff2"][0]

    def block_of(kind, j):
        c = slice(j * P, (j + 1) * P)
        if kind == "mk":
            return w_kv[:, c]
        if kind == "mv":
            return w_kv[:, D + j * P:D + (j + 1) * P]
        if kind == "br":
            return w_br[j // KT][:, j % KT * P:(j % KT + 1) * P]
        if kind == "out":
            return w_out[:, c]
        if kind == "f1":
            return w1[:, c]
        if kind == "f2":
            return w2[j // KT * D:(j // KT + 1) * D, j % KT * P:(j % KT + 1) * P]
        return w_in[:, COL[kind] + j * P:COL[kind] + (j + 1) * P]

    tiles = plan_tiles()[0]
    weights = np.empty((len(tiles), P, KT, P), np.float32)
    for n, (kind, j) in enumerate(tiles):
        weights[n] = block_of(kind, j).reshape(KT, P, P).transpose(1, 0, 2)

    params = np.empty((P, NPAR), np.float32)
    for c, name in ((PC_PRE, "ln_mix_pre"), (PC_MEM, "mem_norm_g"), (PC_FF, "ln_ff_pre")):
        params[:, c:c + KT] = a[name][0].reshape(KT, P).T
    params[:, PC_SUB] = a["da_subln_g"][0]
    params[:, PC_DNG] = a["dn_norm_g"][0]
    params[:, PC_CONV:PC_ALOG] = a["conv_w"][0].reshape(4, 24, P).transpose(2, 1, 0).reshape(P, 96)
    params[:, PC_ALOG:PC_ALOG + HB] = a["dn_a_log"][0][None]
    params[:, PC_DTB:PC_DTB + HB] = a["dn_dt_bias"][0][None]
    params[:, PC_LAM:] = a["da_lambda"][0].reshape(1, 4 * DA)
    post_g = np.empty((P, 2, D), np.float32)
    post_g[:, 0] = a["ln_mix_post"][0][None]
    post_g[:, 1] = a["ln_ff_post"][0][None]
    w_ba = w_in[:, COL["ba"]:COL["ba"] + 2 * HB].reshape(KT, P, 2 * HB).transpose(1, 0, 2)
    arrays = {
        "weights": weights, "x": a["x"][0], "mem": a["mem"][0], "w_ba": w_ba, "params": params,
        "consts": _consts(), "onehot": _onehot(), "relb": a["rel_bias"], "post_g": post_g,
    }
    arrays = {k: np.ascontiguousarray(v) for k, v in arrays.items()}
    nc = bacc.Bacc("TRN2", target_bir_lowering=False, num_devices=1)
    ins = [nc.dram_tensor(k, v.shape, F32, kind="ExternalInput").ap() for k, v in arrays.items()]
    y_dram = nc.dram_tensor("y_scratch", (3, P, KT, S), F32, kind="Internal").ap()
    gate_dram = nc.dram_tensor("gate_scratch", (3 * KT, P, S), F32, kind="Internal").ap()
    f_dram = nc.dram_tensor("bias_scratch", (HA, SPAN), F32, kind="Internal").ap()
    frep_dram = nc.dram_tensor("bias_rows", (HA, P, SPAN), F32, kind="Internal").ap()
    out = nc.dram_tensor("out", (S, D), F32, kind="ExternalOutput").ap()
    build(nc, *ins, y_dram, gate_dram, f_dram, frep_dram, out)
    r = run_bass_kernel_spmd(nc, [arrays], core_ids=[0])
    return r.results[0]["out"].reshape(1, S, D)
```

```python
import math
from contextlib import ExitStack

import numpy as np

import concourse.bass as bass
from concourse import mybir

F32 = mybir.dt.float32
F32R = mybir.dt.float32r
I32 = mybir.dt.int32
ALU = mybir.AluOpType
ACT = mybir.ActivationFunctionType
AX_X = mybir.AxisListType.X

P = 128
D = 1024
S = 512
KT = D // P
ST = S // P
MEM = 256
MT = MEM // P
DFF = 4 * D
HA, DA = 8, 64
HB = 8
HC = 4
EPS = 1e-6
LAM_INIT = 0.8 - 0.6 * math.exp(-0.3 * 0)
BUCKETS, MAX_EXACT, MAX_DIST = 32, 16, 128
SPAN = 3 * P
NEG = -1e30
NM = 7

COL = {"aq": 0, "ak": D, "av": 2 * D, "dq": 3 * D, "dk": 4 * D, "dv": 5 * D, "dz": 6 * D,
       "ba": 7 * D, "cq": 7 * D + 2 * HB, "gate": 8 * D + 2 * HB}

RAW, SPL = 3, 3

C_ID, C_UPTO, C_AFTER, C_MASK0, C_CAUS = 0, 1, 2, 3, 3 + NM
NCONST = 4 + NM
PC_PRE, PC_MEM, PC_FF = 0, 8, 16
PC_SUB, PC_DNG = 24, 25
PC_CONV = 26
PC_ALOG = PC_CONV + 96
PC_DTB = PC_ALOG + HB
PC_LAM = PC_DTB + HB
NPAR = PC_LAM + 4 * DA

PARTS = {"mv": "A", "cs": "AD", "ct": "A", "cv": "A", "av": "A", "as0": "A", "as1": "AD", "at": "A",
         "ap": "AD", "ay": "A",
         "dq": "AD", "dk": "AD", "dv": "DP", "dE": "A", "dqT": "AD", "dqd": "A", "dkT": "AP",
         "dkb": "AP", "dL": "DP", "dA": "DP", "T1": "A", "Za": "A", "Wb": "DP", "Wl": "D", "Tc": "A",
         "dU": "A", "dW": "A", "sa": "D", "sb": "AD", "dO": "D"}
COVER = {"cs": 3, "cv": 2, "as0": 3, "as1": 4, "at": 2, "ap": 2, "dq": 2, "dk": 3, "dO": 2, "sb_last": 2}
EXP_LAG, SCALE_LAG, NORM_LAG = 1, 2, 1

ORDER = [("conv", 0), ("mem", 0), ("cq", 0), ("z", 0), ("conv", 1), ("cq", 1), ("cq", 2), ("cq", 3), ("z", 1),
         ("head", 0), ("head", 1), ("conv", 2), ("head", 2), ("z", 2), ("head", 3), ("head", 4), ("conv", 3),
         ("head", 5), ("head", 6), ("z", 3), ("head", 7)]


def cover(step):
    last_state = step[0] == "sb" and step[2] == ST - 1
    return COVER.get("sb_last" if last_state else step[0], 1)


def attn_steps():
    out = [("mv", 0), ("mv", 1)]
    for h in range(HC):
        out += [("cs", h), ("ct", h), ("cv", h)]
    for h in range(HA):
        out += [("av", h), ("as0", h), ("as1", h), ("at", h), ("ap", h), ("ay", h)]
    return out


def delta_steps():
    out = []
    for p in range(HB // 2):
        out += [(k, p, 0) for k in ("dq", "dk", "dv", "dE", "dqT", "dqd", "dkT", "dkb", "dL", "dA", "T1")]
        for lv in range(1, NM):
            out += [("Za", p, lv), ("Wb" if lv < NM - 1 else "Wl", p, lv)]
            if lv < NM - 1:
                out.append(("Tc", p, lv))
        out += [("dU", p, 0), ("dW", p, 0)]
        for c in range(ST):
            if c:
                out.append(("sa", p, c))
            out.append(("sb", p, c))
        out.append(("dO", p, 0))
    return out


def plan_mixing():
    attn, delta = attn_steps(), delta_steps()
    def group(kind, n):
        return {"mem": [("mk", j) for j in range(KT)] + [("mv", j) for j in range(KT)],
                "conv": [(k, 2 * n + i) for k in ("dq", "dk", "dv") for i in range(2)],
                "z": [("dz", 2 * n + i) for i in range(2)],
                "cq": [("cq", 2 * n + i) for i in range(2)],
                "head": [(k, n) for k in ("aq", "ak", "av")]}[kind]

    groups = [group(*g) for g in ORDER]
    gates = [("gate", i * KT + m) for i in (2, 0, 1) for m in range(KT)]
    tiles, slots = [], []
    done = {}
    evac = {}
    need_free = {}
    for p in range(1, HB // 2):
        for k in ("dq", "dk", "dv"):
            for i in range(2):
                need_free[(k, 2 * p + i)] = ("dv", p - 1, 0)
        for i in range(2):
            need_free[("dz", 2 * p + i)] = ("dO", p - 1, 0)
    for j in range(2 * HC):
        need_free[("cq", j)] = ("mv", 1) if j < 4 else ("cs", j // 2 - 2)
    for h in range(HA):
        for k in ("aq", "ak", "av"):
            need_free[(k, h)] = ("cv", HC - 1) if h < 2 else ("as1", h - 2)
    need_tile = {}
    need_tile[("mv", 0)] = need_tile[("mv", 1)] = ("mv", KT - 1)
    for h in range(HC):
        need_tile[("cs", h)] = ("cq", 2 * h + 1)
    for h in range(HA):
        need_tile[("av", h)] = ("av", h)
    for p in range(HB // 2):
        need_tile[("dq", p, 0)] = ("dv", 2 * p + 1)
        need_tile[("dO", p, 0)] = ("dz", 2 * p + 1)
    ai = di = 0
    a_next = d_next = 0
    finish = {}
    todo = list(groups)
    now = []
    half = 0
    slot = 0
    while todo or gates or now or ai < len(attn) or di < len(delta) or finish.get(slot):
        if not now:
            if todo and all(need_free.get(t) is None or need_free[t] in done for t in todo[0][:1]):
                now = list(todo.pop(0))
            elif gates:
                now = [gates.pop(0)]
        main = ev = None
        if now:
            short = now[0][0] in ("mk", "mv")
            main = (len(tiles), None if short else half)
            if half == 1 or short:
                t = now.pop(0)
                tiles.append(t)
                ev = len(tiles) - 1
                evac[t] = slot
                if t[0] in ("dq", "dk", "dv", "dz"):
                    finish[slot + 1] = ev
                    evac[t] = slot + 1
            half = 0 if short else half ^ 1
        sa = sd = None
        if ai < len(attn) and slot >= a_next:
            t = need_tile.get(attn[ai])
            if t is None or evac.get(t, slot + 9) < slot:
                sa = ai
                done[attn[ai]] = slot
                a_next = slot + cover(attn[ai])
                ai += 1
        if di < len(delta) and slot >= d_next:
            t = need_tile.get(delta[di])
            if t is None or evac.get(t, slot + 9) < slot:
                sd = di
                done[delta[di]] = slot
                d_next = slot + cover(delta[di])
                di += 1
        slots.append((main, ev, finish.get(slot), sa, sd))
        slot += 1
    return tiles, slots, need_free


def plan_tiles():
    tiles, slots, need_free = plan_mixing()
    n_mix = len(tiles)
    tiles = list(tiles)
    for i in (2, 0, 1):
        tiles += [("br", i * KT + m) for m in range(KT)]
    tiles += [("out", m) for m in range(KT)]
    for half in range(2):
        tiles += [("f1", half * 16 + f) for f in range(16)]
        tiles += [("f2", (2 * half + g) * KT + m) for m in range(KT) for g in range(2)]
    return tiles, n_mix, slots, need_free


def counts(steps, part):
    out = [0]
    for s in steps:
        out.append(out[-1] + (part in PARTS[s[0]]))
    return out


def kinds_before(steps, names):
    out = [0]
    for s in steps:
        out.append(out[-1] + (s[0] in names))
    return out


def view(ap, dims, offset=0):
    return bass.AP(tensor=ap.tensor, offset=ap.offset + offset, ap=[list(ap.ap[0])] + [list(d) for d in dims])


def along(ap, n):
    return view(ap, [list(ap.ap[1]), [0, n]])


def over(ap, m):
    return view(ap, [[0, m], list(ap.ap[1])])


def flat(ap3):
    return ap3.rearrange("p a b -> p (a b)")


def build(nc, weights, x, mem, w_ba, params, consts, onehot, relb, post_g, y_dram, gate_dram, f_dram, frep_dram, out):
    TILES, N_MIX, SLOTS, NEED_FREE = plan_tiles()
    NT = len(TILES)
    ATTN, DELTA = attn_steps(), delta_steps()
    a_idx = {s: i for i, s in enumerate(ATTN)}
    d_idx = {s: i for i, s in enumerate(DELTA)}
    aA, aD = counts(ATTN, "A"), counts(ATTN, "D")
    dA, dD, dP = counts(DELTA, "A"), counts(DELTA, "D"), counts(DELTA, "P")
    n_max = kinds_before(ATTN, ("cs", "as0", "as1"))
    n_spill = kinds_before(ATTN, ("cv", "ay"))
    conv_tiles = [t for t in range(N_MIX) if TILES[t][0] in ("dq", "dk", "dv")]
    z_tiles = [t for t in range(N_MIX) if TILES[t][0] == "dz"]
    gate_tiles = [t for t in range(N_MIX) if TILES[t][0] == "gate"]
    n_conv = {t: i for i, t in enumerate(conv_tiles)}
    n_z = {t: i for i, t in enumerate(z_tiles)}
    n_gate = {t: i for i, t in enumerate(gate_tiles)}
    SC_A = DA ** -0.5
    SC_C = (D // HC) ** -0.5

    with ExitStack() as ctx:
        def sem(name):
            return ctx.enter_context(nc.semaphore(name))

        def sb_in(c):
            return lambda name, shape, dt=F32: c.enter_context(nc.sbuf_tensor(name, shape, dt))

        sb = sb_in(ctx)
        acc = ctx.enter_context(nc.psum_tensor("acc", [P, 2, 512], F32))
        ps_a = ctx.enter_context(nc.psum_tensor("ps_a", [P, 3, 512], F32))
        ps_d = ctx.enter_context(nc.psum_tensor("ps_d", [P, 3, 512], F32))
        side = [ps_a, ps_d]

        w_raw = sb("w_raw", [P, RAW, KT, P])
        w_hi = sb("w_hi", [P, SPL, KT, P], F32R)
        w_lo = sb("w_lo", [P, SPL, KT, P], F32R)
        cst = sb("cst", [P, NCONST, P])
        par = sb("par", [P, NPAR])
        ones = sb("ones", [P, P])
        sml = sb("sml", [P, 160])
        smd = sb("smd", [P, 96])
        ident = cst[:, C_ID, :]

        mix = ExitStack()
        sm = sb_in(mix)
        n_hi = sm("n_hi", [P, KT, S], F32R)
        n_lo = sm("n_lo", [P, KT, S], F32R)
        strip = sm("strip", [P, HA, 2 * P])
        beta = sm("beta", [P, HB, ST])
        hbeta = sm("hbeta", [P, HB, ST])
        gdec = sm("gdec", [P, HB, ST])
        e_in = sm("e_in", [P, HB, ST])
        e_tail = sm("e_tail", [P, HB, ST])
        e_all = sm("e_all", [P, HB, ST])
        conv_x = sm("conv_x", [P, 2, S + 4])
        conv_y = sm("conv_y", [P, 2, S])
        conv_o = sm("conv_o", [P, 3, 2, S])
        zs = sm("zs", [P, 2, S])
        z_t = sm("z_t", [P, S])
        y_st = sm("y_st", [P, 2, S])
        gate_st = sm("gate_st", [P, S])
        state = sm("state", [P, 2, P])
        vnew = sm("vnew", [P, 2, P])

        first = ExitStack()
        sf = sb_in(first)
        x_tok = sf("x_tok", [P, ST, D])
        m_tok = sf("m_tok", [P, MT, D])
        full = sf("full", [P, 2, KT, P])
        ba = sf("ba", [P, 6, HB, ST])
        first.close()
        dl = ExitStack()
        sd_ = sb_in(dl)
        names = ["Q", "SCR", "K", "KB", "V", "QT", "QDT", "KTT", "KBT", "ET", "LT", "AT", "TT"]
        B = {n: sd_("d_" + n, [P, 8, P]) for n in names}
        Q, SCR, K, KB, V, QT, QDT, KTT, KBT, ET, LT, AT, TT = (B[n] for n in names)
        XT, TN, Z, U, WT, O = KBT, QT, KTT, Q, SCR, LT

        c1 = ExitStack()
        sc_ = sb_in(c1)
        mk_T = sc_("mk_T", [P, KT, MEM])
        mv_tok = sc_("mv_tok", [P, MT, D])
        p_c = sc_("p_c", [P, ST, MEM])
        pT_c = sc_("pT_c", [P, MT, S])
        c1.close()
        c1 = ExitStack()
        sc_ = sb_in(c1)
        sc_("mk_T_place", [P, KT, MEM])
        m_hi = sc_("m_hi", [P, KT, MEM], F32R)
        m_lo = sc_("m_lo", [P, KT, MEM], F32R)
        c1.close()
        c2 = ExitStack()
        sa_ = sb_in(c2)
        p_a = sa_("p_a", [P, 2, 10 * P])
        wT = sa_("wT", [P, 10 * P])
        v_tok = sa_("v_tok", [P, S])
        o_a = sa_("o_a", [P, ST, P])
        hold = sa_("hold", [P, 1280])
        c3 = ExitStack()
        s3 = sb_in(c3)
        mv_T = s3("mv_T", [P, KT, MEM])
        w_ba_sb = s3("w_ba_sb", [P, KT, 2 * HB])
        wb_hi = s3("wb_hi", [P, KT, 2 * HB], F32R)
        wb_lo = s3("wb_lo", [P, KT, 2 * HB], F32R)
        c3.close()
        c3 = ExitStack()
        s3 = sb_in(c3)
        cq_T = s3("cq_T", [P, 2, 2, S])
        c3.close()
        c3 = ExitStack()
        s3 = sb_in(c3)
        qkv_T = s3("qkv_T", [P, 2, 3, S])
        onehot_sb = strip[0:BUCKETS, 0:2, :].rearrange("p a b -> p (a b)")[:, 0:SPAN]
        c3.close()
        c2.close()
        c2 = ExitStack()
        sa_ = sb_in(c2)
        y0_hi = sa_("y0_hi", [P, KT, S], F32R)
        y0_lo = sa_("y0_lo", [P, KT, S], F32R)
        c2.close()
        dl.close()
        mix.close()

        late = ExitStack()
        sl = sb_in(late)
        mx_hi = sl("mx_hi", [P, KT, S], F32R)
        mx_lo = sl("mx_lo", [P, KT, S], F32R)
        y_raw = sl("y_raw", [P, 2, S])
        mix_acc = sl("mix_acc", [P, KT, S])
        y1_hi = sl("y1_hi", [P, KT, S], F32R)
        y1_lo = sl("y1_lo", [P, KT, S], F32R)
        y_hi, y_lo = (y0_hi, y1_hi, y0_hi), (y0_lo, y1_lo, y0_lo)
        g_in = sl("g_in", [P, 3, S])
        g_tmp = sl("g_tmp", [P, S])
        late.close()
        late = ExitStack()
        sl = sb_in(late)
        h_lo = sl("h_lo", [P, 2 * KT, S], F32R)
        h1 = sl("h1", [P, ST, D])
        post = sl("post", [P, 3, D])
        f_T = sl("f_T", [P, KT, S])
        tok = sl("tok", [P, 2, D])
        part = ExitStack()
        rows = sb_in(part)("rows", [P, 2, D])
        part.close()
        relu = sl("relu", [P, 2, S])
        sq = sl("sq", [P, 2, S])
        ssum = sl("ssum", [P, S])
        part = ExitStack()
        junk = sb_in(part)("junk", [P, D])
        part.close()
        sqs = sl("sqs", [P, 2, S])
        n2_hi = sl("n2_hi", [P, KT, S], F32R)
        n2_lo = sl("n2_lo", [P, KT, S], F32R)
        h_hi = sl("h_hi", [P, 2 * KT, S], F32R)
        late.close()

        ld = [sem(f"ld{i}") for i in range(RAW)]
        hi_ready = sem("hi_ready")
        lo_ready = sem("lo_ready")
        tile_used = sem("tile_used")
        acc_free = sem("acc_free")
        in_par, in_mem, in_oh, in_ba, in_relb, in_id, in_cst = (
            sem(n) for n in ("in_par", "in_mem", "in_oh", "in_ba", "in_relb", "in_id", "in_cst"))
        in_x = [sem(f"in_x{i}") for i in range(ST)]
        ones_set = sem("ones_set")
        pad_set = sem("pad_set")
        vch = sem("vch")
        ach = sem("ach")
        pch = sem("pch")
        su_sq = sem("su_sq")
        su_norm = sem("su_norm")
        su_tr = sem("su_tr")
        su_full = sem("su_full")
        su_hi = sem("su_hi")
        su_lo = sem("su_lo")
        ba_split = sem("ba_split")
        ba_mm = sem("ba_mm")
        ba_act = sem("ba_act")
        ba_dve = sem("ba_dve")
        g_ready = sem("g_ready")
        g_mm = sem("g_mm")
        g_exp = sem("g_exp")
        f_mm = sem("f_mm")
        f_sb = sem("f_sb")
        f_out = sem("f_out")
        f_rep = sem("f_rep")
        strip_in = sem("strip_in")
        strip_ok = sem("strip_ok")
        lam_sum = sem("lam_sum")
        lam_exp = sem("lam_exp")
        a_mm = sem("a_mm")
        a_act = sem("a_act")
        a_dve = sem("a_dve")
        a_max = sem("a_max")
        d_mm = sem("d_mm")
        d_act = sem("d_act")
        d_dve = sem("d_dve")
        d_pool = sem("d_pool")
        at_ready = sem("at_ready")
        cx_ready = sem("cx_ready")
        cy_ready = sem("cy_ready")
        ct_ready = sem("ct_ready")
        co_ready = sem("co_ready")
        zt_ready = sem("zt_ready")
        z_ready = sem("z_ready")
        y_out = sem("y_out")
        yb_out = sem("yb_out")
        gs_ready = sem("gs_ready")
        g_out = sem("g_out")
        y_pre = [sem(f"y_pre{i}") for i in range(2)]
        y_in = [sem(f"y_in{i}") for i in range(2)]
        yh_ready = sem("yh_ready")
        yl_ready = sem("yl_ready")
        gin = [sem(f"gin{i}") for i in range(3)]
        gated = sem("gated")
        merged = sem("merged")
        mxh_ready = sem("mxh_ready")
        mxl_ready = sem("mxl_ready")
        o_ev = sem("o_ev")
        sqs_ok = sem("sqs_ok")
        sqs_sum = sem("sqs_sum")
        ss_mm = sem("ss_mm")
        tr_f = sem("tr_f")
        f_tok = sem("f_tok")
        h1_ok = sem("h1_ok")
        hg_ok = sem("hg_ok")
        ss2 = sem("ss2")
        rs2 = sem("rs2")
        n2n = sem("n2n")
        tr2 = sem("tr2")
        n2h = sem("n2h")
        n2l = sem("n2l")
        in_h1, in_post = sem("in_h1"), sem("in_post")
        relu_ok = sem("relu_ok")
        sq_ok = sem("sq_ok")
        hh_ok = sem("hh_ok")
        hl_ok = sem("hl_ok")
        f_ev = sem("f_ev")
        o_done = sem("o_done")

        block = ctx.enter_context(nc.Block())

        LAMS, LAME, NLAM = smd[:, 2:4], smd[:, 4:6], smd[:, 6:7]
        relb_sb = sml[0:BUCKETS, 32:32 + HA]
        ealog = sml[:, 64:64 + HB]
        f_row = qkv_T[0:HA, 1, 2, 0:SPAN]
        p_a_scr = flat(conv_o[:, 0])
        lam_prod = z_t[:, 0:2 * DA].rearrange("p (a d) -> p a d", a=2)
        BR = (2, 0, 1)
        N_BR = 3 * KT
        A_END = max(n for n, s in enumerate(SLOTS) if s[3] is not None)

        def preload_at(n):
            k = n - A_END - 2
            return range(max(k, 0), KT) if n == len(SLOTS) - 1 else range(k, k + 1) if 0 <= k < KT else ()

        G_SLOT = 11
        BIAS_SLOTS = [9, 14, 20]
        GSUB, GDN = smd[:, 7:8], smd[:, 8:9]
        mxa, nba = smd[:, 16:20], smd[:, 20:24]
        sma, rca = smd[:, 24:32], smd[:, 32:40]
        ssa, rsa, tma = smd[:, 40:44], smd[:, 44:48], smd[:, 48:52]
        ssd, rsd, tmd = smd[:, 56:64], smd[:, 64:72], smd[:, 72:80]

        N_SU = ST + MT
        MEM_SLOTS = [1, 2]
        BA_SLOT, F_SLOT = 4, 6
        bank_of = {3: 0, 2: 512 + 128, 1: 1024 + 256, 0: 512}
        pack_of = {0: 0, 1: P, 2: 3 * P, 3: 6 * P}

        def t_bank(kt, q):
            return {0: q * P, 1: 512 + q * P, 2: 1024 + q * P, 3: 512}[kt]

        def t_pack(kt, q):
            return t_bank(kt, q) if kt != 2 else 1024 + (q - 2) * P

        LATE = []
        t = N_MIX
        while t < NT:
            k = 2 if TILES[t][0] == "f2" else 1
            LATE.append((TILES[t], t, k))
            t += k
        L_F1 = [32, 56]
        L_F2 = [48, 72]

        def tiles_of(n):
            return LATE[n][1] if n < len(LATE) else NT

        EXP_KINDS = ("cs", "as0", "as1")

        def lagged(n, lag, kinds):
            i = SLOTS[n - lag][3] if n >= lag else None
            return i if i is not None and ATTN[i][0] in kinds else None

        def row_parts(j):
            if j < ST:
                return n_hi[:, :, j * P:(j + 1) * P], n_lo[:, :, j * P:(j + 1) * P]
            return m_hi[:, :, (j - ST) * P:(j - ST + 1) * P], m_lo[:, :, (j - ST) * P:(j - ST + 1) * P]

        trio = [ps_a, ps_d, acc]
        from_f, back = (lambda i: trio[i % 3]), (lambda i: trio[(i + 1) % 3])

        def two(ps):
            return flat(ps[:])[:, 0:1024]

        def blocks(ap):
            return ap.rearrange("p (a b) -> p a b", b=P)

        @block.sync
        def _(sp):
            for i in range(ST):
                sp.dma_start(x_tok[:, i], x[i * P:(i + 1) * P]).then_inc(in_x[i], 16)
                if i == 1:
                    sp.dma_start(cst[:, C_ID], consts[:, C_ID]).then_inc(in_id, 16)
            sp.dma_start(par[:], params).then_inc(in_par, 16)

            def load(t):
                if t < NT:
                    if t >= RAW:
                        sp.wait_ge(lo_ready, t - RAW + 1)
                    sp.dma_start(w_raw[:, t % RAW], weights[t]).then_inc(ld[t % RAW], 16)

            load(0)
            sp.dma_start(w_ba_sb[:], w_ba).then_inc(in_ba, 16)
            load(1)
            sp.dma_start(m_tok[:], mem.rearrange("(t p) d -> p t d", p=P)).then_inc(in_mem, 16)
            load(2)
            sp.dma_start(cst[:, C_ID + 1:], consts[:, C_ID + 1:]).then_inc(in_cst, 16)
            sp.dma_start(onehot_sb, onehot).then_inc(in_oh, 16)
            sp.dma_start(relb_sb, relb).then_inc(in_relb, 16)
            def bias(step):
                if step == 0:
                    sp.wait_ge(f_sb, 1)
                    sp.dma_start(f_dram, f_row).then_inc(f_out, 16)
                elif step == 1:
                    sp.wait_ge(f_out, 16)
                    sp.dma_start(frep_dram, bass.AP(tensor=f_dram.tensor, offset=f_dram.offset,
                                                    ap=[[SPAN, HA], [0, P], [1, SPAN]])).then_inc(f_rep, 16)
                elif step == 2:
                    sp.wait_ge(f_rep, 16)
                    sp.dma_start(strip[:], bass.AP(tensor=frep_dram.tensor, offset=frep_dram.offset + P - 1,
                                                   ap=[[SPAN - 1, P], [P * SPAN, HA], [1, 2 * P]])).then_inc(strip_in, 16)

            for slot, (main, ev, fi, sa, sd) in enumerate(SLOTS):
                if slot in BIAS_SLOTS:
                    bias(BIAS_SLOTS.index(slot))
                if ev is not None:
                    load(ev + RAW)
                    if TILES[ev][0] == "gate":
                        n = n_gate[ev]
                        sp.wait_ge(gs_ready, n + 1)
                        sp.dma_start(gate_dram[TILES[ev][1]], gate_st[:]).then_inc(g_out, 16)
                if sa is not None and ATTN[sa][0] in ("cv", "ay"):
                    kind, h = ATTN[sa]
                    sp.wait_ge(a_act, aA[sa + 1])
                    if kind == "cv":
                        sp.dma_start(y_dram[2, :, 2 * h:2 * h + 2], y_st[:]).then_inc(y_out, 16)
                    else:
                        sp.dma_start(y_dram[0, :, h], y_st[:, 0]).then_inc(y_out, 16)
                if sd is not None and DELTA[sd][0] == "dO":
                    p = DELTA[sd][1]
                    sp.wait_ge(d_dve, dD[sd + 1])
                    sp.dma_start(y_dram[1, :, 2 * p:2 * p + 2],
                                 flat(ET[:]).rearrange("p (a b) -> p a b", a=2)).then_inc(yb_out, 16)
                for kk in preload_at(slot):
                    if kk == 0:
                        sp.wait_ge(y_out, 16 * n_spill[-1])
                    if kk >= 2:
                        sp.wait_ge(yl_ready, kk - 1)
                    sp.dma_start(y_st[:, kk % 2], y_dram[BR[0], :, kk]).then_inc(y_pre[kk % 2], 16)
            sp.wait_ge(yb_out, 16 * (HB // 2))
            sp.wait_ge(g_out, 16 * len(gate_tiles))
            sp.wait_ge(tile_used, N_MIX)
            sp.wait_ge(acc_free, N_MIX)
            for r, (tile, t0, k) in enumerate(LATE):
                if r < N_BR:
                    b, m = r // KT, r % KT
                    if r < 2 * KT:
                        sp.wait_ge(yl_ready, KT + max(r - 1, 0))
                        sp.dma_start(y_raw[:, r % 2], y_dram[BR[b + 1], :, m]).then_inc(y_in[r % 2], 16)
                    if r >= 3:
                        sp.wait_ge(gated, r - 2)
                    sp.dma_start(g_in[:, r % 3], gate_dram[tile[1]]).then_inc(gin[r % 3], 16)
                if r == N_BR + 2:
                    sp.wait_ge(tile_used, tiles_of(N_BR))
                    sp.wait_ge(mxl_ready, KT)
                    sp.dma_start(post[:], post_g).then_inc(in_post, 16)
                    sp.dma_start(h1[:], x.rearrange("(t p) d -> p t d", p=P)).then_inc(in_h1, 16)
                for j in range(k):
                    load(t0 + j + RAW)
            for i in range(ST):
                sp.wait_ge(h1_ok, ST + i + 1)
                sp.dma_start(out[i * P:(i + 1) * P, :], h1[:, i]).then_inc(o_done, 16)
            sp.wait_ge(o_done, 16 * ST)

        @block.gpsimd
        def _(pool):
            def split_lo(t):
                if t < NT:
                    pool.wait_ge(hi_ready, t + 1)
                    if t >= SPL:
                        pool.wait_ge(tile_used, t - SPL + 1)
                    nc.gpsimd.tensor_tensor(w_lo[:, t % SPL], w_raw[:, t % RAW],
                                            w_hi[:, t % SPL].bitcast(F32), ALU.subtract).then_inc(lo_ready, 1)

            nc.gpsimd.memset(ones[:], 1.0).then_inc(ones_set, 1)
            nc.gpsimd.memset(conv_x[:, :, 0:3], 0.0).then_inc(pad_set, 1)
            for j in range(N_SU):
                if j == ST:
                    for t in range(SPL):
                        split_lo(t)
                pool.wait_ge(su_hi, j + 1)
                hi, lo = row_parts(j)
                nc.gpsimd.tensor_tensor(lo, full[:, j % 2], hi.bitcast(F32), ALU.subtract).then_inc(su_lo, 1)

            def delta(i):
                kind, p, lv = DELTA[i]
                if "P" not in PARTS[kind]:
                    return
                pool.wait_ge(d_mm, i + 1)
                heads = slice(2 * p, 2 * p + 2)
                if kind == "dv":
                    pool.wait_ge(g_exp, 1)
                    last = nc.gpsimd.tensor_tensor(SCR[:], over(cst[:, C_AFTER, :], 8),
                                                   along(flat(gdec[:, heads]), P), ALU.mult)
                elif kind == "dkT":
                    last = nc.gpsimd.tensor_tensor(K[:], K[:], along(flat(e_tail[:, heads]), P), ALU.mult)
                elif kind == "dkb":
                    last = nc.gpsimd.tensor_tensor(KB[:], KB[:], along(flat(e_in[:, heads]), P), ALU.mult)
                elif kind == "dL":
                    pool.wait_ge(d_dve, dD[i + 1])
                    last = nc.gpsimd.tensor_tensor(SCR[:], LT[:], over(cst[:, C_MASK0, :], 8), ALU.mult)
                elif kind == "dA":
                    nc.gpsimd.tensor_tensor(XT[:], LT[:], over(cst[:, C_MASK0 + 1, :], 8), ALU.mult)
                    pool.wait_ge(at_ready, p + 1)
                    last = nc.gpsimd.tensor_tensor(AT[:], AT[:], over(cst[:, C_UPTO, :], 8), ALU.mult)
                elif kind == "Wb":
                    last = nc.gpsimd.tensor_tensor(XT[:], LT[:], over(cst[:, C_MASK0 + lv + 1, :], 8), ALU.mult)
                last.then_inc(d_pool, 1)

            def y_lo_tile(b, kk):
                pool.wait_ge(yh_ready, b * KT + kk + 1)
                src = y_raw[:, kk % 2] if b else y_st[:, kk % 2]
                nc.gpsimd.tensor_tensor(y_lo[b][:, kk], src, y_hi[b][:, kk].bitcast(F32),
                                        ALU.subtract).then_inc(yl_ready, 1)

            for slot, (main, ev, fi, sa, sd) in enumerate(SLOTS):
                if ev is not None:
                    split_lo(ev + SPL)
                    if TILES[ev][0] == "gate":
                        n = n_gate[ev]
                        pool.wait_ge(acc_free, ev + 1)
                        nc.gpsimd.tensor_scalar(gate_st[:], gate_st[:], 0.5, 0.5, ALU.mult,
                                                ALU.add).then_inc(gs_ready, 1)
                if sd is not None:
                    delta(sd)
                for kk in preload_at(slot):
                    y_lo_tile(0, kk)

            def sum_squares(u, m):
                if m:
                    pool.wait_ge(sqs_ok, u * KT + m + 1)
                    if m > 1:
                        pool.wait_ge(sqs_sum, u * (KT - 1) + m - 1)
                    nc.gpsimd.tensor_tensor(ssum[:], ssum[:], sqs[:, m % 2], ALU.add).then_inc(sqs_sum, 1)

            def residual(u, i):
                n = u * ST + i
                pool.wait_ge(f_tok, n + 1)
                nc.gpsimd.tensor_tensor(h1[:, i], h1[:, i], tok[:, i % 2], ALU.add).then_inc(h1_ok, 1)

            for r, (tile, t0, k) in enumerate(LATE):
                if 1 <= r <= 2 * KT:
                    y_lo_tile(1 + (r - 1) // KT, (r - 1) % KT)
                for j in range(k):
                    split_lo(t0 + j + SPL)
                if r < N_BR and r // KT == 2:
                    m = r % KT
                    pool.wait_ge(mxh_ready, m + 1)
                    nc.gpsimd.tensor_tensor(mx_lo[:, m], mix_acc[:, m], mx_hi[:, m].bitcast(F32),
                                            ALU.subtract).then_inc(mxl_ready, 1)
                if tile[0] == "out":
                    sum_squares(0, tile[1])
                if r == N_BR + KT - 1:
                    for i in range(ST):
                        residual(0, i)
                        pool.wait_ge(h1_ok, i + 1)
                        if i >= 2:
                            pool.wait_ge(tr2, i - 1)
                        nc.gpsimd.tensor_tensor(rows[:, i % 2], h1[:, i], post[:, 1], ALU.mult).then_inc(hg_ok, 1)
                if r >= L_F2[1]:
                    sum_squares(1, tile[1] % KT)
                if tile[0] == "f1":
                    f = tile[1]
                    pool.wait_ge(hh_ok, f + 1)
                    nc.gpsimd.tensor_tensor(h_lo[:, f % 16], sq[:, f % 2], h_hi[:, f % 16].bitcast(F32),
                                            ALU.subtract).then_inc(hl_ok, 1)
            for i in range(ST):
                residual(1, i)

        @block.scalar
        def _(act):
            def square(j):
                if j < ST:
                    act.wait_ge(in_x[j], 16)
                else:
                    act.wait_ge(in_mem, 16)
                if j:
                    act.wait_ge(su_sq, j)
                nc.scalar.activation(p_a_scr, x_tok[:, j] if j < ST else m_tok[:, j - ST], ACT.Square,
                                     accum_out=sml[:, j:j + 1]).then_inc(su_sq, 1)

            def row_hi(j):
                act.wait_ge(su_full, j + 1)
                nc.scalar.copy(row_parts(j)[0], full[:, j % 2]).then_inc(su_hi, 1)

            for j in range(ST):
                square(j)
            for j in range(ST):
                row_hi(j)
            for j in range(ST, N_SU):
                square(j)
            for j in range(ST, N_SU):
                row_hi(j)

            def bias_values():
                act.wait_ge(f_mm, 1)
                nc.scalar.mul(f_row, ps_a[0:HA, 0, 0:SPAN], 1.0 / SC_A).then_inc(f_sb, 1)

            def beta_and_decay():
                act.wait_ge(lam_sum, 1)
                nc.scalar.activation(LAME, LAMS, ACT.Exp).then_inc(lam_exp, 1)
                act.wait_ge(ba_dve, 1)
                nc.scalar.activation(ba[:, 0], ba[:, 0], ACT.Tanh, scale=0.5)
                nc.scalar.activation(ba[:, 2], ba[:, 2], ACT.Exp)
                nc.scalar.activation(ealog, par[:, PC_ALOG:PC_ALOG + HB], ACT.Exp).then_inc(ba_act, 1)

            def evacuate(t):
                kind, j = TILES[t]
                bank = acc[:, t % 2]
                act.wait_ge(tile_used, t + 1)
                free = NEED_FREE.get(TILES[t])
                if free in a_idx:
                    act.wait_ge(a_mm, a_idx[free] + 1)
                elif kind == "dz" and free is not None:
                    act.wait_ge(d_dve, dD[d_idx[free] + 1])
                if kind == "mk":
                    last = nc.scalar.copy(mk_T[:, j], bank[:, 0:MEM])
                elif kind == "mv":
                    if j == 0:
                        act.wait_ge(ba_split, 1)
                    last = nc.scalar.copy(mv_T[:, j], bank[:, 0:MEM])
                elif kind == "cq":
                    last = nc.scalar.copy(cq_T[:, (j // 2) % 2, j % 2], bank)
                elif kind in ("aq", "ak", "av"):
                    if (kind, j) == ("av", 1):
                        act.wait_ge(f_out, 16)
                    last = nc.scalar.copy(qkv_T[:, j % 2, ("aq", "ak", "av").index(kind)], bank)
                elif kind in ("dq", "dk", "dv"):
                    n = n_conv[t]
                    if n == 0:
                        act.wait_ge(pad_set, 1)
                    if n >= 2:
                        act.wait_ge(co_ready, n - 1)
                    last = nc.scalar.copy(conv_x[:, n % 2, 3:3 + S], bank)
                elif kind == "dz":
                    last = nc.scalar.copy(zs[:, j % 2], bank)
                elif kind == "gate":
                    n = n_gate[t]
                    if n:
                        act.wait_ge(g_out, 16 * n)
                    last = nc.scalar.activation(gate_st[:], bank, ACT.Tanh, scale=0.5)
                last.then_inc(acc_free, 1)

            def finish(t):
                if t in n_conv:
                    n = n_conv[t]
                    act.wait_ge(cy_ready, n + 1)
                    nc.scalar.activation(conv_x[:, n % 2, 3:3 + S], conv_y[:, n % 2], ACT.Tanh,
                                         scale=0.5).then_inc(ct_ready, 1)
                else:
                    n = n_z[t]
                    if n:
                        act.wait_ge(z_ready, n)
                    act.wait_ge(acc_free, t + 1)
                    nc.scalar.activation(z_t[:], zs[:, n % 2], ACT.Tanh, scale=0.5).then_inc(zt_ready, 1)

            def attn(i):
                kind, h = ATTN[i]
                act.wait_ge(a_mm, i + 1)
                if kind == "mv":
                    last = nc.scalar.copy(mv_tok[:, :, h * 512:(h + 1) * 512], ps_a[:, 0:2])
                elif kind == "cs":
                    act.wait_ge(a_max, n_max[i + 1])
                    for s in range(ST):
                        last = nc.scalar.activation(p_c[:, s], ps_a[:, s // 2, (s % 2) * MEM:(s % 2 + 1) * MEM],
                                                    ACT.Exp, bias=nba[:, s:s + 1], scale=SC_C,
                                                    accum_out=sma[:, s:s + 1])
                elif kind == "ct":
                    last = nc.scalar.copy(pT_c[:], ps_a[:, 0:2])
                elif kind in ("cv", "ay"):
                    if n_spill[i]:
                        act.wait_ge(y_out, 16 * n_spill[i])
                    if kind == "cv":
                        last = nc.scalar.copy(y_st[:], ps_a[:, 0:2])
                    else:
                        last = nc.scalar.activation(y_st[:, 0], ps_a[:, 0], ACT.Copy, scale=GSUB)
                elif kind == "av":
                    last = nc.scalar.copy(v_tok[:], ps_a[:, 0])
                elif kind in ("as0", "as1"):
                    m = int(kind[2])
                    act.wait_ge(a_max, n_max[i + 1])
                    for q in range(ST):
                        w = (q + 1) * P
                        src = flat(ps_a[:])[:, bank_of[q]:bank_of[q] + w]
                        last = nc.scalar.activation(p_a[:, m, pack_of[q]:pack_of[q] + w], src, ACT.Exp,
                                                    bias=nba[:, q:q + 1], scale=SC_A,
                                                    accum_out=sma[:, 4 * m + q:4 * m + q + 1])
                elif kind == "at":
                    nc.scalar.copy(wT[:, 0:1024], two(ps_a))
                    last = nc.scalar.copy(wT[:, 1024:1280], ps_a[:, 2, 256:512])
                elif kind == "ap":
                    last = nc.scalar.copy(flat(o_a[:]), ps_a[:, 0])
                last.then_inc(a_act, 1)

            def delta(i):
                kind, p, c = DELTA[i]
                if "A" not in PARTS[kind]:
                    return
                act.wait_ge(d_mm, i + 1)
                if kind == "dE":
                    if p:
                        act.wait_ge(yb_out, 16 * p)
                    last = nc.scalar.activation(flat(ET[:]), two(ps_d), ACT.Exp)
                elif kind == "sb":
                    o_v = O[:].rearrange("p (h c) d -> p h c d", h=2)[:, :, c]
                    last = nc.scalar.copy(o_v, ps_d[:, 0, 0:256].rearrange("p (h d) -> p h d", h=2))
                else:
                    dst = {"dq": Q, "dk": K, "dqT": QT, "dqd": QDT, "dkT": KTT, "dkb": KBT, "T1": TN, "Tc": TN,
                           "Za": Z, "dU": U, "dW": WT}[kind]
                    last = nc.scalar.copy(flat(dst[:]), two(ps_d))
                last.then_inc(d_act, 1)

            for n, (main, ev, fi, sa, sd) in enumerate(SLOTS):
                if n == G_SLOT:
                    act.wait_ge(g_mm, 1)
                    for m, dst in enumerate((e_in, e_tail, e_all)):
                        last = nc.scalar.activation(flat(dst[:]), ps_d[:, 2, m * 32:(m + 1) * 32], ACT.Exp)
                    last.then_inc(g_exp, 1)
                if n == BA_SLOT:
                    beta_and_decay()
                if n == F_SLOT:
                    bias_values()
                if ev is not None:
                    evacuate(ev)
                if fi is not None:
                    finish(fi)
                if sd is not None:
                    delta(sd)
                if sa is not None and ATTN[sa][0] not in EXP_KINDS:
                    attn(sa)
                if lagged(n, EXP_LAG, EXP_KINDS) is not None:
                    attn(lagged(n, EXP_LAG, EXP_KINDS))

            def squares(u, m, src):
                if m == 0 and u:
                    act.wait_ge(ss_mm, 1)
                if m > 2:
                    act.wait_ge(sqs_sum, u * (KT - 1) + m - 2)
                nc.scalar.activation(sqs[:, m % 2] if m else ssum[:], src, ACT.Square).then_inc(sqs_ok, 1)

            for r in range(N_BR, N_BR + KT):
                m = r - N_BR
                act.wait_ge(tile_used, tiles_of(r + 1))
                if m == 0:
                    act.wait_ge(mxl_ready, KT)
                squares(0, m, acc[:, r % 2])
                nc.scalar.copy(f_T[:, m], acc[:, r % 2]).then_inc(o_ev, 1)

            def square_row(i):
                act.wait_ge(h1_ok, i + 1)
                if i:
                    act.wait_ge(ss2, i)
                else:
                    act.wait_ge(sqs_sum, KT - 1)
                nc.scalar.activation(junk[:], h1[:, i], ACT.Square, accum_out=sml[:, 100 + i:101 + i]).then_inc(ss2, 1)

            def scale_row(i):
                act.wait_ge(hg_ok, i + 1)
                act.wait_ge(rs2, i // 2 + 1)
                nc.scalar.mul(rows[:, i % 2], rows[:, i % 2], sml[:, 108 + i:109 + i]).then_inc(n2n, 1)

            def row_hi2(i):
                act.wait_ge(tr2, i + 1)
                nc.scalar.copy(n2_hi[:, :, i * P:(i + 1) * P], blocks(two(back(i)))).then_inc(n2h, 1)

            for i in range(2):
                square_row(i)
            for i in range(2):
                scale_row(i)
            for i in range(2, ST):
                square_row(i)
                row_hi2(i - 2)
            for i in range(2, ST):
                scale_row(i)
            for i in range(2, ST):
                row_hi2(i)
            for f in range(DFF // P):
                act.wait_ge(relu_ok, f + 1)
                if f >= 2:
                    act.wait_ge(hl_ok, f - 1)
                nc.scalar.activation(sq[:, f % 2], relu[:, f % 2], ACT.Square).then_inc(sq_ok, 1)
            for m in range(KT):
                act.wait_ge(f_ev, KT + m + 1)
                squares(1, m, f_T[:, m])

        @block.vector
        def _(dve):
            n_own = [0]

            def link(ins):
                n_own[0] += 1
                ins.then_inc(vch, 1)
                dve.wait_ge(vch, n_own[0])

            V_ = nc.vector

            def rsqrt(dst, src, tmp, last_to=None):
                link(V_.tensor_scalar(tmp.bitcast(I32), src.bitcast(I32), 1, None, ALU.logical_shift_right))
                link(V_.tensor_scalar(dst.bitcast(I32), tmp.bitcast(I32), -1.0, float(0x5f3759df), ALU.mult, ALU.add))
                for n in range(3):
                    link(V_.tensor_tensor(tmp, dst, dst, ALU.mult))
                    link(V_.scalar_tensor_tensor(out=tmp, in0=tmp, scalar=-0.5, in1=src, op0=ALU.mult, op1=ALU.mult))
                    ins = V_.scalar_tensor_tensor(out=dst, in0=tmp, scalar=1.5, in1=dst, op0=ALU.add, op1=ALU.mult)
                    if n == 2 and last_to is not None:
                        ins.then_inc(last_to, 1)
                    else:
                        link(ins)

            def split_hi(t):
                if t < NT:
                    dve.wait_ge(ld[t % RAW], 16 * (t // RAW + 1))
                    if t >= SPL:
                        dve.wait_ge(tile_used, t - SPL + 1)
                        dve.wait_ge(lo_ready, t - SPL + 1)
                    V_.tensor_copy(w_hi[:, t % SPL], w_raw[:, t % RAW]).then_inc(hi_ready, 1)

            def rms_of_two(j):
                v, r, tm = sml[:, j:j + 2], sml[:, 8 + j:10 + j], sml[:, 16 + j:18 + j]
                dve.wait_ge(su_sq, j + 2)
                link(V_.tensor_scalar(v, v, 1.0 / D, EPS, ALU.mult, ALU.add))
                rsqrt(r, v, tm)

            def normalise(j):
                rows_in = x_tok[:, j] if j < ST else m_tok[:, j - ST]
                V_.tensor_scalar(rows_in, rows_in, sml[:, 8 + j:9 + j], None, ALU.mult).then_inc(su_norm, 1)

            def gain(j):
                dve.wait_ge(su_tr, j + 1)
                if j >= 2:
                    dve.wait_ge(su_lo, j - 1)
                g = par[:, PC_PRE:PC_PRE + KT] if j < ST else par[:, PC_MEM:PC_MEM + KT]
                V_.tensor_tensor(full[:, j % 2], blocks(two(side[j % 2])), along(g, P), ALU.mult).then_inc(su_full, 1)

            rms_of_two(0)
            normalise(0)
            normalise(1)
            rms_of_two(2)
            normalise(2)
            dve.wait_ge(in_par, 16)
            gain(0)
            normalise(3)
            for j in range(1, ST):
                gain(j)
            for t in range(SPL):
                split_hi(t)
            rms_of_two(ST)
            for j in range(ST, N_SU):
                normalise(j)
            for j in range(ST, N_SU):
                gain(j)
            dve.wait_ge(in_ba, 16)
            link(V_.tensor_copy(wb_hi[:], w_ba_sb[:]))
            V_.tensor_tensor(wb_lo[:], w_ba_sb[:], wb_hi[:].bitcast(F32), ALU.subtract).then_inc(ba_split, 1)
            lamv = par[:, PC_LAM:PC_LAM + 4 * DA].rearrange("p (a b d) -> p a b d", a=2, b=2)
            link(V_.tensor_tensor(lam_prod, lamv[:, :, 0], lamv[:, :, 1], ALU.mult))
            V_.reduce_sum(LAMS, lam_prod, AX_X).then_inc(lam_sum, 1)
            V_.tensor_scalar(GSUB, par[:, PC_SUB:PC_SUB + 1], 1.0 - LAM_INIT, None, ALU.mult)
            V_.tensor_scalar(GDN, par[:, PC_DNG:PC_DNG + 1], 0.5, None, ALU.mult)
            def beta_and_decay_inputs():
                dve.wait_ge(ba_mm, 1)
                bav = ps_a[:, 2, 0:ST * 2 * HB].rearrange("p (c h) -> p h c", c=ST)
                V_.tensor_copy(ba[:, 0], bav[:, 0:HB])
                link(V_.tensor_tensor(ba[:, 1], bav[:, HB:2 * HB], along(par[:, PC_DTB:PC_DTB + HB], ST), ALU.add))
                link(V_.tensor_scalar(ba[:, 2], ba[:, 1], -1.0, None, ALU.mult))
                V_.tensor_tensor(ba[:, 2], ba[:, 2], ba[:, 1], ALU.min).then_inc(ba_dve, 1)

            def beta_and_decay():
                dve.wait_ge(lam_exp, 1)
                link(V_.tensor_tensor(NLAM, LAME[:, 1:2], LAME[:, 0:1], ALU.subtract))
                link(V_.tensor_scalar(NLAM, NLAM, LAM_INIT, None, ALU.subtract))
                dve.wait_ge(ba_act, 1)
                V_.tensor_scalar(beta[:], ba[:, 0], 0.5, 0.5, ALU.mult, ALU.add)
                V_.tensor_scalar(hbeta[:], ba[:, 0], 0.25, 0.25, ALU.mult, ALU.add)
                link(V_.tensor_scalar(ba[:, 3], ba[:, 2], 2.0, None, ALU.add))
                link(V_.reciprocal(ba[:, 4], ba[:, 3]))
                link(V_.tensor_tensor(ba[:, 4], ba[:, 4], ba[:, 2], ALU.mult))
                link(V_.tensor_tensor(ba[:, 5], ba[:, 4], ba[:, 4], ALU.mult))
                link(V_.tensor_scalar(ba[:, 3], ba[:, 5], 1.0 / 17, None, ALU.mult))
                for n in range(15, 1, -2):
                    link(V_.scalar_tensor_tensor(out=ba[:, 3], in0=ba[:, 3], scalar=1.0 / n, in1=ba[:, 5],
                                                 op0=ALU.add, op1=ALU.mult))
                link(V_.scalar_tensor_tensor(out=ba[:, 3], in0=ba[:, 3], scalar=1.0, in1=ba[:, 4], op0=ALU.add, op1=ALU.mult))
                link(V_.tensor_scalar(ba[:, 1], ba[:, 1], 0.0, None, ALU.max))
                link(V_.scalar_tensor_tensor(out=ba[:, 1], in0=ba[:, 3], scalar=2.0, in1=ba[:, 1], op0=ALU.mult, op1=ALU.add))
                V_.scalar_tensor_tensor(out=gdec[:], in0=ba[:, 1], scalar=-1.0, in1=along(ealog, ST),
                                        op0=ALU.mult, op1=ALU.mult).then_inc(g_ready, 1)

            def conv(t):
                kind, h = TILES[t]
                n = n_conv[t]
                col = PC_CONV + 4 * ({"dq": 0, "dk": 8, "dv": 16}[kind] + h)
                dve.wait_ge(acc_free, t + 1)
                y = conv_y[:, n % 2]
                link(V_.tensor_scalar(y, conv_x[:, n % 2, 0:S], par[:, col:col + 1], None, ALU.mult))
                for j in (1, 2, 3):
                    ins = V_.scalar_tensor_tensor(out=y, in0=conv_x[:, n % 2, j:j + S], scalar=par[:, col + j:col + j + 1],
                                                  in1=y, op0=ALU.mult, op1=ALU.add)
                    if j < 3:
                        link(ins)
                ins.then_inc(cy_ready, 1)

            def finish(t):
                kind, h = TILES[t]
                if t in n_conv:
                    n = n_conv[t]
                    dve.wait_ge(ct_ready, n + 1)
                    if h >= 2:
                        dve.wait_ge(d_mm, d_idx[("dv", h // 2 - 1, 0)] + 1)
                    V_.scalar_tensor_tensor(out=conv_o[:, ("dq", "dk", "dv").index(kind), h % 2],
                                            in0=conv_x[:, n % 2, 3:3 + S], scalar=1.0, in1=conv_y[:, n % 2],
                                            op0=ALU.add, op1=ALU.mult).then_inc(co_ready, 1)
                else:
                    n = n_z[t]
                    dve.wait_ge(zt_ready, n + 1)
                    V_.scalar_tensor_tensor(out=zs[:, n % 2], in0=z_t[:], scalar=1.0, in1=zs[:, n % 2],
                                            op0=ALU.add, op1=ALU.mult).then_inc(z_ready, 1)

            def attn(i):
                kind, h = ATTN[i]
                if kind not in EXP_KINDS:
                    return
                dve.wait_ge(a_mm, i + 1)
                if kind == "cs":
                    link(V_.reduce_max(mxa, two(ps_a).rearrange("p (a b) -> p a b", a=ST), AX_X))
                    V_.tensor_scalar(nba, mxa, -SC_C, None, ALU.mult).then_inc(a_max, 1)
                else:
                    if (kind, h) == ("as0", 0):
                        dve.wait_ge(strip_in, 16)
                        link(V_.tensor_tensor(strip[:, :, P:2 * P], strip[:, :, P:2 * P],
                                              over(cst[:, C_CAUS, :], HA), ALU.add))
                    ps = flat(ps_a[:])
                    near = view(ps, [[512, 3], [1, 2 * P]], 256)
                    V_.tensor_tensor(near, near, over(strip[:, h], 3), ALU.add)
                    link(V_.tensor_tensor(ps[:, 512:512 + P], ps[:, 512:512 + P], strip[:, h, P:2 * P], ALU.add))
                    for q in range(ST):
                        ins = V_.reduce_max(mxa[:, q:q + 1], ps[:, bank_of[q]:bank_of[q] + (q + 1) * P], AX_X)
                    link(ins)
                    V_.tensor_scalar(nba, mxa, -SC_A, None, ALU.mult).then_inc(a_max, 1)

            def attn_scale(i):
                kind, h = ATTN[i]
                dve.wait_ge(a_act, aA[i + 1])
                if kind == "cs":
                    link(V_.reciprocal(rca[:, 0:4], sma[:, 0:4]))
                    last = V_.tensor_tensor(p_c[:], p_c[:], along(rca[:, 0:4], MEM), ALU.mult)
                    last.then_inc(a_dve, 1)
                elif kind == "as1":
                    link(V_.reciprocal(rca, sma))
                    link(V_.tensor_scalar(rca[:, 4:8], rca[:, 4:8], NLAM, None, ALU.mult))
                    for q in range(ST):
                        c = slice(pack_of[q], pack_of[q] + (q + 1) * P)
                        ins = V_.tensor_scalar(p_a[:, 1, c], p_a[:, 1, c], rca[:, 4 + q:5 + q], None, ALU.mult)
                    link(ins)
                    for q in range(ST):
                        c = slice(pack_of[q], pack_of[q] + (q + 1) * P)
                        ins = V_.scalar_tensor_tensor(out=p_a[:, 0, c], in0=p_a[:, 0, c], scalar=rca[:, q:q + 1],
                                                      in1=p_a[:, 1, c], op0=ALU.mult, op1=ALU.add)
                    ins.then_inc(a_dve, 1)
                else:
                    link(V_.tensor_tensor(p_a[:, 1, 0:S], flat(o_a[:]), flat(o_a[:]), ALU.mult))
                    link(V_.reduce_sum(ssa, p_a[:, 1, 0:S].rearrange("p (a b) -> p a b", a=ST), AX_X))
                    link(V_.tensor_scalar(ssa, ssa, 1.0 / P, EPS, ALU.mult, ALU.add))
                    rsqrt(rsa, ssa, tma)
                    V_.tensor_tensor(o_a[:], o_a[:], along(rsa, P), ALU.mult).then_inc(a_dve, 1)

            def scale_by_norm(buf, mul, add, factor):
                link(V_.tensor_tensor(SCR[:], buf[:], buf[:], ALU.mult))
                link(V_.reduce_sum(ssd, SCR[:], AX_X))
                link(V_.tensor_scalar(ssd, ssd, mul, add, ALU.mult, ALU.add))
                rsqrt(rsd, ssd, tmd)
                if factor != 1.0:
                    link(V_.tensor_scalar(rsd, rsd, factor, None, ALU.mult))
                return V_.tensor_tensor(buf[:], buf[:], along(rsd, P), ALU.mult)

            def delta(i):
                kind, p, c = DELTA[i]
                if "D" not in PARTS[kind]:
                    return
                dve.wait_ge(d_mm, i + 1)
                heads = slice(2 * p, 2 * p + 2)
                ps = blocks(two(ps_d))
                if kind == "dq":
                    dve.wait_ge(d_act, dA[i + 1])
                    last = scale_by_norm(Q, 1.0, 4 * EPS, P ** -0.5)
                elif kind == "dk":
                    dve.wait_ge(d_act, dA[i + 1])
                    link(scale_by_norm(K, 1.0, 4 * EPS, 1.0))
                    last = V_.tensor_tensor(KB[:], K[:], along(flat(beta[:, heads]), P), ALU.mult)
                elif kind == "dv":
                    last = V_.tensor_tensor(V[:], ps, along(flat(hbeta[:, heads]), P), ALU.mult)
                elif kind == "dqT":
                    dve.wait_ge(g_exp, 1)
                    last = V_.tensor_tensor(Q[:], Q[:], along(flat(e_in[:, heads]), P), ALU.mult)
                elif kind == "dL":
                    last = V_.tensor_tensor(LT[:], ps, ET[:], ALU.mult)
                elif kind == "dA":
                    V_.tensor_tensor(AT[:], ps, ET[:], ALU.mult).then_inc(at_ready, 1)
                    dve.wait_ge(d_pool, dP[i])
                    last = V_.tensor_tensor(TT[:], over(ident, 8), SCR[:], ALU.subtract)
                elif kind in ("Wb", "Wl"):
                    last = V_.tensor_tensor(TT[:], TT[:], ps, ALU.subtract)
                elif kind == "sa":
                    u_v = U[:].rearrange("p (h c) d -> p h c d", h=2)[:, :, c]
                    last = V_.tensor_tensor(vnew[:], u_v, ps_d[:, 0, 0:256].rearrange("p (h d) -> p h d", h=2),
                                            ALU.subtract)
                elif kind == "sb":
                    for hh in range(2):
                        kv = ps_d[:, 1, hh * P:(hh + 1) * P]
                        if c == 0:
                            last = V_.tensor_copy(state[:, hh], kv)
                        else:
                            last = V_.scalar_tensor_tensor(out=state[:, hh], in0=state[:, hh],
                                                           scalar=e_all[:, 2 * p + hh, c:c + 1], in1=kv,
                                                           op0=ALU.mult, op1=ALU.add)
                    if c == ST - 1:
                        link(last)
                        dve.wait_ge(d_act, dA[i + 1])
                        last = scale_by_norm(O, 1.0 / P, EPS, 1.0)
                elif kind == "dO":
                    dve.wait_ge(z_ready, 2 * (p + 1))
                    last = V_.scalar_tensor_tensor(out=flat(ET[:]), in0=two(ps_d), scalar=GDN, in1=flat(zs[:]),
                                                   op0=ALU.mult, op1=ALU.mult)
                last.then_inc(d_dve, 1)

            for n, (main, ev, fi, sa, sd) in enumerate(SLOTS):
                if n == BA_SLOT:
                    beta_and_decay_inputs()
                if n == BA_SLOT + 2:
                    beta_and_decay()
                if ev is not None:
                    split_hi(ev + SPL)
                if sd is not None:
                    delta(sd)
                if sa is not None:
                    attn(sa)
                if ev in n_conv:
                    conv(ev)
                if fi is not None:
                    finish(fi)
                if lagged(n, SCALE_LAG, ("cs", "as1")) is not None:
                    attn_scale(lagged(n, SCALE_LAG, ("cs", "as1")))
                if lagged(n, NORM_LAG, ("ap",)) is not None:
                    attn_scale(lagged(n, NORM_LAG, ("ap",)))
                for kk in preload_at(n):
                    dve.wait_ge(y_pre[kk % 2], 16 * (kk // 2 + 1))
                    if kk == 0:
                        dve.wait_ge(a_mm, len(ATTN))
                    V_.tensor_copy(y_hi[0][:, kk], y_st[:, kk % 2]).then_inc(yh_ready, 1)

            def y_hi_tile(n):
                dve.wait_ge(y_in[n % 2], 16 * (n // 2 + 1))
                if n == KT:
                    dve.wait_ge(tile_used, tiles_of(KT))
                V_.tensor_copy(y_hi[1 + n // KT][:, n % KT], y_raw[:, n % 2]).then_inc(yh_ready, 1)

            def rms_of_f(u):
                v, r, tm = ps_d[:, 2, 0:ST], sml[:, 116:116 + ST], sml[:, 120:120 + ST]
                dve.wait_ge(ss_mm, u + 1)
                link(V_.tensor_scalar(sml[:, 96:96 + ST], v, 1.0 / D, EPS, ALU.mult, ALU.add))
                rsqrt(r, sml[:, 96:96 + ST], tm)

            def norm_row(u, i):
                n = u * ST + i
                dve.wait_ge(tr_f, n + 1)
                if i >= 2:
                    dve.wait_ge(h1_ok, n - 1)
                V_.scalar_tensor_tensor(out=tok[:, i % 2], in0=two(from_f(i)), scalar=sml[:, 116 + i:117 + i],
                                        in1=post[:, 2 * u], op0=ALU.mult, op1=ALU.mult).then_inc(f_tok, 1)

            def rms_of_rows(j):
                v, r, tm = sml[:, 100 + 2 * j:102 + 2 * j], sml[:, 108 + 2 * j:110 + 2 * j], sml[:, 124:126]
                dve.wait_ge(ss2, 2 * j + 2)
                link(V_.tensor_scalar(v, v, 1.0 / D, EPS, ALU.mult, ALU.add))
                rsqrt(r, v, tm, last_to=rs2)

            def row_lo2(i):
                dve.wait_ge(n2h, i + 1)
                c = slice(i * P, (i + 1) * P)
                V_.tensor_tensor(n2_lo[:, :, c], blocks(two(back(i))), n2_hi[:, :, c].bitcast(F32),
                                 ALU.subtract).then_inc(n2l, 1)

            for r, (tile, t0, k) in enumerate(LATE):
                if 1 <= r <= 2 * KT:
                    y_hi_tile(r - 1)
                for j in range(k):
                    split_hi(t0 + j + SPL)
                bank = acc[:, r % 2]
                if r < N_BR:
                    b, m = r // KT, r % KT
                    dve.wait_ge(tile_used, tiles_of(r + 1))
                    dve.wait_ge(gin[r % 3], 16 * (r // 3 + 1))
                    if b == 0:
                        V_.tensor_tensor(mix_acc[:, m], bank, g_in[:, r % 3], ALU.mult).then_inc(gated, 1)
                    else:
                        V_.tensor_tensor(g_tmp[:], bank, g_in[:, r % 3], ALU.mult).then_inc(gated, 1)
                        dve.wait_ge(gated, r + 1)
                        ins = V_.tensor_tensor(mix_acc[:, m], mix_acc[:, m], g_tmp[:], ALU.add)
                        link(ins)
                        if b == 2:
                            V_.tensor_copy(mx_hi[:, m], mix_acc[:, m]).then_inc(mxh_ready, 1)
                elif r == N_BR + KT - 1:
                    rms_of_f(0)
                    dve.wait_ge(in_post, 16)
                    for i in range(3):
                        norm_row(0, i)
                    rms_of_rows(0)
                    norm_row(0, 3)
                    for i in range(2):
                        row_lo2(i)
                    rms_of_rows(1)
                    for i in range(2, ST):
                        row_lo2(i)
                elif tile[0] == "f1":
                    f = tile[1]
                    dve.wait_ge(tile_used, tiles_of(r + 1))
                    if f >= 2:
                        dve.wait_ge(sq_ok, f - 1)
                    V_.tensor_scalar(relu[:, f % 2], bank, 0.0, None, ALU.max).then_inc(relu_ok, 1)
                    dve.wait_ge(sq_ok, f + 1)
                    V_.tensor_copy(h_hi[:, f % 16], sq[:, f % 2]).then_inc(hh_ok, 1)
                elif tile[0] == "f2":
                    dve.wait_ge(tile_used, tiles_of(r + 1))
                    m = tile[1] % KT
                    if r < L_F2[0] + KT:
                        V_.tensor_copy(f_T[:, m], bank).then_inc(f_ev, 1)
                    else:
                        V_.tensor_tensor(f_T[:, m], f_T[:, m], bank, ALU.add).then_inc(f_ev, 1)
            rms_of_f(1)
            for i in range(ST):
                norm_row(1, i)

        @block.tensor
        def _(pe):
            mm = nc.tensor.matmul

            def transpose_rows(j):
                pe.wait_ge(su_norm, j + 1)
                if j >= 2:
                    pe.wait_ge(su_full, j - 1)
                src = x_tok[:, j] if j < ST else m_tok[:, j - ST]
                for m in range(KT):
                    last = nc.tensor.transpose(side[j % 2][:, m // 4, (m % 4) * P:(m % 4 + 1) * P],
                                               src[:, m * P:(m + 1) * P], ident)
                last.then_inc(su_tr, 1)

            def beta_and_decay():
                pe.wait_ge(ba_split, 1)
                for c in range(ST):
                    dst = ps_a[:, 2, c * 2 * HB:(c + 1) * 2 * HB]
                    for k in range(KT):
                        hi, lo = n_hi[:, k, c * P:(c + 1) * P], n_lo[:, k, c * P:(c + 1) * P]
                        mm(dst, hi, wb_hi[:, k], start=k == 0, stop=False)
                        mm(dst, hi, wb_lo[:, k], start=False, stop=False)
                        last = mm(dst, lo, wb_hi[:, k], start=False, stop=k == KT - 1)
                last.then_inc(ba_mm, 1)

            def bias_values():
                pe.wait_ge(in_oh, 16)
                pe.wait_ge(in_relb, 16)
                pe.wait_ge(su_full, N_SU)
                pe.wait_ge(su_lo, N_SU)
                mm(ps_a[0:HA, 0, 0:SPAN], relb_sb, onehot_sb, start=True, stop=True).then_inc(f_mm, 1)

            pe.wait_ge(in_id, 16)
            for j in range(ST):
                transpose_rows(j)
            pe.wait_ge(su_lo, ST)

            def weight_tile(bank, t, ks, hi_of, lo_of, start, stop, k_wait=None):
                for k in ks:
                    if k_wait is not None:
                        k_wait(k)
                    wh, wl = w_hi[:, t % SPL, k], w_lo[:, t % SPL, k]
                    mm(bank, wh, hi_of(k), start=start and k == 0, stop=False)
                    mm(bank, wh, lo_of(k), start=False, stop=False)
                    last = mm(bank, wl, hi_of(k), start=False, stop=stop and k == KT - 1)
                return last

            def main_half(t, half):
                kind = TILES[t][0]
                if half != 1:
                    pe.wait_ge(lo_ready, t + 1)
                    if t >= 2:
                        pe.wait_ge(acc_free, t - 1)
                ks = range(KT) if half is None else range(half * KT // 2, (half + 1) * KT // 2)
                if kind in ("mk", "mv"):
                    pe.wait_ge(su_lo, N_SU)
                    last = weight_tile(acc[:, t % 2, 0:MEM], t, ks, lambda k: m_hi[:, k], lambda k: m_lo[:, k], True, True)
                else:
                    last = weight_tile(acc[:, t % 2], t, ks, lambda k: n_hi[:, k], lambda k: n_lo[:, k], True, True)
                if half != 0:
                    last.then_inc(tile_used, 1)

            def attn(i):
                kind, h = ATTN[i]
                if i:
                    pe.wait_ge(a_act, aA[i])
                    if aD[i]:
                        pe.wait_ge(a_dve, aD[i])
                if kind == "mv":
                    if h == 0:
                        pe.wait_ge(acc_free, TILES.index(("mv", KT - 1)) + 1)
                    for j in range(4):
                        for mt in range(MT):
                            last = nc.tensor.transpose(ps_a[:, mt, j * P:(j + 1) * P],
                                                       mv_T[:, 4 * h + j, mt * P:(mt + 1) * P], ident)
                elif kind == "cs":
                    pe.wait_ge(acc_free, TILES.index(("cq", 2 * h + 1)) + 1)
                    for s in range(ST):
                        for dt in range(2):
                            last = mm(ps_a[:, s // 2, (s % 2) * MEM:(s % 2 + 1) * MEM],
                                      cq_T[:, h % 2, dt, s * P:(s + 1) * P], mk_T[:, 2 * h + dt],
                                      start=dt == 0, stop=dt == 1)
                elif kind == "ct":
                    for mt in range(MT):
                        for s in range(ST):
                            last = nc.tensor.transpose(ps_a[:, mt, s * P:(s + 1) * P],
                                                       p_c[:, s, mt * P:(mt + 1) * P], ident)
                elif kind == "cv":
                    for dt in range(2):
                        for mt in range(MT):
                            last = mm(ps_a[:, dt], mv_tok[:, mt, (2 * h + dt) * P:(2 * h + dt + 1) * P], pT_c[:, mt],
                                      start=mt == 0, stop=mt == MT - 1)
                elif kind == "av":
                    pe.wait_ge(acc_free, TILES.index(("av", h)) + 1)
                    for s in range(ST):
                        last = nc.tensor.transpose(ps_a[:, 0, s * P:(s + 1) * P], qkv_T[:, h % 2, 2, s * P:(s + 1) * P], ident)
                elif kind in ("as0", "as1"):
                    rows_m = slice(DA * int(kind[2]), DA * int(kind[2]) + DA)
                    ps = flat(ps_a[:])
                    for q in range(ST - 1, -1, -1):
                        last = mm(ps[:, bank_of[q]:bank_of[q] + (q + 1) * P], qkv_T[rows_m, h % 2, 0, q * P:(q + 1) * P],
                                  qkv_T[rows_m, h % 2, 1, 0:(q + 1) * P], start=True, stop=True)
                elif kind == "at":
                    ps = flat(ps_a[:])
                    for kt in range(ST):
                        for q in range(kt, ST):
                            last = nc.tensor.transpose(ps[:, t_bank(kt, q):t_bank(kt, q) + P],
                                                       p_a[:, 0, pack_of[q] + kt * P:pack_of[q] + (kt + 1) * P], ident)
                elif kind == "ap":
                    for q in range(ST):
                        for kt in range(q + 1):
                            last = mm(ps_a[:, 0, q * P:(q + 1) * P], wT[:, t_pack(kt, q):t_pack(kt, q) + P],
                                      v_tok[:, kt * P:(kt + 1) * P], start=kt == 0, stop=kt == q)
                elif kind == "ay":
                    for q in range(ST):
                        last = nc.tensor.transpose(ps_a[:, 0, q * P:(q + 1) * P], o_a[:, q], ident)
                last.then_inc(a_mm, 1)

            def delta(i):
                kind, p, c = DELTA[i]
                if i:
                    pe.wait_ge(d_act, dA[i])
                    pe.wait_ge(d_dve, dD[i])
                    if dP[i]:
                        pe.wait_ge(d_pool, dP[i])
                dst = [ps_d[:, m // 4, (m % 4) * P:(m % 4 + 1) * P] for m in range(8)]
                if kind in ("dq", "dk", "dv"):
                    pe.wait_ge(co_ready, 6 * (p + 1))
                    for m in range(8):
                        last = nc.tensor.transpose(dst[m], conv_o[:, ("dq", "dk", "dv").index(kind), m // 4,
                                                                  (m % 4) * P:(m % 4 + 1) * P], ident)
                elif kind in ("dqT", "dqd", "dkT", "dkb", "T1", "Tc", "dO"):
                    src = {"dqT": Q, "dqd": Q, "dkT": K, "dkb": KB, "T1": TT, "Tc": TT, "dO": O}[kind]
                    for m in range(8):
                        last = nc.tensor.transpose(dst[m], src[:, m], ident)
                elif kind == "dE":
                    for m in range(8):
                        last = mm(dst[m], SCR[:, m], cst[:, C_UPTO, :], start=True, stop=True)
                elif kind in ("dL", "dA", "Za", "Wb", "Wl", "dU", "dW"):
                    a, b = {"dL": (KTT, KBT), "dA": (KTT, QT), "Za": (XT, TN), "Wb": (Z, TT), "Wl": (Z, TT),
                            "dU": (TT, V), "dW": (KB, TT)}[kind]
                    for m in range(8):
                        last = mm(dst[m], a[:, m], b[:, m], start=True, stop=True)
                elif kind == "sa":
                    for hh in range(2):
                        last = mm(ps_d[:, 0, hh * P:(hh + 1) * P], WT[:, 4 * hh + c], state[:, hh], start=True, stop=True)
                elif kind == "sb":
                    for hh in range(2):
                        vn = vnew[:, hh] if c else U[:, 4 * hh]
                        o_ps = ps_d[:, 0, hh * P:(hh + 1) * P]
                        if c:
                            mm(o_ps, QDT[:, 4 * hh + c], state[:, hh], start=True, stop=False)
                        mm(o_ps, AT[:, 4 * hh + c], vn, start=c == 0, stop=True)
                    for hh in range(2):
                        vn = vnew[:, hh] if c else U[:, 4 * hh]
                        last = mm(ps_d[:, 1, hh * P:(hh + 1) * P], K[:, 4 * hh + c], vn, start=True, stop=True)
                last.then_inc(d_mm, 1)

            for n, (main, ev, fi, sa, sd) in enumerate(SLOTS):
                if n in MEM_SLOTS:
                    transpose_rows(ST + MEM_SLOTS.index(n))
                if n == BA_SLOT:
                    beta_and_decay()
                if n == F_SLOT:
                    bias_values()
                if n == G_SLOT:
                    pe.wait_ge(g_ready, 1)
                    pe.wait_ge(in_cst, 16)
                    pe.wait_ge(ones_set, 1)
                    for m, w in enumerate((cst[:, C_UPTO, :], cst[:, C_AFTER, :], ones[:])):
                        last = mm(ps_d[:, 2, m * 32:(m + 1) * 32], w, flat(gdec[:]), start=True, stop=True)
                    last.then_inc(g_mm, 1)
                if main is not None:
                    main_half(*main)
                if sd is not None:
                    delta(sd)
                if sa is not None:
                    attn(sa)

            def sum_over_partitions(u):
                pe.wait_ge(sqs_sum, (u + 1) * (KT - 1))
                for i in range(ST):
                    last = mm(ps_d[:, 2, i:i + 1], ssum[:, i * P:(i + 1) * P], ones[:, 0:1], start=True, stop=True)
                last.then_inc(ss_mm, 1)

            def transpose_f(u, i):
                if i == 3:
                    pe.wait_ge(f_tok, u * ST + 1)
                for m in range(KT):
                    last = nc.tensor.transpose(from_f(i)[:, m // 4, (m % 4) * P:(m % 4 + 1) * P],
                                               f_T[:, m, i * P:(i + 1) * P], ident)
                last.then_inc(tr_f, 1)

            def first_f1_half(c, j):
                t = LATE[L_F1[0]][1] + j
                cols = slice(c * 2 * P, (c + 1) * 2 * P)
                pe.wait_ge(n2l, 2 * c + 2)
                pe.wait_ge(lo_ready, t + 1)
                last = weight_tile(acc[:, j, cols], t, range(KT), lambda k: n2_hi[:, k, cols],
                                   lambda k: n2_lo[:, k, cols], True, True)
                if c == 1:
                    last.then_inc(tile_used, 1)

            for r, (tile, t0, k) in enumerate(LATE):
                bank = acc[:, r % 2]
                if r in (L_F1[0], L_F1[0] + 1):
                    if r == L_F1[0]:
                        first_f1_half(0, 1)
                        first_f1_half(1, 0)
                        first_f1_half(1, 1)
                    continue
                k_wait = None
                if r < 2:
                    pe.wait_ge(acc_free, N_MIX - 1 + r)
                elif r - 2 < N_BR:
                    pe.wait_ge(gated, r - 1)
                elif r - 2 < N_BR + KT:
                    pe.wait_ge(o_ev, r - 1 - N_BR)
                elif LATE[r - 2][0][0] == "f1":
                    pe.wait_ge(relu_ok, LATE[r - 2][0][1] + 1)
                else:
                    pe.wait_ge(f_ev, r - 1 - L_F2[0] if r - 2 < L_F1[1] else r - 1 - L_F2[1] + KT)
                if tile[0] == "br":
                    b = r // KT
                    hi_of, lo_of = (lambda k, b=b: y_hi[b][:, k]), (lambda k, b=b: y_lo[b][:, k])
                    if r % KT == 0:
                        k_wait = lambda k, b=b: pe.wait_ge(yl_ready, KT * b + k + 1)
                elif tile[0] == "out":
                    hi_of, lo_of = (lambda k: mx_hi[:, k]), (lambda k: mx_lo[:, k])
                    if r == N_BR:
                        k_wait = lambda k: pe.wait_ge(mxl_ready, k + 1)
                elif tile[0] == "f1":
                    hi_of, lo_of = (lambda k: n2_hi[:, k]), (lambda k: n2_lo[:, k])
                for j in range(k):
                    t = t0 + j
                    pe.wait_ge(lo_ready, t + 1)
                    if tile[0] == "f2":
                        g = TILES[t][1] // KT
                        o = (g % 2) * KT
                        hi_of, lo_of = (lambda k, o=o: h_hi[:, o + k]), (lambda k, o=o: h_lo[:, o + k])
                        if r in L_F2:
                            k_wait = lambda k, g=g: pe.wait_ge(hl_ok, g * KT + k + 1)
                    last = weight_tile(bank, t, range(KT), hi_of, lo_of, j == 0, j == k - 1, k_wait)
                    if j < k - 1:
                        last.then_inc(tile_used, 1)
                last.then_inc(tile_used, 1)
                if r == N_BR + KT - 1:
                    pe.wait_ge(o_ev, KT)
                    for i in range(3):
                        transpose_f(0, i)
                        if i == 0:
                            sum_over_partitions(0)
                    transpose_f(0, 3)
                    for i in range(ST):
                        if i == 2:
                            first_f1_half(0, 0)
                        pe.wait_ge(n2n, i + 1)
                        pe.wait_ge(f_tok, {0: 2, 1: 3, 2: 4, 3: 2}[i])
                        if i == 3:
                            pe.wait_ge(n2l, 1)
                        for m in range(KT):
                            last = nc.tensor.transpose(back(i)[:, m // 4, (m % 4) * P:(m % 4 + 1) * P],
                                                       rows[:, i % 2, m * P:(m + 1) * P], ident)
                        last.then_inc(tr2, 1)
            pe.wait_ge(f_ev, 2 * KT)
            for i in range(ST):
                transpose_f(1, i)
                if i == 0:
                    sum_over_partitions(1)


def _consts():
    i = np.arange(P)
    c = np.zeros((P, NCONST, P), np.float32)
    c[:, C_ID] = np.eye(P)
    c[:, C_UPTO] = i[:, None] <= i[None, :]
    c[:, C_AFTER] = i[:, None] > i[None, :]
    for n in range(NM):
        b = 2 ** n
        c[:, C_MASK0 + n] = ((i[None, :] // (2 * b) == i[:, None] // (2 * b)) & (i[None, :] // b % 2 == 1)
                             & (i[:, None] // b % 2 == 0))
    c[:, C_CAUS] = np.where(i[None, :] > i[:, None], NEG, 0.0)
    return c


def _onehot():
    dist = np.maximum(2 * P - 1 - np.arange(SPAN), 0)
    nf = np.maximum(dist, 1).astype(np.float32)
    large = MAX_EXACT + (np.log(nf / np.float32(MAX_EXACT)) / np.float32(math.log(MAX_DIST / MAX_EXACT))
                         * np.float32(BUCKETS - MAX_EXACT)).astype(np.int32)
    bucket = np.where(dist < MAX_EXACT, dist, np.minimum(large, BUCKETS - 1))
    o = np.zeros((BUCKETS, SPAN), np.float32)
    o[bucket, np.arange(SPAN)] = 1.0
    o[BUCKETS - 1] -= 1.0
    return o


def kernel(**inputs):
    import concourse.bacc as bacc
    from concourse.bass_utils import run_bass_kernel_spmd

    a = {k: np.asarray(v) for k, v in inputs.items()}
    w_in, w_kv, w_br = a["w_in"][0], a["w_mem_kv"][0], a["w_branch"][0]
    w_out, w1, w2 = a["w_out"][0], a["w_ff1"][0], a["w_ff2"][0]

    def block_of(kind, j):
        c = slice(j * P, (j + 1) * P)
        if kind == "mk":
            return w_kv[:, c]
        if kind == "mv":
            return w_kv[:, D + j * P:D + (j + 1) * P]
        if kind == "br":
            return w_br[j // KT][:, j % KT * P:(j % KT + 1) * P]
        if kind == "out":
            return w_out[:, c]
        if kind == "f1":
            return w1[:, c]
        if kind == "f2":
            return w2[j // KT * D:(j // KT + 1) * D, j % KT * P:(j % KT + 1) * P]
        return w_in[:, COL[kind] + j * P:COL[kind] + (j + 1) * P]

    tiles = plan_tiles()[0]
    weights = np.empty((len(tiles), P, KT, P), np.float32)
    for n, (kind, j) in enumerate(tiles):
        weights[n] = block_of(kind, j).reshape(KT, P, P).transpose(1, 0, 2)

    params = np.empty((P, NPAR), np.float32)
    for c, name in ((PC_PRE, "ln_mix_pre"), (PC_MEM, "mem_norm_g"), (PC_FF, "ln_ff_pre")):
        params[:, c:c + KT] = a[name][0].reshape(KT, P).T
    params[:, PC_SUB] = a["da_subln_g"][0]
    params[:, PC_DNG] = a["dn_norm_g"][0]
    params[:, PC_CONV:PC_ALOG] = a["conv_w"][0].reshape(4, 24, P).transpose(2, 1, 0).reshape(P, 96)
    params[:, PC_ALOG:PC_ALOG + HB] = a["dn_a_log"][0][None]
    params[:, PC_DTB:PC_DTB + HB] = a["dn_dt_bias"][0][None]
    params[:, PC_LAM:] = a["da_lambda"][0].reshape(1, 4 * DA)
    post_g = np.empty((P, 3, D), np.float32)
    for n, name in enumerate(("ln_mix_post", "ln_ff_pre", "ln_ff_post")):
        post_g[:, n] = a[name][0][None]
    w_ba = w_in[:, COL["ba"]:COL["ba"] + 2 * HB].reshape(KT, P, 2 * HB).transpose(1, 0, 2)
    arrays = {
        "weights": weights, "x": a["x"][0], "mem": a["mem"][0], "w_ba": w_ba, "params": params,
        "consts": _consts(), "onehot": _onehot(), "relb": a["rel_bias"], "post_g": post_g,
    }
    arrays = {k: np.ascontiguousarray(v) for k, v in arrays.items()}
    nc = bacc.Bacc("TRN2", target_bir_lowering=False, num_devices=1)
    ins = [nc.dram_tensor(k, v.shape, F32, kind="ExternalInput").ap() for k, v in arrays.items()]
    y_dram = nc.dram_tensor("y_scratch", (3, P, KT, S), F32, kind="Internal").ap()
    gate_dram = nc.dram_tensor("gate_scratch", (3 * KT, P, S), F32, kind="Internal").ap()
    f_dram = nc.dram_tensor("bias_scratch", (HA, SPAN), F32, kind="Internal").ap()
    frep_dram = nc.dram_tensor("bias_rows", (HA, P, SPAN), F32, kind="Internal").ap()
    out = nc.dram_tensor("out", (S, D), F32, kind="ExternalOutput").ap()
    build(nc, *ins, y_dram, gate_dram, f_dram, frep_dram, out)
    r = run_bass_kernel_spmd(nc, [arrays], core_ids=[0])
    return r.results[0]["out"].reshape(1, S, D)
```

```python
import math
from contextlib import ExitStack

import numpy as np

import concourse.bass as bass
from concourse import mybir

F32 = mybir.dt.float32
F32R = mybir.dt.float32r
I32 = mybir.dt.int32
ALU = mybir.AluOpType
ACT = mybir.ActivationFunctionType
AX_X = mybir.AxisListType.X

P = 128
D = 1024
S = 512
KT = D // P
ST = S // P
MEM = 256
MT = MEM // P
DFF = 4 * D
HA, DA = 8, 64
HB = 8
HC = 4
EPS = 1e-6
LAM_INIT = 0.8 - 0.6 * math.exp(-0.3 * 0)
BUCKETS, MAX_EXACT, MAX_DIST = 32, 16, 128
SPAN = 3 * P
NEG = -1e30
NM = 7

COL = {"aq": 0, "ak": D, "av": 2 * D, "dq": 3 * D, "dk": 4 * D, "dv": 5 * D, "dz": 6 * D,
       "ba": 7 * D, "cq": 7 * D + 2 * HB, "gate": 8 * D + 2 * HB}

RAW, SPL = 3, 3

C_ID, C_UPTO, C_AFTER, C_MASK0, C_CAUS = 0, 1, 2, 3, 3 + NM
NCONST = 4 + NM
PC_PRE, PC_MEM, PC_FF = 0, 8, 16
PC_SUB, PC_DNG = 24, 25
PC_CONV = 26
PC_ALOG = PC_CONV + 96
PC_DTB = PC_ALOG + HB
PC_LAM = PC_DTB + HB
PC_POST = PC_LAM + 4 * DA
NPAR = PC_POST + 2 * KT

PARTS = {"mv": "A", "cs": "AD", "ct": "A", "cv": "A", "av": "A", "as0": "A", "as1": "AD", "at": "A",
         "ap": "AD", "ay": "A",
         "dq": "AD", "dk": "ADP", "dv": "D", "dE": "A", "dqT": "AD", "dqd": "A", "dkT": "AP",
         "dkb": "AP", "dL": "DP", "dA": "DP", "T1": "AP", "Za": "AP", "Wb": "D", "Wl": "D", "Tc": "AP",
         "dU": "A", "dW": "A", "sa": "D", "sb": "AD", "dO": "D"}
COVER = {"cs": 3, "cv": 2, "as0": 3, "as1": 4, "ap": 2, "dq": 2, "dk": 3, "dO": 2, "sb_last": 3, "dA": 2}
EXP_LAG, SCALE_LAG, NORM_LAG = 1, 2, 0

ORDER = [("conv", 0), ("mem", 0), ("cq", 0), ("z", 0), ("conv", 1), ("cq", 1), ("cq", 2), ("cq", 3), ("z", 1),
         ("head", 0), ("head", 1), ("conv", 2), ("head", 2), ("head", 3), ("z", 2), ("head", 4), ("conv", 3),
         ("head", 5), ("head", 6), ("z", 3), ("head", 7)]


def cover(step):
    last_state = step[0] == "sb" and step[2] == ST - 1
    return COVER.get("sb_last" if last_state else step[0], 1)


def attn_steps():
    out = [("mv", 0), ("mv", 1)]
    for h in range(HC):
        out += [("cs", h), ("ct", h), ("cv", h)]
    for h in range(HA):
        out += [("av", h), ("as0", h), ("as1", h), ("at", h), ("ap", h), ("ay", h)]
    return out


def delta_steps():
    out = []
    for p in range(HB // 2):
        out += [(k, p, 0) for k in ("dq", "dk", "dv", "dE", "dqT", "dqd", "dkT", "dkb", "dL", "dA", "T1")]
        for lv in range(1, NM):
            out += [("Za", p, lv), ("Wb" if lv < NM - 1 else "Wl", p, lv)]
            if lv < NM - 1:
                out.append(("Tc", p, lv))
        out += [("dU", p, 0), ("dW", p, 0)]
        for c in range(ST):
            if c:
                out.append(("sa", p, c))
            out.append(("sb", p, c))
        out.append(("dO", p, 0))
    return out


def plan_mixing():
    attn, delta = attn_steps(), delta_steps()
    def group(kind, n):
        return {"mem": [("mk", j) for j in range(KT)] + [("mv", j) for j in range(KT)],
                "conv": [(k, 2 * n + i) for k in ("dq", "dk", "dv") for i in range(2)],
                "z": [("dz", 2 * n + i) for i in range(2)],
                "cq": [("cq", 2 * n + i) for i in range(2)],
                "head": [(k, n) for k in ("aq", "ak", "av")]}[kind]

    groups = [group(*g) for g in ORDER]
    gates = [("gate", i * KT + m) for i in (2, 0, 1) for m in range(KT)]
    tiles, slots = [], []
    done = {}
    evac = {}
    need_free = {}
    for p in range(1, HB // 2):
        for k in ("dq", "dk", "dv"):
            for i in range(2):
                need_free[(k, 2 * p + i)] = ("dv", p - 1, 0)
        for i in range(2):
            need_free[("dz", 2 * p + i)] = ("dO", p - 1, 0)
    for j in range(2 * HC):
        need_free[("cq", j)] = ("mv", 1) if j < 4 else ("cs", j // 2 - 2)
    for h in range(HA):
        for k in ("aq", "ak", "av"):
            need_free[(k, h)] = ("cv", HC - 1) if h < 2 else ("as1", h - 2)
    need_tile = {}
    need_tile[("mv", 0)] = need_tile[("mv", 1)] = ("mv", KT - 1)
    for h in range(HC):
        need_tile[("cs", h)] = ("cq", 2 * h + 1)
    for h in range(HA):
        need_tile[("av", h)] = ("av", h)
    for p in range(HB // 2):
        need_tile[("dq", p, 0)] = ("dv", 2 * p + 1)
        need_tile[("dO", p, 0)] = ("dz", 2 * p + 1)
    ai = di = 0
    a_next = d_next = 0
    finish = {}
    todo = list(groups)
    now = []
    half = 0
    slot = 0
    while todo or gates or now or ai < len(attn) or di < len(delta) or finish.get(slot):
        if not now:
            if todo and all(need_free.get(t) is None or need_free[t] in done for t in todo[0][:1]):
                now = list(todo.pop(0))
            elif gates:
                now = [gates.pop(0)]
        main = ev = None
        if now:
            short = now[0][0] in ("mk", "mv")
            main = (len(tiles), None if short else half)
            if half == 1 or short:
                t = now.pop(0)
                tiles.append(t)
                ev = len(tiles) - 1
                evac[t] = slot
                if t[0] in ("dq", "dk", "dv", "dz"):
                    finish[slot + 1] = ev
                    evac[t] = slot + 1
            half = 0 if short else half ^ 1
        sa = sd = None
        if ai < len(attn) and slot >= a_next:
            t = need_tile.get(attn[ai])
            if t is None or evac.get(t, slot + 9) < slot:
                sa = ai
                done[attn[ai]] = slot
                a_next = slot + cover(attn[ai])
                ai += 1
        if di < len(delta) and slot >= d_next:
            t = need_tile.get(delta[di])
            if t is None or evac.get(t, slot + 9) < slot:
                sd = di
                done[delta[di]] = slot
                d_next = slot + cover(delta[di])
                di += 1
        slots.append((main, ev, finish.get(slot), sa, sd))
        slot += 1
    return tiles, slots, need_free


def plan_tiles():
    tiles, slots, need_free = plan_mixing()
    n_mix = len(tiles)
    tiles = list(tiles)
    for i in (2, 0, 1):
        tiles += [("br", i * KT + m) for m in range(KT)]
    tiles += [("out", m) for m in range(KT)]
    for half in range(2):
        tiles += [("f1", half * 16 + f) for f in range(16)]
        tiles += [("f2", (2 * half + g) * KT + m) for m in range(KT) for g in range(2)]
    return tiles, n_mix, slots, need_free


def counts(steps, part):
    out = [0]
    for s in steps:
        last_levels = part == "P" and s[0] == "Za" and s[2] + 2 >= NM
        out.append(out[-1] + (part in PARTS[s[0]] and not last_levels))
    return out


def kinds_before(steps, names):
    out = [0]
    for s in steps:
        out.append(out[-1] + (s[0] in names))
    return out


def view(ap, dims, offset=0):
    return bass.AP(tensor=ap.tensor, offset=ap.offset + offset, ap=[list(ap.ap[0])] + [list(d) for d in dims])


def along(ap, n):
    return view(ap, [list(ap.ap[1]), [0, n]])


def over(ap, m):
    return view(ap, [[0, m], list(ap.ap[1])])


def halves(ap, lv, second):
    b = 2 ** lv
    return view(ap, [list(d) for d in ap.ap[1:-1]] + [[2 * b, P // (2 * b)], [1, b]], second * b)


def flat(ap3):
    return ap3.rearrange("p a b -> p (a b)")


def build(nc, weights, x, mem, w_ba, params, consts, onehot, relb, post_g, y_dram, gate_dram, f_dram, frep_dram, out):
    TILES, N_MIX, SLOTS, NEED_FREE = plan_tiles()
    NT = len(TILES)
    ATTN, DELTA = attn_steps(), delta_steps()
    a_idx = {s: i for i, s in enumerate(ATTN)}
    d_idx = {s: i for i, s in enumerate(DELTA)}
    aA, aD = counts(ATTN, "A"), counts(ATTN, "D")
    dA, dD, dP = counts(DELTA, "A"), counts(DELTA, "D"), counts(DELTA, "P")
    n_max = kinds_before(ATTN, ("cs", "as0", "as1"))
    n_spill = kinds_before(ATTN, ("cv", "ay"))
    conv_tiles = [t for t in range(N_MIX) if TILES[t][0] in ("dq", "dk", "dv")]
    z_tiles = [t for t in range(N_MIX) if TILES[t][0] == "dz"]
    gate_tiles = [t for t in range(N_MIX) if TILES[t][0] == "gate"]
    n_conv = {t: i for i, t in enumerate(conv_tiles)}
    n_z = {t: i for i, t in enumerate(z_tiles)}
    n_gate = {t: i for i, t in enumerate(gate_tiles)}
    SC_A = DA ** -0.5
    SC_C = (D // HC) ** -0.5

    with ExitStack() as ctx:
        def sem(name):
            return ctx.enter_context(nc.semaphore(name))

        def sb_in(c):
            return lambda name, shape, dt=F32: c.enter_context(nc.sbuf_tensor(name, shape, dt))

        sb = sb_in(ctx)
        acc = ctx.enter_context(nc.psum_tensor("acc", [P, 2, 512], F32))
        ps_a = ctx.enter_context(nc.psum_tensor("ps_a", [P, 3, 512], F32))
        ps_d = ctx.enter_context(nc.psum_tensor("ps_d", [P, 3, 512], F32))
        side = [ps_a, ps_d]

        w_raw = sb("w_raw", [P, RAW, KT, P])
        w_hi = sb("w_hi", [P, SPL, KT, P], F32R)
        w_lo = sb("w_lo", [P, SPL, KT, P], F32R)
        cst = sb("cst", [P, NCONST, P])
        par = sb("par", [P, NPAR])
        ones = sb("ones", [P, P])
        sml = sb("sml", [P, 160])
        smd = sb("smd", [P, 96])
        ident = cst[:, C_ID, :]

        mix = ExitStack()
        sm = sb_in(mix)
        n_hi = sm("n_hi", [P, KT, S], F32R)
        n_lo = sm("n_lo", [P, KT, S], F32R)
        strip = sm("strip", [P, HA, 2 * P])
        beta = sm("beta", [P, HB, ST])
        hbeta = sm("hbeta", [P, HB, ST])
        gdec = sm("gdec", [P, HB, ST])
        e_in = sm("e_in", [P, HB, ST])
        e_tail = sm("e_tail", [P, HB, ST])
        e_all = sm("e_all", [P, HB, ST])
        conv_x = sm("conv_x", [P, 2, S + 4])
        conv_y = sm("conv_y", [P, 2, S])
        conv_o = sm("conv_o", [P, 3, 2, S])
        zs = sm("zs", [P, 2, S])
        z_t = sm("z_t", [P, S])
        y_st = sm("y_st", [P, 2, S])
        gate_st = sm("gate_st", [P, S])
        state = sm("state", [P, 2, P])
        vnew = sm("vnew", [P, 2, P])

        first = ExitStack()
        sf = sb_in(first)
        x_tok = sf("x_tok", [P, ST, D])
        m_tok = sf("m_tok", [P, MT, D])
        full = sf("full", [P, 4, KT, P])
        ba_T = sf("ba_T", [P, S])
        ba = sf("ba", [P, 6, HB, ST])
        first.close()
        dl = ExitStack()
        sd_ = sb_in(dl)
        names = ["Q", "SCR", "K", "KB", "V", "QT", "QDT", "KTT", "KBT", "ET", "LT", "AT", "TT"]
        B = {n: sd_("d_" + n, [P, 8, P]) for n in names}
        Q, SCR, K, KB, V, QT, QDT, KTT, KBT, ET, LT, AT, TT = (B[n] for n in names)
        TN, Z, U, WT, O = QT, KTT, Q, SCR, LT
        XT = (SCR, KBT)

        c1 = ExitStack()
        sc_ = sb_in(c1)
        mk_T = sc_("mk_T", [P, KT, MEM])
        mv_tok = sc_("mv_tok", [P, MT, D])
        p_c = sc_("p_c", [P, ST, MEM])
        pT_c = sc_("pT_c", [P, MT, S])
        c1.close()
        c1 = ExitStack()
        sc_ = sb_in(c1)
        sc_("mk_T_place", [P, KT, MEM])
        m_hi = sc_("m_hi", [P, KT, MEM], F32R)
        m_lo = sc_("m_lo", [P, KT, MEM], F32R)
        c1.close()
        c2 = ExitStack()
        sa_ = sb_in(c2)
        p_a = sa_("p_a", [P, 2, 10 * P])
        wT = sa_("wT", [P, 10 * P])
        v_tok = sa_("v_tok", [P, S])
        o_a = sa_("o_a", [P, ST, P])
        sa_("rest_of_area", [P, 1280])
        c3 = ExitStack()
        s3 = sb_in(c3)
        mv_T = s3("mv_T", [P, KT, MEM])
        w_ba_sb = s3("w_ba_sb", [P, KT, 2 * HB])
        wb_hi = s3("wb_hi", [P, KT, 2 * HB], F32R)
        wb_lo = s3("wb_lo", [P, KT, 2 * HB], F32R)
        c3.close()
        c3 = ExitStack()
        s3 = sb_in(c3)
        cq_T = s3("cq_T", [P, 2, 2, S])
        c3.close()
        c3 = ExitStack()
        s3 = sb_in(c3)
        qkv_T = s3("qkv_T", [P, 2, 3, S])
        onehot_sb = strip[0:BUCKETS, 0:2, :].rearrange("p a b -> p (a b)")[:, 0:SPAN]
        c3.close()
        c2.close()
        c2 = ExitStack()
        sa_ = sb_in(c2)
        y0_hi = sa_("y0_hi", [P, KT, S], F32R)
        y0_lo = sa_("y0_lo", [P, KT, S], F32R)
        g_in = sa_("g_in", [P, 2, S])
        c2.close()
        dl.close()
        mix.close()

        late = ExitStack()
        sl = sb_in(late)
        mx_hi = sl("mx_hi", [P, KT, S], F32R)
        mx_lo = sl("mx_lo", [P, KT, S], F32R)
        y_raw = sl("y_raw", [P, 2, S])
        mix_acc = sl("mix_acc", [P, KT, S])
        y1_hi = sl("y1_hi", [P, KT, S], F32R)
        y1_lo = sl("y1_lo", [P, KT, S], F32R)
        y_hi, y_lo = (y0_hi, y1_hi, y0_hi), (y0_lo, y1_lo, y0_lo)
        g_tmp = sl("g_tmp", [P, S])
        late.close()
        late = ExitStack()
        sl = sb_in(late)
        h_lo = sl("h_lo", [P, 2 * KT, S], F32R)
        h1 = sl("h1", [P, ST, D])
        post = sl("post", [P, D])
        f_T = sl("f_T", [P, KT, S])
        part = ExitStack()
        rows = sb_in(part)("rows", [P, 2, D])
        part.close()
        relu = sl("relu", [P, 2, S])
        sq = sl("sq", [P, 2, S])
        ssum = sl("ssum", [P, S])
        sqs = sl("sqs", [P, 2, S])
        n2_hi = sl("n2_hi", [P, KT, S], F32R)
        n2_lo = sl("n2_lo", [P, KT, S], F32R)
        part = ExitStack()
        junk = sb_in(part)("junk", [P, D])
        part.close()
        h_hi = sl("h_hi", [P, 2 * KT, S], F32R)
        late.close()

        ld = [sem(f"ld{i}") for i in range(RAW)]
        hi_ready = sem("hi_ready")
        lo_ready = sem("lo_ready")
        tile_used = sem("tile_used")
        acc_free = sem("acc_free")
        in_par, in_mem, in_oh, in_ba, in_relb, in_id, in_cst = (
            sem(n) for n in ("in_par", "in_mem", "in_oh", "in_ba", "in_relb", "in_id", "in_cst"))
        in_x = [sem(f"in_x{i}") for i in range(ST)]
        ones_set = sem("ones_set")
        pad_set = sem("pad_set")
        vch = sem("vch")
        ach = sem("ach")
        pch = sem("pch")
        su_sq = sem("su_sq")
        su_rms = sem("su_rms")
        su_norm = sem("su_norm")
        su_norm2 = sem("su_norm2")
        su_lo2 = sem("su_lo2")
        su_tr = sem("su_tr")
        su_full = sem("su_full")
        su_hi = sem("su_hi")
        su_lo = sem("su_lo")
        ba_split = sem("ba_split")
        ba_rows = sem("ba_rows")
        ba_sb = sem("ba_sb")
        ba_mm = sem("ba_mm")
        ba_act = sem("ba_act")
        ba_dve = sem("ba_dve")
        g_ready = sem("g_ready")
        g_mm = sem("g_mm")
        g_exp = sem("g_exp")
        f_mm = sem("f_mm")
        f_sb = sem("f_sb")
        f_out = sem("f_out")
        f_rep = sem("f_rep")
        strip_in = sem("strip_in")
        strip_ok = sem("strip_ok")
        lam_sum = sem("lam_sum")
        lam_exp = sem("lam_exp")
        a_mm = sem("a_mm")
        a_act = sem("a_act")
        a_dve = sem("a_dve")
        a_max = sem("a_max")
        d_mm = sem("d_mm")
        d_act = sem("d_act")
        d_dve = sem("d_dve")
        d_pool = sem("d_pool")
        at_ready = sem("at_ready")
        cx_ready = sem("cx_ready")
        cy_ready = sem("cy_ready")
        ct_ready = sem("ct_ready")
        co_ready = sem("co_ready")
        zt_ready = sem("zt_ready")
        z_ready = sem("z_ready")
        y_out = sem("y_out")
        yb_out = sem("yb_out")
        gs_ready = sem("gs_ready")
        g_out = sem("g_out")
        y_pre = [sem(f"y_pre{i}") for i in range(2)]
        y_in = [sem(f"y_in{i}") for i in range(2)]
        yh_ready = sem("yh_ready")
        yl_ready = sem("yl_ready")
        gin = [sem(f"gin{i}") for i in range(2)]
        gated = sem("gated")
        merged = sem("merged")
        mxh_ready = sem("mxh_ready")
        mxl_ready = sem("mxl_ready")
        o_ev = sem("o_ev")
        sqs_ok = sem("sqs_ok")
        sqs_sum = sem("sqs_sum")
        out_half = sem("out_half")
        ss_mm = sem("ss_mm")
        tr_f = sem("tr_f")
        h1_ok = sem("h1_ok")
        fg_ok = sem("fg_ok")
        hg_ok = sem("hg_ok")
        ss2 = sem("ss2")
        rs2 = sem("rs2")
        n2n = sem("n2n")
        tr2 = sem("tr2")
        n2h = sem("n2h")
        n2l = sem("n2l")
        in_h1, in_post = sem("in_h1"), sem("in_post")
        relu_ok = sem("relu_ok")
        sq_ok = sem("sq_ok")
        hh_ok = sem("hh_ok")
        hl_ok = sem("hl_ok")
        f_ev = sem("f_ev")
        o_done = sem("o_done")

        block = ctx.enter_context(nc.Block())

        LAMS, LAME, NLAM = smd[:, 2:4], smd[:, 4:6], smd[:, 6:7]
        relb_sb = sml[0:BUCKETS, 32:32 + HA]
        ealog = sml[:, 64:64 + HB]
        f_row = qkv_T[0:HA, 1, 2, 0:SPAN]
        p_a_scr = flat(conv_o[:, 0])
        lam_prod = z_t[:, 0:2 * DA].rearrange("p (a d) -> p a d", a=2)
        BR = (2, 0, 1)
        N_BR = 3 * KT
        A_END = max(n for n, s in enumerate(SLOTS) if s[3] is not None)

        def preload_at(n):
            k = n - A_END - 2
            return range(max(k, 0), KT) if n == len(SLOTS) - 1 else range(k, k + 1) if 0 <= k < KT else ()

        G_SLOT = 11
        BIAS_SLOTS = [9, 14, 20]
        GSUB, GDN = smd[:, 7:8], smd[:, 8:9]
        mxa, nba = smd[:, 16:20], smd[:, 20:24]
        sma, rca = smd[:, 24:32], smd[:, 32:40]
        ssa, rsa, tma = smd[:, 40:44], smd[:, 44:48], smd[:, 48:52]
        ssd, rsd, tmd = smd[:, 56:64], smd[:, 64:72], smd[:, 72:80]

        N_SU = ST + MT
        POOL_ROWS = (0, 2, 4, 5)
        MEM_SLOTS = [3, 4]
        BA_SLOT, F_SLOT = 4, 6
        bank_of = {3: 0, 2: 512 + 128, 1: 1024 + 256, 0: 512}
        pack_of = {0: 0, 1: P, 2: 3 * P, 3: 6 * P}

        def t_bank(kt, q):
            return {0: q * P, 1: 512 + q * P, 2: 1024 + q * P, 3: 512}[kt]

        def t_pack(kt, q):
            return t_bank(kt, q) if kt != 2 else 1024 + (q - 2) * P

        LATE = []
        t = N_MIX
        while t < NT:
            k = 2 if TILES[t][0] == "f2" else 1
            LATE.append((TILES[t], t, k))
            t += k
        L_F1 = [32, 56]
        L_F2 = [48, 72]

        def tiles_of(n):
            return LATE[n][1] if n < len(LATE) else NT

        EXP_KINDS = ("cs", "as0", "as1")

        def lagged(n, lag, kinds):
            i = SLOTS[n - lag][3] if n >= lag else None
            return i if i is not None and ATTN[i][0] in kinds else None

        def compact(lv):
            b = 2 ** lv
            return view(ps_d[:, 0], [[P // 2, 8], [b, P // (2 * b)], [1, b]])

        def row_parts(j):
            if j < ST:
                return n_hi[:, :, j * P:(j + 1) * P], n_lo[:, :, j * P:(j + 1) * P]
            return m_hi[:, :, (j - ST) * P:(j - ST + 1) * P], m_lo[:, :, (j - ST) * P:(j - ST + 1) * P]

        H = 3
        HALF = (slice(0, S // 2), slice(S // 2, S))
        OUT_PARTS = ([(m, slice(0, S)) for m in range(KT - H)] + [(m, HALF[0]) for m in range(KT - H, KT)]
                     + [(m, HALF[1]) for m in range(KT - H, KT)])
        sums_before = [sum(0 < m < KT - 1 for m, _ in OUT_PARTS[:e]) for e in range(len(OUT_PARTS) + 1)]
        SUMS = (0, sums_before[-1])

        def result_bank(r):
            return ps_a[:, 2] if r in (N_BR + KT - 1, L_F1[0] + H - 1) else acc[:, r % 2]

        trio = [ps_a, ps_d, acc]
        from_f, back = (lambda i: trio[i % 3]), (lambda i: trio[(i + 1) % 3])

        def two(ps):
            return flat(ps[:])[:, 0:1024]

        def blocks(ap):
            return ap.rearrange("p (a b) -> p a b", b=P)

        @block.sync
        def _(sp):
            for i in range(ST):
                sp.dma_start(x_tok[:, i], x[i * P:(i + 1) * P]).then_inc(in_x[i], 16)
                if i == 1:
                    sp.dma_start(cst[:, C_ID], consts[:, C_ID]).then_inc(in_id, 16)
            sp.dma_start(par[:], params).then_inc(in_par, 16)

            def load(t):
                if t < NT:
                    if t >= RAW:
                        sp.wait_ge(lo_ready, t - RAW + 1)
                    sp.dma_start(w_raw[:, t % RAW], weights[t]).then_inc(ld[t % RAW], 16)

            load(0)
            sp.dma_start(w_ba_sb[:], w_ba).then_inc(in_ba, 16)
            load(1)
            sp.dma_start(m_tok[:], mem.rearrange("(t p) d -> p t d", p=P)).then_inc(in_mem, 16)
            load(2)
            sp.dma_start(cst[:, C_ID + 1:], consts[:, C_ID + 1:]).then_inc(in_cst, 16)
            sp.dma_start(onehot_sb, onehot).then_inc(in_oh, 16)
            sp.dma_start(relb_sb, relb).then_inc(in_relb, 16)
            def bias(step):
                if step == 0:
                    sp.wait_ge(f_sb, 1)
                    sp.dma_start(f_dram, f_row).then_inc(f_out, 16)
                elif step == 1:
                    sp.wait_ge(f_out, 16)
                    sp.dma_start(frep_dram, bass.AP(tensor=f_dram.tensor, offset=f_dram.offset,
                                                    ap=[[SPAN, HA], [0, P], [1, SPAN]])).then_inc(f_rep, 16)
                elif step == 2:
                    sp.wait_ge(f_rep, 16)
                    sp.dma_start(strip[:], bass.AP(tensor=frep_dram.tensor, offset=frep_dram.offset + P - 1,
                                                   ap=[[SPAN - 1, P], [P * SPAN, HA], [1, 2 * P]])).then_inc(strip_in, 16)

            def load_gate(r):
                if r >= 2:
                    sp.wait_ge(gated, r - 1)
                else:
                    sp.wait_ge(g_out, 16 * KT)
                    sp.wait_ge(a_mm, len(ATTN))
                sp.dma_start(g_in[:, r % 2], gate_dram[LATE[r][0][1]]).then_inc(gin[r % 2], 16)

            for slot, (main, ev, fi, sa, sd) in enumerate(SLOTS):
                if slot in BIAS_SLOTS:
                    bias(BIAS_SLOTS.index(slot))
                if ev is not None:
                    load(ev + RAW)
                    if ev == N_MIX - 1:
                        load(ev + RAW + 1)
                    if TILES[ev][0] == "gate":
                        n = n_gate[ev]
                        sp.wait_ge(gs_ready, n + 1)
                        sp.dma_start(gate_dram[TILES[ev][1]], gate_st[:]).then_inc(g_out, 16)
                if sa is not None and ATTN[sa][0] in ("cv", "ay"):
                    kind, h = ATTN[sa]
                    sp.wait_ge(a_act, aA[sa + 1])
                    if kind == "cv":
                        sp.dma_start(y_dram[2, :, 2 * h:2 * h + 2], y_st[:]).then_inc(y_out, 16)
                    else:
                        sp.dma_start(y_dram[0, :, h], y_st[:, 0]).then_inc(y_out, 16)
                if sd is not None and DELTA[sd][0] == "dO":
                    p = DELTA[sd][1]
                    sp.wait_ge(d_dve, dD[sd + 1])
                    sp.dma_start(y_dram[1, :, 2 * p:2 * p + 2],
                                 flat(ET[:]).rearrange("p (a b) -> p a b", a=2)).then_inc(yb_out, 16)
                for kk in preload_at(slot):
                    if kk == 0:
                        sp.wait_ge(y_out, 16 * n_spill[-1])
                    if kk >= 2:
                        sp.wait_ge(yl_ready, kk - 1)
                    sp.dma_start(y_st[:, kk % 2], y_dram[BR[0], :, kk]).then_inc(y_pre[kk % 2], 16)
                    if kk >= KT - 2:
                        load_gate(kk - KT + 2)
            for r, (tile, t0, k) in enumerate(LATE):
                for j in range(k):
                    load(t0 + j + RAW + 1)
                if r == 0:
                    sp.wait_ge(yb_out, 16 * (HB // 2))
                    sp.wait_ge(g_out, 16 * len(gate_tiles))
                    sp.wait_ge(tile_used, N_MIX)
                    sp.wait_ge(acc_free, N_MIX)
                if r < N_BR:
                    b, m = r // KT, r % KT
                    if r < 2 * KT:
                        sp.wait_ge(yl_ready, KT + max(r - 1, 0))
                        sp.dma_start(y_raw[:, r % 2], y_dram[BR[b + 1], :, m]).then_inc(y_in[r % 2], 16)
                    if r >= 2:
                        load_gate(r)
                if r == N_BR + 2:
                    sp.wait_ge(tile_used, tiles_of(N_BR))
                    sp.wait_ge(mxl_ready, KT)
                    sp.dma_start(post[:], post_g).then_inc(in_post, 16)
                    sp.dma_start(h1[:], x.rearrange("(t p) d -> p t d", p=P)).then_inc(in_h1, 16)
            for i in range(ST):
                sp.wait_ge(h1_ok, ST + i + 1)
                sp.dma_start(out[i * P:(i + 1) * P, :], h1[:, i]).then_inc(o_done, 16)
            sp.wait_ge(o_done, 16 * ST)

        @block.gpsimd
        def _(pool):
            def split_lo(t):
                if t < NT:
                    pool.wait_ge(hi_ready, t + 1)
                    if t >= SPL:
                        pool.wait_ge(tile_used, t - SPL + 1)
                    nc.gpsimd.tensor_tensor(w_lo[:, t % SPL], w_raw[:, t % RAW],
                                            w_hi[:, t % SPL].bitcast(F32), ALU.subtract).then_inc(lo_ready, 1)

            nc.gpsimd.memset(ones[:], 1.0).then_inc(ones_set, 1)
            nc.gpsimd.memset(conv_x[:, :, 0:3], 0.0).then_inc(pad_set, 1)
            for j in POOL_ROWS:
                if j <= ST:
                    split_lo(j // 2)
                pool.wait_ge(su_hi, j + 1)
                hi, lo = row_parts(j)
                nc.gpsimd.tensor_tensor(lo, full[:, j % 4], hi.bitcast(F32), ALU.subtract).then_inc(su_lo, 1)

            def level_operand(lv):
                return nc.gpsimd.tensor_tensor(XT[lv % 2][:], LT[:], over(cst[:, C_MASK0 + lv, :], 8), ALU.mult)

            def delta(i):
                kind, p, lv = DELTA[i]
                if "P" not in PARTS[kind]:
                    return
                if kind == "Za" and lv + 2 >= NM:
                    return
                pool.wait_ge(d_mm, i + 1)
                heads = slice(2 * p, 2 * p + 2)
                if kind == "dk":
                    pool.wait_ge(g_exp, 1)
                    if p:
                        pool.wait_ge(yb_out, 16 * p)
                    last = nc.gpsimd.tensor_tensor(ET[:], over(cst[:, C_AFTER, :], 8),
                                                   along(flat(gdec[:, heads]), P), ALU.mult)
                elif kind == "dkT":
                    last = nc.gpsimd.tensor_tensor(K[:], K[:], along(flat(e_tail[:, heads]), P), ALU.mult)
                elif kind == "dkb":
                    last = nc.gpsimd.tensor_tensor(KB[:], KB[:], along(flat(e_in[:, heads]), P), ALU.mult)
                elif kind == "dL":
                    pool.wait_ge(d_dve, dD[i + 1])
                    last = level_operand(1)
                elif kind == "dA":
                    pool.wait_ge(at_ready, p + 1)
                    last = nc.gpsimd.tensor_tensor(AT[:], AT[:], over(cst[:, C_UPTO, :], 8), ALU.mult)
                elif kind in ("T1", "Tc"):
                    last = nc.gpsimd.memset(halves(Z[:], lv + 1, 1), 0.0)
                    if kind == "T1":
                        last = level_operand(2)
                elif kind == "Za":
                    last = level_operand(lv + 2)
                last.then_inc(d_pool, 1)

            def y_lo_tile(b, kk):
                pool.wait_ge(yh_ready, b * KT + kk + 1)
                src = y_raw[:, kk % 2] if b else y_st[:, kk % 2]
                nc.gpsimd.tensor_tensor(y_lo[b][:, kk], src, y_hi[b][:, kk].bitcast(F32),
                                        ALU.subtract).then_inc(yl_ready, 1)

            for slot, (main, ev, fi, sa, sd) in enumerate(SLOTS):
                if ev is not None:
                    split_lo(ev + SPL)
                    if TILES[ev][0] == "gate":
                        n = n_gate[ev]
                        pool.wait_ge(acc_free, ev + 1)
                        nc.gpsimd.tensor_scalar(gate_st[:], gate_st[:], 0.5, 0.5, ALU.mult,
                                                ALU.add).then_inc(gs_ready, 1)
                if sd is not None:
                    delta(sd)
                for kk in preload_at(slot):
                    y_lo_tile(0, kk)

            def sum_out(e):
                m, cols = OUT_PARTS[e]
                if 0 < m < KT - 1:
                    pool.wait_ge(sqs_ok, e + 1)
                    if sums_before[e]:
                        pool.wait_ge(sqs_sum, sums_before[e])
                    nc.gpsimd.tensor_tensor(ssum[:, cols], ssum[:, cols], sqs[:, m % 2, cols], ALU.add).then_inc(sqs_sum, 1)

            def sum_f(m):
                if 0 < m < KT - 1:
                    pool.wait_ge(sqs_ok, len(OUT_PARTS) + m + 1)
                    if m > 1:
                        pool.wait_ge(sqs_sum, SUMS[1] + m - 1)
                    nc.gpsimd.tensor_tensor(ssum[:], ssum[:], sqs[:, m % 2], ALU.add).then_inc(sqs_sum, 1)

            def gain_row(i):
                pool.wait_ge(in_post, 16)
                pool.wait_ge(h1_ok, i + 1)
                if i >= 2:
                    pool.wait_ge(tr2, i - 1)
                nc.gpsimd.tensor_tensor(rows[:, i % 2], h1[:, i], post[:], ALU.mult).then_inc(hg_ok, 1)

            for r, (tile, t0, k) in enumerate(LATE):
                if 1 <= r <= 2 * KT:
                    y_lo_tile(1 + (r - 1) // KT, (r - 1) % KT)
                if r == N_BR + KT - H:
                    for e in range(KT - H, KT):
                        sum_out(e)
                if r == N_BR + KT - 1:
                    gain_row(1)
                for j in range(k):
                    split_lo(t0 + j + SPL)
                if r < N_BR and r // KT == 2:
                    m = r % KT
                    pool.wait_ge(mxh_ready, m + 1)
                    nc.gpsimd.tensor_tensor(mx_lo[:, m], mix_acc[:, m], mx_hi[:, m].bitcast(F32),
                                            ALU.subtract).then_inc(mxl_ready, 1)
                if tile[0] == "out" and tile[1] < KT - H:
                    sum_out(tile[1])
                if r == N_BR + KT - H:
                    for e in range(KT, len(OUT_PARTS)):
                        sum_out(e)
                    gain_row(0)
                if r == N_BR + KT - 1:
                    for i in range(2, ST):
                        gain_row(i)
                if r >= L_F2[1]:
                    sum_f(tile[1] % KT)
                if tile[0] == "f1":
                    f = tile[1]
                    pool.wait_ge(hh_ok, f + 1)
                    nc.gpsimd.tensor_tensor(h_lo[:, f % 16], sq[:, f % 2], h_hi[:, f % 16].bitcast(F32),
                                            ALU.subtract).then_inc(hl_ok, 1)

        @block.scalar
        def _(act):
            def square(j):
                if j < ST:
                    act.wait_ge(in_x[j], 16)
                else:
                    act.wait_ge(in_mem, 16)
                if j:
                    act.wait_ge(su_sq, j)
                nc.scalar.activation(p_a_scr, x_tok[:, j] if j < ST else m_tok[:, j - ST], ACT.Square,
                                     accum_out=sml[:, j:j + 1]).then_inc(su_sq, 1)

            def row_hi(j):
                act.wait_ge(su_full, j + 1)
                nc.scalar.copy(row_parts(j)[0], full[:, j % 4]).then_inc(su_hi, 1)

            for j in range(ST):
                square(j)
            for j in (2, 3):
                act.wait_ge(su_rms, 1)
                nc.scalar.mul(x_tok[:, j], x_tok[:, j], sml[:, 8 + j:9 + j]).then_inc(su_norm2, 1)
            for j in range(ST):
                row_hi(j)
            for j in range(ST, N_SU):
                square(j)
            for j in range(ST, N_SU):
                row_hi(j)

            def bias_values():
                act.wait_ge(f_mm, 1)
                nc.scalar.mul(f_row, ps_a[0:HA, 0, 0:SPAN], 1.0 / SC_A).then_inc(f_sb, 1)

            def beta_and_decay():
                act.wait_ge(lam_sum, 1)
                nc.scalar.activation(LAME, LAMS, ACT.Exp).then_inc(lam_exp, 1)
                act.wait_ge(ba_dve, 1)
                nc.scalar.activation(ba[:, 0], ba[:, 0], ACT.Tanh, scale=0.5)
                nc.scalar.activation(ba[:, 2], ba[:, 2], ACT.Exp)
                nc.scalar.activation(ealog, par[:, PC_ALOG:PC_ALOG + HB], ACT.Exp).then_inc(ba_act, 1)

            def evacuate(t):
                kind, j = TILES[t]
                bank = acc[:, t % 2]
                act.wait_ge(tile_used, t + 1)
                free = NEED_FREE.get(TILES[t])
                if free in a_idx:
                    act.wait_ge(a_mm, a_idx[free] + 1)
                elif kind == "dz" and free is not None:
                    act.wait_ge(d_dve, dD[d_idx[free] + 1])
                if kind == "mk":
                    last = nc.scalar.copy(mk_T[:, j], bank[:, 0:MEM])
                elif kind == "mv":
                    if j == 0:
                        act.wait_ge(ba_split, 1)
                    last = nc.scalar.copy(mv_T[:, j], bank[:, 0:MEM])
                elif kind == "cq":
                    last = nc.scalar.copy(cq_T[:, (j // 2) % 2, j % 2], bank)
                elif kind in ("aq", "ak", "av"):
                    if (kind, j) == ("av", 1):
                        act.wait_ge(f_out, 16)
                    last = nc.scalar.copy(qkv_T[:, j % 2, ("aq", "ak", "av").index(kind)], bank)
                elif kind in ("dq", "dk", "dv"):
                    n = n_conv[t]
                    if n == 0:
                        act.wait_ge(pad_set, 1)
                    if n >= 2:
                        act.wait_ge(co_ready, n - 1)
                    last = nc.scalar.copy(conv_x[:, n % 2, 3:3 + S], bank)
                elif kind == "dz":
                    last = nc.scalar.copy(zs[:, j % 2], bank)
                elif kind == "gate":
                    n = n_gate[t]
                    if n:
                        act.wait_ge(g_out, 16 * n)
                    last = nc.scalar.activation(gate_st[:], bank, ACT.Tanh, scale=0.5)
                last.then_inc(acc_free, 1)

            def finish(t):
                if t in n_conv:
                    n = n_conv[t]
                    act.wait_ge(cy_ready, n + 1)
                    nc.scalar.activation(conv_x[:, n % 2, 3:3 + S], conv_y[:, n % 2], ACT.Tanh,
                                         scale=0.5).then_inc(ct_ready, 1)
                else:
                    n = n_z[t]
                    if n:
                        act.wait_ge(z_ready, n)
                    act.wait_ge(acc_free, t + 1)
                    nc.scalar.activation(z_t[:], zs[:, n % 2], ACT.Tanh, scale=0.5).then_inc(zt_ready, 1)

            def attn(i):
                kind, h = ATTN[i]
                act.wait_ge(a_mm, i + 1)
                if kind == "mv":
                    last = nc.scalar.copy(mv_tok[:, :, h * 512:(h + 1) * 512], ps_a[:, 0:2])
                elif kind == "cs":
                    act.wait_ge(a_max, n_max[i + 1])
                    for s in range(ST):
                        last = nc.scalar.activation(p_c[:, s], ps_a[:, s // 2, (s % 2) * MEM:(s % 2 + 1) * MEM],
                                                    ACT.Exp, bias=nba[:, s:s + 1], scale=SC_C,
                                                    accum_out=sma[:, s:s + 1])
                elif kind == "ct":
                    last = nc.scalar.copy(pT_c[:], ps_a[:, 0:2])
                elif kind in ("cv", "ay"):
                    if n_spill[i]:
                        act.wait_ge(y_out, 16 * n_spill[i])
                    if kind == "cv":
                        last = nc.scalar.copy(y_st[:], ps_a[:, 0:2])
                    else:
                        last = nc.scalar.activation(y_st[:, 0], ps_a[:, 0], ACT.Copy, scale=GSUB)
                elif kind == "av":
                    last = nc.scalar.copy(v_tok[:], ps_a[:, 0])
                elif kind in ("as0", "as1"):
                    m = int(kind[2])
                    act.wait_ge(a_max, n_max[i + 1])
                    for q in range(ST):
                        w = (q + 1) * P
                        src = flat(ps_a[:])[:, bank_of[q]:bank_of[q] + w]
                        last = nc.scalar.activation(p_a[:, m, pack_of[q]:pack_of[q] + w], src, ACT.Exp,
                                                    bias=nba[:, q:q + 1], scale=SC_A,
                                                    accum_out=sma[:, 4 * m + q:4 * m + q + 1])
                elif kind == "at":
                    nc.scalar.copy(wT[:, 0:1024], two(ps_a))
                    last = nc.scalar.copy(wT[:, 1024:1280], ps_a[:, 2, 256:512])
                elif kind == "ap":
                    last = nc.scalar.copy(flat(o_a[:]), ps_a[:, 0])
                last.then_inc(a_act, 1)

            def delta(i):
                kind, p, c = DELTA[i]
                if "A" not in PARTS[kind]:
                    return
                act.wait_ge(d_mm, i + 1)
                if kind == "dE":
                    last = nc.scalar.activation(flat(ET[:]), two(ps_d), ACT.Exp)
                elif kind == "sb":
                    o_v = O[:].rearrange("p (h c) d -> p h c d", h=2)[:, :, c]
                    last = nc.scalar.copy(o_v, ps_d[:, 0, 0:256].rearrange("p (h d) -> p h d", h=2))
                elif kind in ("T1", "Tc"):
                    last = nc.scalar.copy(halves(TN[:], c + 1, 0), halves(blocks(two(ps_d)), c + 1, 0))
                elif kind == "Za":
                    last = nc.scalar.copy(halves(Z[:], c, 0), compact(c))
                else:
                    dst = {"dq": Q, "dk": K, "dqT": QT, "dqd": QDT, "dkT": KTT, "dkb": KBT, "dU": U, "dW": WT}[kind]
                    last = nc.scalar.copy(flat(dst[:]), two(ps_d))
                last.then_inc(d_act, 1)

            for n, (main, ev, fi, sa, sd) in enumerate(SLOTS):
                if n == G_SLOT:
                    act.wait_ge(g_mm, 1)
                    for m, dst in enumerate((e_in, e_tail, e_all)):
                        last = nc.scalar.activation(flat(dst[:]), ps_d[:, 2, m * 32:(m + 1) * 32], ACT.Exp)
                    last.then_inc(g_exp, 1)
                if n == BA_SLOT:
                    act.wait_ge(ba_rows, 1)
                    nc.scalar.copy(ba_T[0:2 * HB], ps_a[0:2 * HB, 2]).then_inc(ba_sb, 1)
                if n == BA_SLOT + 1:
                    beta_and_decay()
                if n == F_SLOT:
                    bias_values()
                if ev is not None:
                    evacuate(ev)
                if fi is not None:
                    finish(fi)
                if sd is not None:
                    delta(sd)
                if sa is not None and ATTN[sa][0] not in EXP_KINDS:
                    attn(sa)
                if lagged(n, EXP_LAG, EXP_KINDS) is not None:
                    attn(lagged(n, EXP_LAG, EXP_KINDS))

            def out_part(e):
                m, cols = OUT_PARTS[e]
                first_half = KT - H <= e < KT
                if first_half:
                    act.wait_ge(out_half, e - (KT - H) + 1)
                else:
                    act.wait_ge(tile_used, tiles_of(N_BR + m + 1))
                if m == 0:
                    act.wait_ge(mxl_ready, KT)
                if m > 2:
                    last = max(i for i in range(e) if OUT_PARTS[i][0] == m - 2
                               and OUT_PARTS[i][1].start <= cols.start and cols.stop <= OUT_PARTS[i][1].stop)
                    act.wait_ge(sqs_sum, sums_before[last + 1])
                bank = result_bank(N_BR + m)[:, cols]
                nc.scalar.activation(sqs[:, m % 2, cols] if m else ssum[:], bank, ACT.Square).then_inc(sqs_ok, 1)
                nc.scalar.mul(f_T[:, m, cols], bank, par[:, PC_POST + m:PC_POST + m + 1]).then_inc(o_ev, 1)

            def square_row(i):
                act.wait_ge(h1_ok, i + 1)
                if i:
                    act.wait_ge(ss2, i)
                nc.scalar.activation(junk[:], h1[:, i], ACT.Square, accum_out=sml[:, 100 + i:101 + i]).then_inc(ss2, 1)

            def scale_row(i):
                act.wait_ge(hg_ok, i + 1)
                act.wait_ge(rs2, i // 2 + 1)
                nc.scalar.mul(rows[:, i % 2], rows[:, i % 2], sml[:, 108 + i:109 + i]).then_inc(n2n, 1)

            def row_hi2(i):
                act.wait_ge(tr2, i + 1)
                nc.scalar.copy(n2_hi[:, :, i * P:(i + 1) * P], blocks(two(back(i)))).then_inc(n2h, 1)

            for e in range(len(OUT_PARTS) - 1):
                out_part(e)
            square_row(0)
            out_part(len(OUT_PARTS) - 1)
            square_row(1)
            for i in range(2):
                scale_row(i)
            for i in range(2):
                row_hi2(i)
            for i in range(2, ST):
                square_row(i)
            for i in range(2, ST):
                scale_row(i)
            for i in range(2, ST):
                row_hi2(i)
            for f in range(DFF // P):
                act.wait_ge(relu_ok, f + 1)
                if f >= 2:
                    act.wait_ge(hl_ok, f - 1)
                nc.scalar.activation(sq[:, f % 2], relu[:, f % 2], ACT.Square).then_inc(sq_ok, 1)
            for m in range(KT):
                act.wait_ge(f_ev, KT + m + 1)
                if m == 0:
                    act.wait_ge(ss_mm, 2)
                if m > 2:
                    act.wait_ge(sqs_sum, SUMS[1] + m - 2)
                nc.scalar.activation(sqs[:, m % 2] if m else ssum[:], f_T[:, m], ACT.Square).then_inc(sqs_ok, 1)
                nc.scalar.mul(f_T[:, m], f_T[:, m], par[:, PC_POST + KT + m:PC_POST + KT + m + 1]).then_inc(fg_ok, 1)

        @block.vector
        def _(dve):
            n_own = [0]

            def link(ins):
                n_own[0] += 1
                ins.then_inc(vch, 1)
                dve.wait_ge(vch, n_own[0])

            V_ = nc.vector

            def rsqrt(dst, src, tmp, last_to=None):
                link(V_.tensor_scalar(tmp.bitcast(I32), src.bitcast(I32), 1, None, ALU.logical_shift_right))
                link(V_.tensor_scalar(dst.bitcast(I32), tmp.bitcast(I32), -1.0, float(0x5f3759df), ALU.mult, ALU.add))
                for n in range(3):
                    link(V_.tensor_tensor(tmp, dst, dst, ALU.mult))
                    link(V_.scalar_tensor_tensor(out=tmp, in0=tmp, scalar=-0.5, in1=src, op0=ALU.mult, op1=ALU.mult))
                    ins = V_.scalar_tensor_tensor(out=dst, in0=tmp, scalar=1.5, in1=dst, op0=ALU.add, op1=ALU.mult)
                    if n == 2 and last_to is not None:
                        ins.then_inc(last_to, 1)
                    else:
                        link(ins)

            def split_hi(t):
                if t < NT:
                    dve.wait_ge(ld[t % RAW], 16 * (t // RAW + 1))
                    if t >= SPL:
                        dve.wait_ge(tile_used, t - SPL + 1)
                        dve.wait_ge(lo_ready, t - SPL + 1)
                    V_.tensor_copy(w_hi[:, t % SPL], w_raw[:, t % RAW]).then_inc(hi_ready, 1)

            def rms_of_two(j, last_to=None):
                v, r, tm = sml[:, j:j + 2], sml[:, 8 + j:10 + j], sml[:, 16 + j:18 + j]
                dve.wait_ge(su_sq, j + 2)
                link(V_.tensor_scalar(v, v, 1.0 / D, EPS, ALU.mult, ALU.add))
                rsqrt(r, v, tm, last_to)

            def normalise(j):
                rows_in = x_tok[:, j] if j < ST else m_tok[:, j - ST]
                V_.tensor_scalar(rows_in, rows_in, sml[:, 8 + j:9 + j], None, ALU.mult).then_inc(su_norm, 1)

            def gain(j):
                dve.wait_ge(su_tr, j + 1)
                if j >= 4:
                    dve.wait_ge(su_lo, 1)
                    dve.wait_ge(su_lo2, 1)
                g = par[:, PC_PRE:PC_PRE + KT] if j < ST else par[:, PC_MEM:PC_MEM + KT]
                V_.tensor_tensor(full[:, j % 4], blocks(two(side[j % 2])), along(g, P), ALU.mult).then_inc(su_full, 1)

            def row_lo(j):
                dve.wait_ge(su_hi, j + 1)
                hi, lo = row_parts(j)
                V_.tensor_tensor(lo, full[:, j % 4], hi.bitcast(F32), ALU.subtract).then_inc(su_lo2, 1)

            rms_of_two(0)
            normalise(0)
            normalise(1)
            rms_of_two(2, su_rms)
            dve.wait_ge(in_par, 16)
            split_hi(0)
            gain(0)
            gain(1)
            split_hi(1)
            gain(2)
            row_lo(1)
            gain(3)
            row_lo(3)
            split_hi(2)
            rms_of_two(ST)
            for j in range(ST, N_SU):
                normalise(j)
            for j in range(ST, N_SU):
                gain(j)
            dve.wait_ge(in_ba, 16)
            link(V_.tensor_copy(wb_hi[:], w_ba_sb[:]))
            V_.tensor_tensor(wb_lo[:], w_ba_sb[:], wb_hi[:].bitcast(F32), ALU.subtract).then_inc(ba_split, 1)
            lamv = par[:, PC_LAM:PC_LAM + 4 * DA].rearrange("p (a b d) -> p a b d", a=2, b=2)
            link(V_.tensor_tensor(lam_prod, lamv[:, :, 0], lamv[:, :, 1], ALU.mult))
            V_.reduce_sum(LAMS, lam_prod, AX_X).then_inc(lam_sum, 1)
            V_.tensor_scalar(GSUB, par[:, PC_SUB:PC_SUB + 1], 1.0 - LAM_INIT, None, ALU.mult)
            V_.tensor_scalar(GDN, par[:, PC_DNG:PC_DNG + 1], 0.5, None, ALU.mult)
            def beta_and_decay_inputs():
                dve.wait_ge(ba_mm, 1)
                bav = ps_a[:, 2, 0:ST * 2 * HB].rearrange("p (c h) -> p h c", c=ST)
                V_.tensor_copy(ba[:, 0], bav[:, 0:HB])
                link(V_.tensor_tensor(ba[:, 1], bav[:, HB:2 * HB], along(par[:, PC_DTB:PC_DTB + HB], ST), ALU.add))
                link(V_.tensor_scalar(ba[:, 2], ba[:, 1], -1.0, None, ALU.mult))
                V_.tensor_tensor(ba[:, 2], ba[:, 2], ba[:, 1], ALU.min).then_inc(ba_dve, 1)

            def beta_and_decay():
                dve.wait_ge(lam_exp, 1)
                link(V_.tensor_tensor(NLAM, LAME[:, 1:2], LAME[:, 0:1], ALU.subtract))
                link(V_.tensor_scalar(NLAM, NLAM, LAM_INIT, None, ALU.subtract))
                dve.wait_ge(ba_act, 1)
                V_.tensor_scalar(beta[:], ba[:, 0], 0.5, 0.5, ALU.mult, ALU.add)
                V_.tensor_scalar(hbeta[:], ba[:, 0], 0.25, 0.25, ALU.mult, ALU.add)
                link(V_.tensor_scalar(ba[:, 3], ba[:, 2], 2.0, None, ALU.add))
                link(V_.reciprocal(ba[:, 4], ba[:, 3]))
                link(V_.tensor_tensor(ba[:, 4], ba[:, 4], ba[:, 2], ALU.mult))
                link(V_.tensor_tensor(ba[:, 5], ba[:, 4], ba[:, 4], ALU.mult))
                link(V_.tensor_scalar(ba[:, 3], ba[:, 5], 1.0 / 17, None, ALU.mult))
                for n in range(15, 1, -2):
                    link(V_.scalar_tensor_tensor(out=ba[:, 3], in0=ba[:, 3], scalar=1.0 / n, in1=ba[:, 5],
                                                 op0=ALU.add, op1=ALU.mult))
                link(V_.scalar_tensor_tensor(out=ba[:, 3], in0=ba[:, 3], scalar=1.0, in1=ba[:, 4], op0=ALU.add, op1=ALU.mult))
                link(V_.tensor_scalar(ba[:, 1], ba[:, 1], 0.0, None, ALU.max))
                link(V_.scalar_tensor_tensor(out=ba[:, 1], in0=ba[:, 3], scalar=2.0, in1=ba[:, 1], op0=ALU.mult, op1=ALU.add))
                V_.scalar_tensor_tensor(out=gdec[:], in0=ba[:, 1], scalar=-1.0, in1=along(ealog, ST),
                                        op0=ALU.mult, op1=ALU.mult).then_inc(g_ready, 1)

            def conv(t):
                kind, h = TILES[t]
                n = n_conv[t]
                col = PC_CONV + 4 * ({"dq": 0, "dk": 8, "dv": 16}[kind] + h)
                dve.wait_ge(acc_free, t + 1)
                y = conv_y[:, n % 2]
                link(V_.tensor_scalar(y, conv_x[:, n % 2, 0:S], par[:, col:col + 1], None, ALU.mult))
                for j in (1, 2, 3):
                    ins = V_.scalar_tensor_tensor(out=y, in0=conv_x[:, n % 2, j:j + S], scalar=par[:, col + j:col + j + 1],
                                                  in1=y, op0=ALU.mult, op1=ALU.add)
                    if j < 3:
                        link(ins)
                ins.then_inc(cy_ready, 1)

            def finish(t):
                kind, h = TILES[t]
                if t in n_conv:
                    n = n_conv[t]
                    dve.wait_ge(ct_ready, n + 1)
                    if h >= 2:
                        dve.wait_ge(d_mm, d_idx[("dv", h // 2 - 1, 0)] + 1)
                    V_.scalar_tensor_tensor(out=conv_o[:, ("dq", "dk", "dv").index(kind), h % 2],
                                            in0=conv_x[:, n % 2, 3:3 + S], scalar=1.0, in1=conv_y[:, n % 2],
                                            op0=ALU.add, op1=ALU.mult).then_inc(co_ready, 1)
                else:
                    n = n_z[t]
                    dve.wait_ge(zt_ready, n + 1)
                    V_.scalar_tensor_tensor(out=zs[:, n % 2], in0=z_t[:], scalar=1.0, in1=zs[:, n % 2],
                                            op0=ALU.add, op1=ALU.mult).then_inc(z_ready, 1)

            def attn(i):
                kind, h = ATTN[i]
                if kind not in EXP_KINDS:
                    return
                dve.wait_ge(a_mm, i + 1)
                if kind == "cs":
                    link(V_.reduce_max(mxa, two(ps_a).rearrange("p (a b) -> p a b", a=ST), AX_X))
                    V_.tensor_scalar(nba, mxa, -SC_C, None, ALU.mult).then_inc(a_max, 1)
                else:
                    if (kind, h) == ("as0", 0):
                        dve.wait_ge(strip_in, 16)
                        link(V_.tensor_tensor(strip[:, :, P:2 * P], strip[:, :, P:2 * P],
                                              over(cst[:, C_CAUS, :], HA), ALU.add))
                    ps = flat(ps_a[:])
                    near = view(ps, [[512, 3], [1, 2 * P]], 256)
                    V_.tensor_tensor(near, near, over(strip[:, h], 3), ALU.add)
                    link(V_.tensor_tensor(ps[:, 512:512 + P], ps[:, 512:512 + P], strip[:, h, P:2 * P], ALU.add))
                    for q in range(ST):
                        ins = V_.reduce_max(mxa[:, q:q + 1], ps[:, bank_of[q]:bank_of[q] + (q + 1) * P], AX_X)
                    link(ins)
                    V_.tensor_scalar(nba, mxa, -SC_A, None, ALU.mult).then_inc(a_max, 1)

            def attn_scale(i):
                kind, h = ATTN[i]
                dve.wait_ge(a_act, aA[i + 1])
                if kind == "cs":
                    link(V_.reciprocal(rca[:, 0:4], sma[:, 0:4]))
                    last = V_.tensor_tensor(p_c[:], p_c[:], along(rca[:, 0:4], MEM), ALU.mult)
                    last.then_inc(a_dve, 1)
                elif kind == "as1":
                    link(V_.reciprocal(rca, sma))
                    link(V_.tensor_scalar(rca[:, 4:8], rca[:, 4:8], NLAM, None, ALU.mult))
                    for q in range(ST):
                        c = slice(pack_of[q], pack_of[q] + (q + 1) * P)
                        ins = V_.tensor_scalar(p_a[:, 1, c], p_a[:, 1, c], rca[:, 4 + q:5 + q], None, ALU.mult)
                    link(ins)
                    for q in range(ST):
                        c = slice(pack_of[q], pack_of[q] + (q + 1) * P)
                        ins = V_.scalar_tensor_tensor(out=p_a[:, 0, c], in0=p_a[:, 0, c], scalar=rca[:, q:q + 1],
                                                      in1=p_a[:, 1, c], op0=ALU.mult, op1=ALU.add)
                    ins.then_inc(a_dve, 1)
                else:
                    link(V_.tensor_tensor(p_a[:, 1, 0:S], flat(o_a[:]), flat(o_a[:]), ALU.mult))
                    link(V_.reduce_sum(ssa, p_a[:, 1, 0:S].rearrange("p (a b) -> p a b", a=ST), AX_X))
                    link(V_.tensor_scalar(ssa, ssa, 1.0 / P, EPS, ALU.mult, ALU.add))
                    rsqrt(rsa, ssa, tma)
                    V_.tensor_tensor(o_a[:], o_a[:], along(rsa, P), ALU.mult).then_inc(a_dve, 1)

            def scale_by_norm(buf, mul, add, factor):
                link(V_.tensor_tensor(SCR[:], buf[:], buf[:], ALU.mult))
                link(V_.reduce_sum(ssd, SCR[:], AX_X))
                link(V_.tensor_scalar(ssd, ssd, mul, add, ALU.mult, ALU.add))
                rsqrt(rsd, ssd, tmd)
                if factor != 1.0:
                    link(V_.tensor_scalar(rsd, rsd, factor, None, ALU.mult))
                return V_.tensor_tensor(buf[:], buf[:], along(rsd, P), ALU.mult)

            def delta(i):
                kind, p, c = DELTA[i]
                if "D" not in PARTS[kind]:
                    return
                dve.wait_ge(d_mm, i + 1)
                heads = slice(2 * p, 2 * p + 2)
                ps = blocks(two(ps_d))
                if kind == "dq":
                    dve.wait_ge(d_act, dA[i + 1])
                    last = scale_by_norm(Q, 1.0, 4 * EPS, P ** -0.5)
                elif kind == "dk":
                    dve.wait_ge(d_act, dA[i + 1])
                    link(scale_by_norm(K, 1.0, 4 * EPS, 1.0))
                    last = V_.tensor_tensor(KB[:], K[:], along(flat(beta[:, heads]), P), ALU.mult)
                elif kind == "dv":
                    last = V_.tensor_tensor(V[:], ps, along(flat(hbeta[:, heads]), P), ALU.mult)
                elif kind == "dqT":
                    dve.wait_ge(g_exp, 1)
                    last = V_.tensor_tensor(Q[:], Q[:], along(flat(e_in[:, heads]), P), ALU.mult)
                elif kind == "dL":
                    link(V_.tensor_tensor(LT[:], ps, ET[:], ALU.mult))
                    last = V_.tensor_tensor(TT[:], LT[:], over(cst[:, C_MASK0, :], 8), ALU.mult)
                elif kind == "dA":
                    V_.tensor_tensor(AT[:], ps, ET[:], ALU.mult).then_inc(at_ready, 1)
                    last = V_.tensor_tensor(TT[:], over(ident, 8), TT[:], ALU.subtract)
                elif kind in ("Wb", "Wl"):
                    part = halves(TT[:], c, 1)
                    last = V_.tensor_tensor(part, part, compact(c), ALU.subtract)
                elif kind == "sa":
                    u_v = U[:].rearrange("p (h c) d -> p h c d", h=2)[:, :, c]
                    last = V_.tensor_tensor(vnew[:], u_v, ps_d[:, 0, 0:256].rearrange("p (h d) -> p h d", h=2),
                                            ALU.subtract)
                elif kind == "sb":
                    for hh in range(2):
                        kv = ps_d[:, 1, hh * P:(hh + 1) * P]
                        if c == 0:
                            last = V_.tensor_copy(state[:, hh], kv)
                        else:
                            last = V_.scalar_tensor_tensor(out=state[:, hh], in0=state[:, hh],
                                                           scalar=e_all[:, 2 * p + hh, c:c + 1], in1=kv,
                                                           op0=ALU.mult, op1=ALU.add)
                    if c == ST - 1:
                        link(last)
                        dve.wait_ge(d_act, dA[i + 1])
                        last = scale_by_norm(O, 1.0 / P, EPS, 1.0)
                elif kind == "dO":
                    dve.wait_ge(z_ready, 2 * (p + 1))
                    last = V_.scalar_tensor_tensor(out=flat(ET[:]), in0=two(ps_d), scalar=GDN, in1=flat(zs[:]),
                                                   op0=ALU.mult, op1=ALU.mult)
                last.then_inc(d_dve, 1)

            for n, (main, ev, fi, sa, sd) in enumerate(SLOTS):
                if n == BA_SLOT + 1:
                    beta_and_decay_inputs()
                if n == BA_SLOT + 3:
                    beta_and_decay()
                if ev is not None:
                    split_hi(ev + SPL)
                if sd is not None:
                    delta(sd)
                if sa is not None:
                    attn(sa)
                if ev in n_conv:
                    conv(ev)
                if fi is not None:
                    finish(fi)
                if lagged(n, SCALE_LAG, ("cs", "as1")) is not None:
                    attn_scale(lagged(n, SCALE_LAG, ("cs", "as1")))
                if lagged(n, NORM_LAG, ("ap",)) is not None:
                    attn_scale(lagged(n, NORM_LAG, ("ap",)))
                for kk in preload_at(n):
                    dve.wait_ge(y_pre[kk % 2], 16 * (kk // 2 + 1))
                    if kk == 0:
                        dve.wait_ge(a_mm, len(ATTN))
                    V_.tensor_copy(y_hi[0][:, kk], y_st[:, kk % 2]).then_inc(yh_ready, 1)

            def y_hi_tile(n):
                dve.wait_ge(y_in[n % 2], 16 * (n // 2 + 1))
                if n == KT:
                    dve.wait_ge(tile_used, tiles_of(KT))
                V_.tensor_copy(y_hi[1 + n // KT][:, n % KT], y_raw[:, n % 2]).then_inc(yh_ready, 1)

            def rms_of_f(n, i, cnt, sums):
                v, r, tm = sml[:, 96 + i:96 + i + cnt], sml[:, 116 + i:116 + i + cnt], sml[:, 120 + i:120 + i + cnt]
                dve.wait_ge(ss_mm, n)
                link(V_.tensor_scalar(v, sums[:, i:i + cnt], 1.0 / D, EPS, ALU.mult, ALU.add))
                rsqrt(r, v, tm)

            def norm_row(u, i):
                dve.wait_ge(tr_f, u * ST + i + 1)
                V_.scalar_tensor_tensor(out=h1[:, i], in0=two(from_f(i)), scalar=sml[:, 116 + i:117 + i],
                                        in1=h1[:, i], op0=ALU.mult, op1=ALU.add).then_inc(h1_ok, 1)

            def rms_of_rows(j):
                v, r, tm = sml[:, 100 + 2 * j:102 + 2 * j], sml[:, 108 + 2 * j:110 + 2 * j], sml[:, 124:126]
                dve.wait_ge(ss2, 2 * j + 2)
                link(V_.tensor_scalar(v, v, 1.0 / D, EPS, ALU.mult, ALU.add))
                rsqrt(r, v, tm, last_to=rs2)

            def row_lo2(i):
                dve.wait_ge(n2h, i + 1)
                c = slice(i * P, (i + 1) * P)
                V_.tensor_tensor(n2_lo[:, :, c], blocks(two(back(i))), n2_hi[:, :, c].bitcast(F32),
                                 ALU.subtract).then_inc(n2l, 1)

            for r, (tile, t0, k) in enumerate(LATE):
                if 1 <= r <= 2 * KT:
                    y_hi_tile(r - 1)
                for j in range(k):
                    split_hi(t0 + j + SPL)
                bank = result_bank(r)
                if r < N_BR:
                    b, m = r // KT, r % KT
                    dve.wait_ge(tile_used, tiles_of(r + 1))
                    dve.wait_ge(gin[r % 2], 16 * (r // 2 + 1))
                    if b == 0:
                        V_.tensor_tensor(mix_acc[:, m], bank, g_in[:, r % 2], ALU.mult).then_inc(gated, 1)
                    else:
                        V_.tensor_tensor(g_tmp[:], bank, g_in[:, r % 2], ALU.mult).then_inc(gated, 1)
                        dve.wait_ge(gated, r + 1)
                        ins = V_.tensor_tensor(mix_acc[:, m], mix_acc[:, m], g_tmp[:], ALU.add)
                        link(ins)
                        if b == 2:
                            V_.tensor_copy(mx_hi[:, m], mix_acc[:, m]).then_inc(mxh_ready, 1)
                elif r == N_BR + KT - H:
                    rms_of_f(1, 0, 2, ps_d[:, 2])
                    dve.wait_ge(in_h1, 16)
                    for i in range(2):
                        norm_row(0, i)
                elif r == N_BR + KT - 1:
                    rms_of_rows(0)
                    rms_of_f(2, 2, 2, ps_a[:, 2])
                    norm_row(0, 2)
                    norm_row(0, 3)
                    for i in range(2):
                        row_lo2(i)
                    rms_of_rows(1)
                    for i in range(2, ST):
                        row_lo2(i)
                elif tile[0] == "f1":
                    f = tile[1]
                    dve.wait_ge(tile_used, tiles_of(r + 1))
                    if f >= 2:
                        dve.wait_ge(sq_ok, f - 1)
                    V_.tensor_scalar(relu[:, f % 2], bank, 0.0, None, ALU.max).then_inc(relu_ok, 1)
                    dve.wait_ge(sq_ok, f + 1)
                    V_.tensor_copy(h_hi[:, f % 16], sq[:, f % 2]).then_inc(hh_ok, 1)
                elif tile[0] == "f2":
                    dve.wait_ge(tile_used, tiles_of(r + 1))
                    m = tile[1] % KT
                    if r < L_F2[0] + KT:
                        V_.tensor_copy(f_T[:, m], bank).then_inc(f_ev, 1)
                    else:
                        V_.tensor_tensor(f_T[:, m], f_T[:, m], bank, ALU.add).then_inc(f_ev, 1)
            rms_of_f(3, 0, ST, ps_d[:, 2])
            for i in range(ST):
                norm_row(1, i)

        @block.tensor
        def _(pe):
            mm = nc.tensor.matmul

            def transpose_rows(j):
                if j in (2, 3):
                    pe.wait_ge(su_norm2, j - 1)
                else:
                    pe.wait_ge(su_norm, j + 1 if j < 2 else j - 1)
                if j >= 2:
                    pe.wait_ge(su_full, j - 1)
                src = x_tok[:, j] if j < ST else m_tok[:, j - ST]
                for m in range(KT):
                    last = nc.tensor.transpose(side[j % 2][:, m // 4, (m % 4) * P:(m % 4 + 1) * P],
                                               src[:, m * P:(m + 1) * P], ident)
                last.then_inc(su_tr, 1)

            def beta_and_decay_rows():
                pe.wait_ge(ba_split, 1)
                dst = ps_a[0:2 * HB, 2]
                for k in range(KT):
                    mm(dst, wb_hi[:, k], n_hi[:, k], start=k == 0, stop=False)
                    mm(dst, wb_hi[:, k], n_lo[:, k], start=False, stop=False)
                    last = mm(dst, wb_lo[:, k], n_hi[:, k], start=False, stop=k == KT - 1)
                last.then_inc(ba_rows, 1)

            def beta_and_decay():
                pe.wait_ge(ba_sb, 1)
                for c in range(ST):
                    last = nc.tensor.transpose(ps_a[:, 2, c * 2 * HB:(c + 1) * 2 * HB],
                                               ba_T[0:2 * HB, c * P:(c + 1) * P], ident[0:2 * HB, 0:2 * HB])
                last.then_inc(ba_mm, 1)

            def bias_values():
                pe.wait_ge(in_oh, 16)
                pe.wait_ge(in_relb, 16)
                pe.wait_ge(su_full, N_SU)
                pe.wait_ge(su_lo, len(POOL_ROWS))
                mm(ps_a[0:HA, 0, 0:SPAN], relb_sb, onehot_sb, start=True, stop=True).then_inc(f_mm, 1)

            pe.wait_ge(in_id, 16)
            for j in range(ST):
                transpose_rows(j)
            def weight_tile(bank, t, ks, hi_of, lo_of, start, stop, k_wait=None):
                for k in ks:
                    if k_wait is not None:
                        k_wait(k)
                    wh, wl = w_hi[:, t % SPL, k], w_lo[:, t % SPL, k]
                    mm(bank, wh, hi_of(k), start=start and k == 0, stop=False)
                    mm(bank, wh, lo_of(k), start=False, stop=False)
                    last = mm(bank, wl, hi_of(k), start=False, stop=stop and k == KT - 1)
                return last

            def first_tiles(c, t):
                pe.wait_ge(su_lo, c + 1)
                pe.wait_ge(su_lo2, c + 1)
                pe.wait_ge(lo_ready, t + 1)
                cols = HALF[c]
                last = weight_tile(acc[:, t, cols], t, range(KT), lambda k: n_hi[:, k, cols],
                                   lambda k: n_lo[:, k, cols], True, True)
                if c:
                    last.then_inc(tile_used, 1)

            def main_half(t, half):
                kind = TILES[t][0]
                if t < 2:
                    if (t, half) in ((0, 0), (0, 1)):
                        first_tiles(0, half)
                    if half == 1:
                        first_tiles(1, t)
                    return
                if half != 1:
                    pe.wait_ge(lo_ready, t + 1)
                    if t >= 2:
                        pe.wait_ge(acc_free, t - 1)
                ks = range(KT) if half is None else range(half * KT // 2, (half + 1) * KT // 2)
                if kind in ("mk", "mv"):
                    pe.wait_ge(su_lo, len(POOL_ROWS))
                    last = weight_tile(acc[:, t % 2, 0:MEM], t, ks, lambda k: m_hi[:, k], lambda k: m_lo[:, k], True, True)
                else:
                    last = weight_tile(acc[:, t % 2], t, ks, lambda k: n_hi[:, k], lambda k: n_lo[:, k], True, True)
                if half != 0:
                    last.then_inc(tile_used, 1)

            def attn(i):
                kind, h = ATTN[i]
                if i:
                    pe.wait_ge(a_act, aA[i])
                    if aD[i]:
                        pe.wait_ge(a_dve, aD[i])
                if kind == "mv":
                    if h == 0:
                        pe.wait_ge(acc_free, TILES.index(("mv", KT - 1)) + 1)
                    for j in range(4):
                        for mt in range(MT):
                            last = nc.tensor.transpose(ps_a[:, mt, j * P:(j + 1) * P],
                                                       mv_T[:, 4 * h + j, mt * P:(mt + 1) * P], ident)
                elif kind == "cs":
                    pe.wait_ge(acc_free, TILES.index(("cq", 2 * h + 1)) + 1)
                    for s in range(ST):
                        for dt in range(2):
                            last = mm(ps_a[:, s // 2, (s % 2) * MEM:(s % 2 + 1) * MEM],
                                      cq_T[:, h % 2, dt, s * P:(s + 1) * P], mk_T[:, 2 * h + dt],
                                      start=dt == 0, stop=dt == 1)
                elif kind == "ct":
                    for mt in range(MT):
                        for s in range(ST):
                            last = nc.tensor.transpose(ps_a[:, mt, s * P:(s + 1) * P],
                                                       p_c[:, s, mt * P:(mt + 1) * P], ident)
                elif kind == "cv":
                    for dt in range(2):
                        for mt in range(MT):
                            last = mm(ps_a[:, dt], mv_tok[:, mt, (2 * h + dt) * P:(2 * h + dt + 1) * P], pT_c[:, mt],
                                      start=mt == 0, stop=mt == MT - 1)
                elif kind == "av":
                    pe.wait_ge(acc_free, TILES.index(("av", h)) + 1)
                    for s in range(ST):
                        last = nc.tensor.transpose(ps_a[:, 0, s * P:(s + 1) * P], qkv_T[:, h % 2, 2, s * P:(s + 1) * P], ident)
                elif kind in ("as0", "as1"):
                    rows_m = slice(DA * int(kind[2]), DA * int(kind[2]) + DA)
                    ps = flat(ps_a[:])
                    for q in range(ST - 1, -1, -1):
                        last = mm(ps[:, bank_of[q]:bank_of[q] + (q + 1) * P], qkv_T[rows_m, h % 2, 0, q * P:(q + 1) * P],
                                  qkv_T[rows_m, h % 2, 1, 0:(q + 1) * P], start=True, stop=True)
                elif kind == "at":
                    ps = flat(ps_a[:])
                    for kt in range(ST):
                        for q in range(kt, ST):
                            last = nc.tensor.transpose(ps[:, t_bank(kt, q):t_bank(kt, q) + P],
                                                       p_a[:, 0, pack_of[q] + kt * P:pack_of[q] + (kt + 1) * P], ident)
                elif kind == "ap":
                    for q in range(ST):
                        for kt in range(q + 1):
                            last = mm(ps_a[:, 0, q * P:(q + 1) * P], wT[:, t_pack(kt, q):t_pack(kt, q) + P],
                                      v_tok[:, kt * P:(kt + 1) * P], start=kt == 0, stop=kt == q)
                elif kind == "ay":
                    for q in range(ST):
                        last = nc.tensor.transpose(ps_a[:, 0, q * P:(q + 1) * P], o_a[:, q], ident)
                last.then_inc(a_mm, 1)

            def pool_step(i):
                kind, p, c = DELTA[i]
                before = {("dE", 0): ("dk", p, 0), ("dW", 0): ("dkb", p, 0), ("sb", 0): ("dA", p, 0),
                          ("Za", 1): ("dL", p, 0), ("Za", 2): ("T1", p, 0), ("Wb", 1): ("T1", p, 0)}.get((kind, c))
                if before is None and kind == "Za":
                    before = ("Za", p, c - 2)
                if before is None and kind in ("Wb", "Wl"):
                    before = ("Tc", p, c - 1)
                return d_idx.get(before)

            def delta(i):
                kind, p, c = DELTA[i]
                if i:
                    pe.wait_ge(d_act, dA[i])
                    pe.wait_ge(d_dve, dD[i])
                if pool_step(i) is not None:
                    pe.wait_ge(d_pool, dP[pool_step(i) + 1])
                dst = [ps_d[:, m // 4, (m % 4) * P:(m % 4 + 1) * P] for m in range(8)]
                if kind in ("dq", "dk", "dv"):
                    pe.wait_ge(co_ready, 6 * (p + 1))
                    for m in range(8):
                        last = nc.tensor.transpose(dst[m], conv_o[:, ("dq", "dk", "dv").index(kind), m // 4,
                                                                  (m % 4) * P:(m % 4 + 1) * P], ident)
                elif kind in ("dqT", "dqd", "dkT", "dkb", "T1", "Tc", "dO"):
                    src = {"dqT": Q, "dqd": Q, "dkT": K, "dkb": KB, "T1": TT, "Tc": TT, "dO": O}[kind]
                    for m in range(8):
                        last = nc.tensor.transpose(dst[m], src[:, m], ident)
                elif kind == "dE":
                    for m in range(8):
                        last = mm(dst[m], ET[:, m], cst[:, C_UPTO, :], start=True, stop=True)
                elif kind in ("Za", "Wb", "Wl"):
                    a, b, second = (XT[c % 2], TN, 0) if kind == "Za" else (Z, TT, 1)
                    for m in range(8):
                        last = mm(ps_d[:, 0, m * P // 2:(m + 1) * P // 2], a[:, m], halves(b[:, m], c, second),
                                  start=True, stop=True)
                elif kind in ("dL", "dA", "dU", "dW"):
                    a, b = {"dL": (KTT, KBT), "dA": (KTT, QT), "dU": (TT, V), "dW": (KB, TT)}[kind]
                    for m in range(8):
                        last = mm(dst[m], a[:, m], b[:, m], start=True, stop=True)
                elif kind == "sa":
                    for hh in range(2):
                        last = mm(ps_d[:, 0, hh * P:(hh + 1) * P], WT[:, 4 * hh + c], state[:, hh], start=True, stop=True)
                elif kind == "sb":
                    for hh in range(2):
                        vn = vnew[:, hh] if c else U[:, 4 * hh]
                        o_ps = ps_d[:, 0, hh * P:(hh + 1) * P]
                        if c:
                            mm(o_ps, QDT[:, 4 * hh + c], state[:, hh], start=True, stop=False)
                        mm(o_ps, AT[:, 4 * hh + c], vn, start=c == 0, stop=True)
                    for hh in range(2):
                        vn = vnew[:, hh] if c else U[:, 4 * hh]
                        last = mm(ps_d[:, 1, hh * P:(hh + 1) * P], K[:, 4 * hh + c], vn, start=True, stop=True)
                last.then_inc(d_mm, 1)

            for n, (main, ev, fi, sa, sd) in enumerate(SLOTS):
                if n in MEM_SLOTS:
                    transpose_rows(ST + MEM_SLOTS.index(n))
                if n == BA_SLOT:
                    beta_and_decay_rows()
                if n == BA_SLOT + 1:
                    beta_and_decay()
                if n == F_SLOT:
                    bias_values()
                if n == G_SLOT:
                    pe.wait_ge(g_ready, 1)
                    pe.wait_ge(in_cst, 16)
                    pe.wait_ge(ones_set, 1)
                    for m, w in enumerate((cst[:, C_UPTO, :], cst[:, C_AFTER, :], ones[:])):
                        last = mm(ps_d[:, 2, m * 32:(m + 1) * 32], w, flat(gdec[:]), start=True, stop=True)
                    last.then_inc(g_mm, 1)
                if main is not None:
                    main_half(*main)
                if sd is not None:
                    delta(sd)
                if sa is not None:
                    attn(sa)

            def sum_over_partitions(tiles, dst):
                for i in tiles:
                    c = slice(i * P, (i + 1) * P)
                    mm(dst[:, i:i + 1], ssum[:, c], ones[:, 0:1], start=True, stop=False)
                    last = mm(dst[:, i:i + 1], sqs[:, (KT - 1) % 2, c], ones[:, 0:1], start=False, stop=True)
                last.then_inc(ss_mm, 1)

            def transpose_f(u, i):
                if i == 3:
                    pe.wait_ge(h1_ok, u * ST + 1)
                for m in range(KT):
                    last = nc.tensor.transpose(from_f(i)[:, m // 4, (m % 4) * P:(m % 4 + 1) * P],
                                               f_T[:, m, i * P:(i + 1) * P], ident)
                last.then_inc(tr_f, 1)

            def out_half_tile(c, m):
                t = LATE[N_BR + m][1]
                cols = HALF[c]
                if c == 0:
                    pe.wait_ge(lo_ready, t + 1)
                    if m < KT - 1:
                        pe.wait_ge(o_ev, m - 1)
                else:
                    pe.wait_ge(o_ev, m + 1)
                last = weight_tile(result_bank(N_BR + m)[:, cols], t, range(KT), lambda k: mx_hi[:, k, cols],
                                   lambda k: mx_lo[:, k, cols], True, True)
                last.then_inc(tile_used if c else out_half, 1)

            def first_f1_half(c, j):
                t = LATE[L_F1[0]][1] + j
                cols = HALF[c]
                pe.wait_ge(n2l, 2 * c + 2)
                pe.wait_ge(lo_ready, t + 1)
                last = weight_tile(result_bank(L_F1[0] + j)[:, cols], t, range(KT), lambda k: n2_hi[:, k, cols],
                                   lambda k: n2_lo[:, k, cols], True, True)
                if c == 1:
                    last.then_inc(tile_used, 1)

            def row_back(i):
                pe.wait_ge(n2n, i + 1)
                pe.wait_ge(h1_ok, {0: 2, 1: 3, 2: 4, 3: 2}[i])
                if i == 3:
                    pe.wait_ge(n2l, 1)
                for m in range(KT):
                    last = nc.tensor.transpose(back(i)[:, m // 4, (m % 4) * P:(m % 4 + 1) * P],
                                               rows[:, i % 2, m * P:(m + 1) * P], ident)
                last.then_inc(tr2, 1)

            def between():
                M0 = KT - H
                for m in range(M0, KT):
                    out_half_tile(0, m)
                out_half_tile(1, M0)
                pe.wait_ge(o_ev, KT)
                transpose_f(0, 0)
                pe.wait_ge(sqs_sum, sums_before[KT])
                pe.wait_ge(sqs_ok, KT)
                sum_over_partitions((0, 1), ps_d[:, 2])
                transpose_f(0, 1)
                for m in range(M0 + 1, KT):
                    out_half_tile(1, m)
                pe.wait_ge(o_ev, len(OUT_PARTS))
                transpose_f(0, 2)
                pe.wait_ge(sqs_sum, sums_before[-1])
                pe.wait_ge(sqs_ok, len(OUT_PARTS))
                sum_over_partitions((2, 3), ps_a[:, 2])
                transpose_f(0, 3)
                row_back(0)
                row_back(1)
                for j in range(H - 1):
                    first_f1_half(0, j)
                row_back(2)
                row_back(3)
                first_f1_half(0, H - 1)
                for j in range(H):
                    first_f1_half(1, j)

            for r, (tile, t0, k) in enumerate(LATE):
                bank = acc[:, r % 2]
                if N_BR + KT - H <= r < L_F1[0] + H:
                    if r == N_BR + KT - H:
                        between()
                    continue
                k_wait = None
                if r < 2:
                    pe.wait_ge(acc_free, N_MIX - 1 + r)
                elif r - 2 < N_BR:
                    pe.wait_ge(gated, r - 1)
                elif r - 2 < N_BR + KT:
                    pe.wait_ge(o_ev, r - 1 - N_BR)
                elif LATE[r - 2][0][0] == "f1":
                    pe.wait_ge(relu_ok, LATE[r - 2][0][1] + 1)
                else:
                    pe.wait_ge(f_ev, r - 1 - L_F2[0] if r - 2 < L_F1[1] else r - 1 - L_F2[1] + KT)
                if tile[0] == "br":
                    b = r // KT
                    hi_of, lo_of = (lambda k, b=b: y_hi[b][:, k]), (lambda k, b=b: y_lo[b][:, k])
                    if r % KT == 0:
                        k_wait = lambda k, b=b: pe.wait_ge(yl_ready, KT * b + k + 1)
                elif tile[0] == "out":
                    hi_of, lo_of = (lambda k: mx_hi[:, k]), (lambda k: mx_lo[:, k])
                    if r == N_BR:
                        k_wait = lambda k: pe.wait_ge(mxl_ready, k + 1)
                elif tile[0] == "f1":
                    hi_of, lo_of = (lambda k: n2_hi[:, k]), (lambda k: n2_lo[:, k])
                for j in range(k):
                    t = t0 + j
                    pe.wait_ge(lo_ready, t + 1)
                    if tile[0] == "f2":
                        g = TILES[t][1] // KT
                        o = (g % 2) * KT
                        hi_of, lo_of = (lambda k, o=o: h_hi[:, o + k]), (lambda k, o=o: h_lo[:, o + k])
                        if r in L_F2:
                            k_wait = lambda k, g=g: pe.wait_ge(hl_ok, g * KT + k + 1)
                    last = weight_tile(bank, t, range(KT), hi_of, lo_of, j == 0, j == k - 1, k_wait)
                    if j < k - 1:
                        last.then_inc(tile_used, 1)
                last.then_inc(tile_used, 1)
            pe.wait_ge(sqs_sum, SUMS[1] + KT - 2)
            pe.wait_ge(sqs_ok, len(OUT_PARTS) + KT)
            sum_over_partitions(range(ST), ps_d[:, 2])
            pe.wait_ge(fg_ok, KT)
            for i in range(ST):
                transpose_f(1, i)


def _consts():
    i = np.arange(P)
    c = np.zeros((P, NCONST, P), np.float32)
    c[:, C_ID] = np.eye(P)
    c[:, C_UPTO] = i[:, None] <= i[None, :]
    c[:, C_AFTER] = i[:, None] > i[None, :]
    for n in range(NM):
        b = 2 ** n
        c[:, C_MASK0 + n] = ((i[None, :] // (2 * b) == i[:, None] // (2 * b)) & (i[None, :] // b % 2 == 1)
                             & (i[:, None] // b % 2 == 0))
    c[:, C_CAUS] = np.where(i[None, :] > i[:, None], NEG, 0.0)
    return c


def _onehot():
    dist = np.maximum(2 * P - 1 - np.arange(SPAN), 0)
    nf = np.maximum(dist, 1).astype(np.float32)
    large = MAX_EXACT + (np.log(nf / np.float32(MAX_EXACT)) / np.float32(math.log(MAX_DIST / MAX_EXACT))
                         * np.float32(BUCKETS - MAX_EXACT)).astype(np.int32)
    bucket = np.where(dist < MAX_EXACT, dist, np.minimum(large, BUCKETS - 1))
    o = np.zeros((BUCKETS, SPAN), np.float32)
    o[bucket, np.arange(SPAN)] = 1.0
    o[BUCKETS - 1] -= 1.0
    return o


def kernel(**inputs):
    import concourse.bacc as bacc
    from concourse.bass_utils import run_bass_kernel_spmd

    a = {k: np.asarray(v) for k, v in inputs.items()}
    w_in, w_kv, w_br = a["w_in"][0], a["w_mem_kv"][0], a["w_branch"][0]
    w_out, w1, w2 = a["w_out"][0], a["w_ff1"][0], a["w_ff2"][0]

    def block_of(kind, j):
        c = slice(j * P, (j + 1) * P)
        if kind == "mk":
            return w_kv[:, c]
        if kind == "mv":
            return w_kv[:, D + j * P:D + (j + 1) * P]
        if kind == "br":
            return w_br[j // KT][:, j % KT * P:(j % KT + 1) * P]
        if kind == "out":
            return w_out[:, c]
        if kind == "f1":
            return w1[:, c]
        if kind == "f2":
            return w2[j // KT * D:(j // KT + 1) * D, j % KT * P:(j % KT + 1) * P]
        return w_in[:, COL[kind] + j * P:COL[kind] + (j + 1) * P]

    tiles = plan_tiles()[0]
    weights = np.empty((len(tiles), P, KT, P), np.float32)
    for n, (kind, j) in enumerate(tiles):
        weights[n] = block_of(kind, j).reshape(KT, P, P).transpose(1, 0, 2)

    params = np.empty((P, NPAR), np.float32)
    for c, name in ((PC_PRE, "ln_mix_pre"), (PC_MEM, "mem_norm_g"), (PC_FF, "ln_ff_pre")):
        params[:, c:c + KT] = a[name][0].reshape(KT, P).T
    params[:, PC_SUB] = a["da_subln_g"][0]
    params[:, PC_DNG] = a["dn_norm_g"][0]
    params[:, PC_CONV:PC_ALOG] = a["conv_w"][0].reshape(4, 24, P).transpose(2, 1, 0).reshape(P, 96)
    params[:, PC_ALOG:PC_ALOG + HB] = a["dn_a_log"][0][None]
    params[:, PC_DTB:PC_DTB + HB] = a["dn_dt_bias"][0][None]
    params[:, PC_LAM:PC_POST] = a["da_lambda"][0].reshape(1, 4 * DA)
    params[:, PC_POST:PC_POST + KT] = a["ln_mix_post"][0].reshape(KT, P).T
    params[:, PC_POST + KT:] = a["ln_ff_post"][0].reshape(KT, P).T
    post_g = np.empty((P, D), np.float32)
    post_g[:] = a["ln_ff_pre"][0][None]
    w_ba = w_in[:, COL["ba"]:COL["ba"] + 2 * HB].reshape(KT, P, 2 * HB).transpose(1, 0, 2)
    arrays = {
        "weights": weights, "x": a["x"][0], "mem": a["mem"][0], "w_ba": w_ba, "params": params,
        "consts": _consts(), "onehot": _onehot(), "relb": a["rel_bias"], "post_g": post_g,
    }
    arrays = {k: np.ascontiguousarray(v) for k, v in arrays.items()}
    nc = bacc.Bacc("TRN2", target_bir_lowering=False, num_devices=1)
    ins = [nc.dram_tensor(k, v.shape, F32, kind="ExternalInput").ap() for k, v in arrays.items()]
    y_dram = nc.dram_tensor("y_scratch", (3, P, KT, S), F32, kind="Internal").ap()
    gate_dram = nc.dram_tensor("gate_scratch", (3 * KT, P, S), F32, kind="Internal").ap()
    f_dram = nc.dram_tensor("bias_scratch", (HA, SPAN), F32, kind="Internal").ap()
    frep_dram = nc.dram_tensor("bias_rows", (HA, P, SPAN), F32, kind="Internal").ap()
    out = nc.dram_tensor("out", (S, D), F32, kind="ExternalOutput").ap()
    build(nc, *ins, y_dram, gate_dram, f_dram, frep_dram, out)
    r = run_bass_kernel_spmd(nc, [arrays], core_ids=[0])
    return r.results[0]["out"].reshape(1, S, D)
```
